# Optimizing a Trainium2 kernel written in Bass

```python
import jax, jax.numpy as jnp
from jax import lax
import numpy as np

D_MODEL = 2048
BATCH = 1
SEQ = 256
DEPTH = 1
DEC_BATCH = 8
DEC_SEQ = 1
PAST_LEN = 256
PAGE_SIZE = 128

N_META = 16
SB_HEADS = 16
SB_HEAD_DIM = 64
D_ATTN = SB_HEADS * SB_HEAD_DIM
SB_SCALE = SB_HEAD_DIM ** -0.5
SB_BIAS_INIT = -7.0
Q_BLOCK = 128
D_CONV = D_MODEL // 2
CONV_WIDTH = 31
PEER_HEADS = 8
PEER_N_KEYS = 128
PEER_N_EXPERTS = PEER_N_KEYS * PEER_N_KEYS
PEER_QUERY_DIM = 256
PEER_HALF = PEER_QUERY_DIM // 2
PEER_TOPK = 16
PEER_TOKEN_CHUNK = 128
IN_COLS = 3 * D_ATTN + 2 * D_CONV + 2 * D_MODEL
SPLITS = (D_ATTN, 2 * D_ATTN, 3 * D_ATTN, 3 * D_ATTN + 2 * D_CONV, 3 * D_ATTN + 2 * D_CONV + D_MODEL)
RMS_EPS = 1e-6
LN_EPS = 1e-5

kernel_name = "hybrid_stickbreak_conformer_peer_step"

def rmsnorm(x, g):
    xf = x.astype(jnp.float32)
    y = xf * lax.rsqrt(jnp.mean(xf * xf, axis=-1, keepdims=True) + RMS_EPS)
    return (y * g.astype(jnp.float32)).astype(x.dtype)

def layernorm(x, g, b):
    xf = x.astype(jnp.float32)
    mu = jnp.mean(xf, axis=-1, keepdims=True)
    var = jnp.mean(jnp.square(xf - mu), axis=-1, keepdims=True)
    y = (xf - mu) * lax.rsqrt(var + LN_EPS)
    return (y * g.astype(jnp.float32) + b.astype(jnp.float32)).astype(x.dtype)

def split_projection(h, w_in):
    bsz, t = h.shape[0], h.shape[1]
    proj = jnp.einsum('btd,dc->btc', h, w_in)
    q, k, v, glu_in, gate_a, gate_c = jnp.split(proj, SPLITS, axis=-1)
    conv_in = glu_in[..., :D_CONV] * jax.nn.sigmoid(glu_in[..., D_CONV:])
    def heads(z):
        return z.reshape(bsz, t, SB_HEADS, SB_HEAD_DIM)
    return heads(q), heads(k), heads(v), conv_in, gate_a, gate_c

def stick_breaking(q, k, v, bias, q_pos, k_pos):
    z = jnp.einsum('bqhd,bshd->bhqs', q, k).astype(jnp.float32) * SB_SCALE
    z = z + bias.astype(jnp.float32)[None, :, None, None]
    visible = (k_pos[None, :] < q_pos[:, None])[None, None]
    log_1m = jnp.where(visible, jax.nn.log_sigmoid(-z), 0.0)
    tail = lax.cumsum(log_1m, axis=3, reverse=True) - log_1m
    a = jnp.where(visible, jnp.exp(jax.nn.log_sigmoid(z) + tail), 0.0)
    o = jnp.einsum('bhqs,bshd->bqhd', a.astype(v.dtype), v)
    return o.reshape(o.shape[0], o.shape[1], D_ATTN)

def sb_prompt(q, k, v, bias):
    bsz, t = q.shape[0], q.shape[1]
    n_blocks = (t - N_META) // Q_BLOCK
    key_pos = jnp.arange(t, dtype=jnp.int32)
    meta_pos = jnp.arange(N_META, dtype=jnp.int32)
    meta_out = stick_breaking(q[:, :N_META], k[:, :N_META], v[:, :N_META], bias, meta_pos, meta_pos)

    def block(b):
        start = N_META + b * Q_BLOCK
        qb = lax.dynamic_slice_in_dim(q, start, Q_BLOCK, axis=1)
        return stick_breaking(qb, k, v, bias, start + jnp.arange(Q_BLOCK, dtype=jnp.int32), key_pos)

    blocks = lax.map(block, jnp.arange(n_blocks, dtype=jnp.int32))
    real = jnp.moveaxis(blocks, 0, 1).reshape(bsz, n_blocks * Q_BLOCK, D_ATTN)
    return jnp.concatenate([meta_out, real], axis=1)

def conv_branch(padded, w_dw, b_dw, ln_g, ln_b):
    y = lax.conv_general_dilated(padded, w_dw[:, None, :], window_strides=(1,), padding='VALID',
                                 dimension_numbers=('NWC', 'WIO', 'NWC'), feature_group_count=D_CONV)
    y = y + b_dw
    return jax.nn.silu(layernorm(y, ln_g, ln_b))

def peer_ffn(h, w_query, sub_keys, expert_u, expert_v):
    shape = h.shape
    flat = h.reshape(-1, shape[-1])
    n = flat.shape[0]
    n_chunks = -(-n // PEER_TOKEN_CHUNK)
    flat = jnp.pad(flat, ((0, n_chunks * PEER_TOKEN_CHUNK - n), (0, 0)))

    def chunk(hc):
        qry = (hc @ w_query).reshape(-1, PEER_HEADS, 2, PEER_HALF)
        s = jnp.einsum('chpk,pnk->chpn', qry, sub_keys).astype(jnp.float32)
        s1, i1 = lax.top_k(s[:, :, 0], PEER_TOPK)
        s2, i2 = lax.top_k(s[:, :, 1], PEER_TOPK)
        cand_s = (s1[..., :, None] + s2[..., None, :]).reshape(-1, PEER_HEADS, PEER_TOPK * PEER_TOPK)
        cand_i = (i1[..., :, None] * PEER_N_KEYS + i2[..., None, :]).reshape(-1, PEER_HEADS, PEER_TOPK * PEER_TOPK)
        top_s, pos = lax.top_k(cand_s, PEER_TOPK)
        idx = jnp.take_along_axis(cand_i, pos, axis=-1)
        gate = jax.nn.softmax(top_s, axis=-1).astype(hc.dtype)
        act = jax.nn.gelu(jnp.einsum('cd,chkd->chk', hc, expert_u[idx]))
        return jnp.einsum('chk,chkd->cd', gate * act, expert_v[idx])

    out = lax.map(chunk, flat.reshape(n_chunks, PEER_TOKEN_CHUNK, shape[-1]))
    return out.reshape(-1, shape[-1])[:n].reshape(shape)

def layer_tail(x, attn, conv_act, gate_a, gate_c, w_pa, w_pc, w_o, g_ffn, w_query, sub_keys, expert_u, expert_v):
    branch_a = jnp.einsum('bta,ad->btd', attn, w_pa)
    branch_c = jnp.einsum('btc,cd->btd', conv_act, w_pc)
    mixed = jax.nn.sigmoid(gate_a) * branch_a + jax.nn.sigmoid(gate_c) * branch_c
    x = x + jnp.einsum('btd,de->bte', mixed, w_o)
    return x + peer_ffn(rmsnorm(x, g_ffn), w_query, sub_keys, expert_u, expert_v)

def setup_inputs(seed: int = 0) -> dict:
    key = jax.random.key(seed)
    ks = jax.random.split(key, 24)
    n_pages = PAST_LEN // PAGE_SIZE
    n_used = DEC_BATCH * n_pages
    n_pool = n_used + (n_used + 3) // 4
    f32 = jnp.float32
    def nrm(k, shape, scale):
        return jax.random.normal(k, shape, f32) * scale
    page_table = jax.random.permutation(ks[0], n_pool)[:n_used].reshape(DEC_BATCH, n_pages).astype(jnp.int32)
    return {
        'x_prompt': nrm(ks[1], (BATCH, SEQ, D_MODEL), 1.0),
        'x_sample': nrm(ks[2], (DEC_BATCH, DEC_SEQ, D_MODEL), 1.0),
        'cache_k': nrm(ks[3], (DEPTH, n_pool, PAGE_SIZE, SB_HEADS, SB_HEAD_DIM), 1.0),
        'cache_v': nrm(ks[4], (DEPTH, n_pool, PAGE_SIZE, SB_HEADS, SB_HEAD_DIM), 1.0),
        'state_conv': nrm(ks[5], (DEPTH, DEC_BATCH, CONV_WIDTH - 1, D_CONV), 0.5),
        'page_table': page_table,
        'meta_tokens': nrm(ks[6], (N_META, D_MODEL), 1.0),
        'norm_mix_g': 1.0 + nrm(ks[7], (DEPTH, D_MODEL), 0.02),
        'w_in': nrm(ks[8], (DEPTH, D_MODEL, IN_COLS), D_MODEL ** -0.5),
        'sb_bias': SB_BIAS_INIT + nrm(ks[22], (DEPTH, SB_HEADS), 0.1),
        'w_dw': nrm(ks[9], (DEPTH, CONV_WIDTH, D_CONV), CONV_WIDTH ** -0.5),
        'b_dw': nrm(ks[10], (DEPTH, D_CONV), 0.02),
        'conv_ln_g': 1.0 + nrm(ks[11], (DEPTH, D_CONV), 0.02),
        'conv_ln_b': nrm(ks[12], (DEPTH, D_CONV), 0.02),
        'w_branch_attn': nrm(ks[13], (DEPTH, D_ATTN, D_MODEL), D_ATTN ** -0.5),
        'w_branch_conv': nrm(ks[14], (DEPTH, D_CONV, D_MODEL), D_CONV ** -0.5),
        'w_out': nrm(ks[15], (DEPTH, D_MODEL, D_MODEL), D_MODEL ** -0.5),
        'norm_ffn_g': 1.0 + nrm(ks[16], (DEPTH, D_MODEL), 0.02),
        'w_query': nrm(ks[17], (DEPTH, D_MODEL, PEER_HEADS * PEER_QUERY_DIM), D_MODEL ** -0.5),
        'sub_keys': nrm(ks[18], (DEPTH, 2, PEER_N_KEYS, PEER_HALF), PEER_HALF ** -0.5),
        'expert_u': nrm(ks[19], (DEPTH, PEER_N_EXPERTS, D_MODEL), D_MODEL ** -0.5),
        'expert_v': nrm(ks[20], (DEPTH, PEER_N_EXPERTS, D_MODEL), 0.5 * PEER_HEADS ** -0.5),
        'norm_final_g': 1.0 + nrm(ks[21], (D_MODEL,), 0.02),
    }

def reference(x_prompt, x_sample, cache_k, cache_v, state_conv, page_table, meta_tokens, norm_mix_g, w_in,
              sb_bias, w_dw, b_dw, conv_ln_g, conv_ln_b, w_branch_attn, w_branch_conv, w_out, norm_ffn_g, w_query,
              sub_keys, expert_u, expert_v, norm_final_g):
    bsz = x_prompt.shape[0]
    dec_b, dec_s = x_sample.shape[0], x_sample.shape[1]
    past_len = page_table.shape[1] * cache_k.shape[2]
    meta = jnp.broadcast_to(meta_tokens[None].astype(x_prompt.dtype), (bsz, N_META, D_MODEL))
    xp = jnp.concatenate([meta, x_prompt], axis=1)
    xs = x_sample
    q_pos_s = past_len + jnp.arange(dec_s, dtype=jnp.int32)
    k_pos_s = jnp.arange(past_len + dec_s, dtype=jnp.int32)
    k_p_list, v_p_list, c_p_list, k_s_list, v_s_list, c_s_list = [], [], [], [], [], []
    for l in range(DEPTH):
        h = rmsnorm(xp, norm_mix_g[l])
        q, k, v, conv_in, gate_a, gate_c = split_projection(h, w_in[l])
        attn = sb_prompt(q, k, v, sb_bias[l])
        padded = jnp.concatenate([jnp.zeros((bsz, CONV_WIDTH - 1, D_CONV), conv_in.dtype), conv_in], axis=1)
        conv_act = conv_branch(padded, w_dw[l], b_dw[l], conv_ln_g[l], conv_ln_b[l])
        xp = layer_tail(xp, attn, conv_act, gate_a, gate_c, w_branch_attn[l], w_branch_conv[l], w_out[l],
                        norm_ffn_g[l], w_query[l], sub_keys[l], expert_u[l], expert_v[l])
        k_p_list.append(k)
        v_p_list.append(v)
        c_p_list.append(padded[:, -(CONV_WIDTH - 1):])
        hs = rmsnorm(xs, norm_mix_g[l])
        q_s, k_s, v_s, conv_in_s, gate_a_s, gate_c_s = split_projection(hs, w_in[l])
        k_past = cache_k[l][page_table].reshape(dec_b, past_len, SB_HEADS, SB_HEAD_DIM)
        v_past = cache_v[l][page_table].reshape(dec_b, past_len, SB_HEADS, SB_HEAD_DIM)
        k_all = jnp.concatenate([k_past, k_s], axis=1)
        v_all = jnp.concatenate([v_past, v_s], axis=1)
        attn_s = stick_breaking(q_s, k_all, v_all, sb_bias[l], q_pos_s, k_pos_s)
        padded_s = jnp.concatenate([state_conv[l].astype(conv_in_s.dtype), conv_in_s], axis=1)
        conv_act_s = conv_branch(padded_s, w_dw[l], b_dw[l], conv_ln_g[l], conv_ln_b[l])
        xs = layer_tail(xs, attn_s, conv_act_s, gate_a_s, gate_c_s, w_branch_attn[l], w_branch_conv[l], w_out[l],
                        norm_ffn_g[l], w_query[l], sub_keys[l], expert_u[l], expert_v[l])
        k_s_list.append(k_s)
        v_s_list.append(v_s)
        c_s_list.append(padded_s[:, -(CONV_WIDTH - 1):])
    y_prompt = rmsnorm(xp, norm_final_g)[:, N_META:]
    y_sample = rmsnorm(xs, norm_final_g)
    k_prompt = jnp.stack(k_p_list)
    v_prompt = jnp.stack(v_p_list)
    conv_prompt = jnp.stack(c_p_list)
    k_sample = jnp.stack(k_s_list)
    v_sample = jnp.stack(v_s_list)
    conv_sample = jnp.stack(c_s_list)
    return (y_prompt, y_sample, k_prompt, v_prompt, conv_prompt, k_sample, v_sample, conv_sample)


_drawn_inputs = setup_inputs


def setup_inputs(seed=0):
    import zlib

    import numpy as np

    out = dict(_drawn_inputs(seed))
    spreads = {}
    factors = {'cache_k': 3.058,
     'cache_v': 2.873,
     'sb_bias': 8.0,
     'b_dw': 3.749,
     'conv_ln_g': 4.952,
     'conv_ln_b': 5.439,
     'w_branch_attn': 2.854,
     'norm_ffn_g': 4.301,
     'norm_final_g': 2.759}
    for name, (base, spread) in spreads.items():
        noise = np.random.default_rng([zlib.crc32(name.encode()), seed]).standard_normal(out[name].shape)
        drawn = base * np.exp(spread * noise) if base else spread * noise
        out[name] = __import__('jax').numpy.asarray(drawn.astype(out[name].dtype))
    for name, factor in factors.items():
        out[name] = (out[name] * factor).astype(out[name].dtype)
    return out
```

```python
from contextlib import ExitStack

import concourse.bass as bass
from concourse import mybir

F32 = mybir.dt.float32
F32R = mybir.dt.float32r
U32 = mybir.dt.uint32
I32 = mybir.dt.int32
ACT = mybir.ActivationFunctionType
ALU = mybir.AluOpType
AX_X = mybir.AxisListType.X

P = 128
D = 2048
KD = D // P
SEQ, DEC, META = 256, 8, 16
LIVE = SEQ + DEC
NT = LIVE + META
HEADS, HD = 16, 64
DA = HEADS * HD
KA = DA // P
DC = 1024
KC = DC // P
TAPS = 31
PAGES = 2
PH, PK = 8, 16
NK = 128
RMS_EPS, LN_EPS = 1e-6, 1e-5

HALF = 8
RAW, SPLIT = 4, 2
T_IN, T_BR, T_OUT, T_QRY = 72, 16, 16, 16
PAIR_Q, PAIR_V, PAIR_GLU, PAIR_IN = 4, 12, 20, T_IN // 2
PAIR_BR = PAIR_IN + T_BR // 2
PAIR_OUT = PAIR_BR + T_OUT // 2
PAIR_QRY = PAIR_OUT + T_QRY // 2
PAIR_U = PAIR_QRY + NK // 2
HEAD_PAIRS = 5
SPARE_TILE = PH * HEAD_PAIRS * 2
TT = 3
NEG_BIG = -3.0e38
MASKED = -1.0e30


def spread(ap, at, count):
    wide = ap.unsqueeze(at)
    shape = list(wide.shape)
    shape[at] = count
    return wide.broadcast_to(shape)


def trunk(nc, *args):
    with ExitStack() as ctx:
        program(nc, ctx, *args)


def program(nc, ctx, weights, xT, gains, u_tiles, expert_v, cache_k, cache_v, stateT, page_table, sb_bias,
          w_dwT, conv_vecs, sub_keysT, yT, kvT, conv_p, conv_s):
    at = {}
    base = 16512

    def place(name, offset, shape, dt=F32):
        size = 4
        for n in shape[1:]:
            size *= n
        t = nc.alloc_sbuf_tensor_at(name, shape, dt, offset=base + offset)
        at[name] = -(-(offset + size) // 32) * 32
        return t

    raw = place("raw", 0, [P, RAW, HALF, P])
    hi = [place(f"hi{s}", at["raw"] + 4096 * s, [P, HALF, P], F32R) for s in range(SPLIT)]
    lo = [place(f"lo{s}", at["hi1"] + 4096 * s, [P, HALF, P], F32R) for s in range(SPLIT)]
    ident = place("ident", at["lo1"], [P, P])
    ones = place("ones", at["ident"], [P, P])
    neg_tri = place("neg_tri", at["ones"], [P, P])
    neg_ones = place("neg_ones", at["neg_tri"], [P, P])
    mask = place("mask", at["neg_ones"], [P, P])
    pen = place("pen", at["mask"], [P, P])
    iota = place("iota", at["pen"], [P, P])
    gain = place("gain", at["iota"], [P, 3, KD])
    dw = place("dw", at["gain"], [P, KC, TAPS])
    cvec = place("cvec", at["dw"], [P, 3, KC])
    bias = place("bias", at["cvec"], [P, HEADS])
    eps = place("eps", at["bias"], [P, 2])
    pages = place("pages", at["eps"], [P, DEC * PAGES], I32)
    page_f = place("page_f", at["pages"], [P, DEC * PAGES])
    part = place("part", at["page_f"], [P, 2])
    rows = place("rows", at["part"], [P, DEC * PAGES], I32)
    X = 38400
    assert at["rows"] <= X
    gates = place("gates", X, [P, 2 * KD, LIVE])
    h2 = [place("h2_hi", X, [P, KD, LIVE], F32R), place("h2_lo", X + 16896, [P, KD, LIVE], F32R)]
    Y = X + 33792
    x = place("x", Y, [P, KD, NT])
    yc = place("yc", at["x"], [P, KC, LIVE])
    attn = place("attn", at["yc"], [P, KA, LIVE])
    qkv = place("qkv", at["attn"], [P, 3 * KA, NT])
    work = place("work", at["qkv"], [P, 4, NT])
    rstd = place("rstd", at["work"], [P, NT])
    root = place("root", at["rstd"], [P, NT])
    tmp = place("tmp", at["root"], [P, NT])
    Z = at["tmp"]
    h = [place("h_hi", Z, [P, KD, NT], F32R), place("h_lo", Z + 17920, [P, KD, NT], F32R)]
    PADC = TAPS - 1
    cv = place("cv", at["h_lo"], [P, KC, PADC + META + SEQ])
    st = place("st", at["cv"], [P, KC, DEC, TAPS])
    sg = place("sg", at["st"], [P, NT])
    stp = place("stp", at["sg"], [P, DEC, TAPS])
    GH = 4
    eab = place("eab", Z, [P, GH, 384])
    sab = place("sab", at["eab"], [P, GH, 384])
    em = place("em", at["sab"], [META, GH, 256])
    sm = place("sm", at["em"], [META, GH, 256])
    vn = place("vn", at["sm"], [P, 3, DA])
    ring = place("ring", at["vn"], [P, 4, DA])
    dg = place("dg", at["ring"], [P, 2, KA, P])
    prod = place("prod", at["dg"], [P, DA])
    zd = place("zd", at["prod"], [P, DEC, PAGES, HEADS])
    ed = place("ed", at["zd"], [P, DEC, PAGES, HEADS])
    sd = place("sd", at["ed"], [P, DEC, PAGES, HEADS])
    QK = at["attn"]
    at_p = [place("at_hi", QK, [P, KA, LIVE], F32R), place("at_lo", QK + 8448, [P, KA, LIVE], F32R)]
    cv_p = [place("cv_hi", QK + 16896, [P, KC, LIVE], F32R), place("cv_lo", QK + 25344, [P, KC, LIVE], F32R)]
    mx = [place("mx_hi", QK + 33792, [P, KD, LIVE], F32R), place("mx_lo", QK + 50688, [P, KD, LIVE], F32R)]
    t2 = place("t2", at["mx_lo"], [P, 2, LIVE])
    work2 = place("work2", at["t2"], [P, 4, LIVE])
    W = place("W", Y, [P, NK, LIVE])
    Wf = W[:].rearrange("p a b -> p (a b)")
    spare = SPARE_TILE * LIVE
    offs = [spare]

    def carve(n):
        a = offs[0]
        offs[0] += n
        return Wf[:, a:a + n]

    sc_all = carve(TT * 2 * PH * NK).rearrange("p (t q n) -> p t q n", t=TT, q=2 * PH)
    sh = carve(TT * 2 * NK).rearrange("p (t q n) -> p t q n", t=TT, q=2)
    cand = carve(TT * PK * PK).rearrange("p (t a b) -> p t a b", t=TT, a=PK)
    eq = carve(TT * PK * PK).rearrange("p (t a b) -> p t a b", t=TT, a=PK)
    top1 = carve(TT * 2 * PK).rearrange("p (t q k) -> p t q k", t=TT, q=2)
    idx1 = carve(TT * 2 * PK).rearrange("p (t q k) -> p t q k", t=TT, q=2)
    idx1f = carve(TT * 2 * PK).rearrange("p (t q k) -> p t q k", t=TT, q=2)
    top2 = carve(TT * PK).rearrange("p (t k) -> p t k", t=TT)
    pos2 = carve(TT * PK).rearrange("p (t k) -> p t k", t=TT)
    pab = carve(2 * TT * PK).rearrange("p (q t k) -> p q t k", q=2, t=TT)
    pabf = carve(2 * TT * PK).rearrange("p (q t k) -> p q t k", q=2, t=TT)
    assert offs[0] <= NK * LIVE
    qry = W[:, 30:32, :]
    skT = W[:, 32, 0:2 * NK].rearrange("p (q n) -> p q n", q=2)
    chosen = place("chosen", at["W"], [P, 3, TT, PH, PK])
    lhot = place("lhot", X, [P, 2, 4, NK])
    rhot = place("rhot", at["lhot"], [P, 2, 4, NK])
    rdiff = place("rdiff", at["rhot"], [P, 2, 4, NK])
    chT = place("chT", at["rdiff"], [P, 3, LIVE])
    sums = place("sums", at["chT"], [P, 2, TT, PH])
    x2 = place("x2", X, [P, KD, LIVE])
    w_hi = [place(f"w_hi{s}", at["x2"] + 1056 * s, [P, LIVE], F32R) for s in range(2)]
    w_lo = [place(f"w_lo{s}", at["w_hi1"] + 1056 * s, [P, LIVE], F32R) for s in range(2)]
    fin = place("fin", Y, [P, 4, LIVE])
    fin_r = place("fin_r", at["fin"], [P, 3, LIVE])

    ps = ctx.enter_context(nc.psum_tensor("ps", [P, 8, 512], F32))
    x2_dram = nc.dram_tensor("x2_spill", [P, KD, LIVE], F32, kind="Internal").ap()

    def sem(name):
        return ctx.enter_context(nc.semaphore(name))

    raw_in = [sem(f"raw_in{s}") for s in range(RAW)]
    hi_done, lo_done, mm_done = sem("hi_done"), sem("lo_done"), sem("mm_done")
    tile_free = [sem("tile_free0"), sem("tile_free1")]
    vec_step = sem("vec_step")
    act_step = sem("act_step")
    steps = {"vec": 0, "act": 0}

    def vchain(ins):
        steps["vec"] += 1
        ins.then_inc(vec_step, 1)

    def vwait(dve):
        dve.wait_ge(vec_step, steps["vec"])

    a_halves = weights

    def load_half(sp, c, s, src):
        sp.wait_ge(hi_done, c + 1)
        sp.wait_ge(lo_done, c + 1)
        sp.dma_start(raw[:, s].rearrange("p a b -> p (a b)"), src).then_inc(raw_in[s], 16)

    def split_hi(act, c, k):
        act.wait_ge(raw_in[k % RAW], 4 * c + 16 - 4 * (k % RAW))
        act.wait_ge(mm_done, c + 1)
        nc.scalar.copy(hi[k % SPLIT][:], raw[:, k % RAW]).then_inc(hi_done, 1)

    def split_lo(dve, c, k):
        dve.wait_ge(hi_done, c + RAW + 1)
        dve.wait_ge(mm_done, c + 1)
        nc.vector.tensor_tensor(lo[k % SPLIT][:], raw[:, k % RAW], hi[k % SPLIT][:].bitcast(F32),
                                ALU.subtract).then_inc(lo_done, 1)

    def half_products(pe, c, k, out, rhs, first, n, start, stop):
        pe.wait_ge(lo_done, c + RAW + 1)
        for j in range(HALF):
            a, b = hi[k % SPLIT][:, j], lo[k % SPLIT][:, j]
            rh, rl = rhs[0][:, first + j, 0:n], rhs[1][:, first + j, 0:n]
            pe.matmul(out, a, rh, start=start and j == 0, stop=False)
            pe.matmul(out, a, rl, start=False, stop=False)
            m = pe.matmul(out, b, rh, start=False, stop=stop and j == HALF - 1)
        m.then_inc(mm_done, 1)

    def pe_pairs(pe, first, last, rhs, n):
        with pe.Fori(first, last) as i:
            for b in range(2):
                pe.wait_ge(tile_free[b], i + 1)
                for hf in range(2):
                    half_products(pe, 4 * i + 2 * b + hf, 2 * b + hf, ps[:, b, 0:n], rhs, HALF * hf, n,
                                  hf == 0, hf == 1)

    def act_pairs(act, first, last, even, odd):
        with act.Fori(first, last) as i:
            split_hi(act, 4 * i + 1, 1)
            split_hi(act, 4 * i + 2, 2)
            if even:
                act.wait_ge(mm_done, 4 * i + 4)
                even(i)
            split_hi(act, 4 * i + 3, 3)
            split_hi(act, 4 * i + 4, 4)
            if odd:
                act.wait_ge(mm_done, 4 * i + 6)
                odd(i)

    sq_ready, sq_used, root_ready = sem("sq_ready"), sem("sq_used"), sem("root_ready")
    norm_ready, norm_hi = sem("norm_ready"), sem("norm_hi")

    def act_norm(act, src, tiles, n, slots, rt, call, dim, e):
        for j in range(tiles):
            if call + j >= 4:
                act.wait_ge(sq_used, call + j - 3)
            nc.scalar.square(slots[:, j % 4, 0:n], src[:, j, 0:n]).then_inc(sq_ready, 1)
        act.wait_ge(sq_used, call + tiles)
        nc.scalar.activation(rt[:, 0:n], ps[:, 7, 0:n], ACT.Sqrt, bias=eps[:, e:e + 1],
                             scale=1.0 / dim).then_inc(root_ready, 1)

    def pe_norm(pe, tiles, n, slots, call):
        for j in range(tiles):
            pe.wait_ge(sq_ready, call + j + 1)
            pe.matmul(ps[:, 7, 0:n], ones[:], slots[:, j % 4, 0:n], start=j == 0,
                      stop=j == tiles - 1).then_inc(sq_used, 1)

    def dve_rstd(dve, n, rt, rs, tp, nth, dim, e):
        dve.wait_ge(root_ready, nth)
        vchain(nc.vector.reciprocal(rs[:, 0:n], rt[:, 0:n]))
        vwait(dve)
        vchain(nc.vector.tensor_scalar(rt[:, 0:n], ps[:, 7, 0:n], 1.0 / dim, eps[:, e:e + 1], ALU.mult, ALU.add))
        vchain(nc.vector.tensor_tensor(tp[:, 0:n], rs[:, 0:n], rs[:, 0:n], ALU.mult))
        vwait(dve)
        vchain(nc.vector.tensor_tensor(tp[:, 0:n], tp[:, 0:n], rt[:, 0:n], ALU.mult))
        vwait(dve)
        vchain(nc.vector.tensor_scalar(tp[:, 0:n], tp[:, 0:n], -0.5, 1.5, ALU.mult, ALU.add))
        vwait(dve)
        vchain(nc.vector.tensor_tensor(rs[:, 0:n], rs[:, 0:n], tp[:, 0:n], ALU.mult))
        vwait(dve)

    def dve_norm_split(dve, src, parts, n, slots, rs, g, call):
        def scaled(j):
            nc.vector.scalar_tensor_tensor(out=slots[:, j % 4, 0:n], in0=src[:, j, 0:n],
                                           scalar=gain[:, g, j:j + 1], in1=rs[:, 0:n],
                                           op0=ALU.mult, op1=ALU.mult).then_inc(norm_ready, 1)
        scaled(0)
        scaled(1)
        for j in range(KD):
            dve.wait_ge(norm_hi, call + j + 1)
            vchain(nc.vector.tensor_tensor(parts[1][:, j, 0:n], slots[:, j % 4, 0:n],
                                           parts[0][:, j, 0:n].bitcast(F32), ALU.subtract))
            if j + 2 < KD:
                scaled(j + 2)

    def act_norm_split(act, parts, n, slots, call):
        for j in range(KD):
            act.wait_ge(norm_ready, call + j + 1)
            nc.scalar.copy(parts[0][:, j, 0:n], slots[:, j % 4, 0:n]).then_inc(norm_hi, 1)

    x_in, vec_in, const_ready, conv_in_sem = sem("x_in"), sem("vec_in"), sem("const_ready"), sem("conv_in")
    fill0, sig_done, glu_done = sem("fill0"), sem("sig_done"), sem("glu_done")
    rows_ready, part_ready, out_done, kv_done = sem("rows_ready"), sem("part_ready"), sem("out_done"), sem("kv_done")
    conv_done, norm_split0, tap_done = sem("conv_done"), sem("norm_split0"), sem("tap_done")

    with nc.Block() as block:
        @block.sync
        def _(sp):
            sp.dma_start(x[:], xT).then_inc(x_in, 16)
            for t, src in ((gain, gains), (dw, w_dwT), (cvec, conv_vecs), (bias, sb_bias), (pages, page_table)):
                sp.dma_start(t[:], src).then_inc(vec_in, 16)
            for j in range(KC):
                sp.dma_start(st[:, j, :, 0:PADC], stateT[:, j]).then_inc(vec_in, 16)
            for s in range(RAW):
                sp.dma_start(raw[:, s].rearrange("p a b -> p (a b)"), a_halves[s]).then_inc(raw_in[s], 16)
            with sp.Fori(1, PAIR_IN + 1) as i:
                for s in range(RAW):
                    load_half(sp, 4 * i + s, s, a_halves[4 * i + s])

        @block.gpsimd
        def _(pool):
            pool.sem_inc(tile_free[0], 1)
            pool.sem_inc(tile_free[1], 1)
            nc.gpsimd.memset(ones[:], 1.0).then_inc(fill0, 1)
            nc.gpsimd.memset(eps[:, 0:1], RMS_EPS).then_inc(fill0, 1)
            nc.gpsimd.memset(eps[:, 1:2], LN_EPS).then_inc(fill0, 1)
            nc.gpsimd.memset(ident[:], 0.0).then_inc(const_ready, 1)
            nc.gpsimd.memset(neg_tri[:], -1.0).then_inc(const_ready, 1)
            nc.gpsimd.memset(mask[:], 1.0).then_inc(const_ready, 1)
            nc.gpsimd.memset(neg_ones[:], -1.0).then_inc(const_ready, 1)
            nc.gpsimd.memset(pen[:], 0.0).then_inc(const_ready, 1)
            for j in range(KC):
                nc.gpsimd.memset(cv[:, j, 0:PADC], 0.0).then_inc(const_ready, 1)
            pool.wait_ge(const_ready, 5 + KC)
            nc.gpsimd.affine_select(out=ident[:], in_=ident[:], compare_op=ALU.not_equal, fill=1.0, base=0,
                                    pattern=[[-1, P]], channel_multiplier=1).then_inc(const_ready, 1)
            nc.gpsimd.affine_select(out=neg_tri[:], in_=neg_tri[:], compare_op=ALU.is_ge, fill=0.0, base=0,
                                    pattern=[[-1, P]], channel_multiplier=1).then_inc(const_ready, 1)
            nc.gpsimd.affine_select(out=mask[:], in_=mask[:], compare_op=ALU.is_gt, fill=0.0, base=0,
                                    pattern=[[1, P]], channel_multiplier=-1).then_inc(const_ready, 1)
            nc.gpsimd.affine_select(out=pen[:], in_=pen[:], compare_op=ALU.is_gt, fill=MASKED, base=0,
                                    pattern=[[1, P]], channel_multiplier=-1).then_inc(const_ready, 1)
            nc.gpsimd.iota(iota[:], pattern=[[1, P]], base=0, channel_multiplier=0,
                           allow_small_or_imprecise_dtypes=True).then_inc(const_ready, 1)
            nc.gpsimd.iota(part[:], pattern=[[0, 2]], base=0, channel_multiplier=1,
                           allow_small_or_imprecise_dtypes=True).then_inc(part_ready, 1)

        @block.scalar
        def _(act):
            act.sem_inc(hi_done, RAW)
            act.wait_ge(x_in, 16)
            act.wait_ge(fill0, 3)
            act_norm(act, x, KD, NT, work, root, 0, D, 0)
            act_norm_split(act, h, NT, work, 0)
            act.wait_ge(raw_in[0], 16)
            nc.scalar.copy(hi[0][:], raw[:, 0]).then_inc(hi_done, 1)

            def copy_out(b):
                def f(i):
                    nc.scalar.copy(qkv[:, 2 * i + b, :], ps[:, b, 0:NT]).then_inc(tile_free[b], 1)
                return f

            def q_out(b):
                def f(i):
                    nc.scalar.mul(qkv[:, 2 * i + b, :], ps[:, b, 0:NT], HD ** -0.5).then_inc(tile_free[b], 1)
                return f

            def glu_gate(i):
                act.wait_ge(glu_done, i - PAIR_V + 1)
                nc.scalar.activation(sg[:], ps[:, 0, 0:NT], ACT.Sigmoid).then_inc(tile_free[0], 1)

            def gate_out(b):
                def f(i):
                    nc.scalar.activation(gates[:, 2 * (i - PAIR_GLU) + b, :], ps[:, b, 0:LIVE],
                                         ACT.Sigmoid).then_inc(tile_free[b], 1)
                return f

            act_pairs(act, 0, PAIR_Q, q_out(0), q_out(1))
            act_pairs(act, PAIR_Q, PAIR_V, copy_out(0), copy_out(1))
            act_pairs(act, PAIR_V, PAIR_GLU, glu_gate, None)
            act_pairs(act, PAIR_GLU, PAIR_IN, gate_out(0), gate_out(1))

        @block.tensor
        def _(pe):
            pe.sem_inc(mm_done, 2)
            pe.wait_ge(fill0, 3)
            pe_norm(pe, KD, NT, work, 0)
            pe.wait_ge(norm_split0, 1)
            pe_pairs(pe, 0, PAIR_IN, h, NT)

        @block.vector
        def _(dve):
            dve.sem_inc(lo_done, RAW)
            dve.sem_inc(glu_done, 1)
            dve.wait_ge(vec_in, 16 * (5 + KC))
            dve_rstd(dve, NT, root, rstd, tmp, 1, D, 0)
            dve_norm_split(dve, x, h, NT, work, rstd, 0, 0)
            vwait(dve)
            dve.sem_inc(norm_split0, 1)
            dve.wait_ge(part_ready, 1)
            vchain(nc.vector.tensor_copy(page_f[:], pages[:]))
            vwait(dve)
            nc.vector.tensor_scalar(rows[:], page_f[:], float(P), part[:, 0:1], ALU.mult,
                                    ALU.add).then_inc(rows_ready, 1)
            dve.wait_ge(hi_done, RAW + 1)
            nc.vector.tensor_tensor(lo[0][:], raw[:, 0], hi[0][:].bitcast(F32), ALU.subtract).then_inc(lo_done, 1)
            with dve.Fori(0, PAIR_V) as i:
                for k in range(1, 5):
                    split_lo(dve, 4 * i + k, k)
            with dve.Fori(PAIR_V, PAIR_GLU) as i:
                for k in range(1, 5):
                    split_lo(dve, 4 * i + k, k)
                dve.wait_ge(mm_done, 4 * i + 6)
                dve.wait_ge(tile_free[0], i + 2)
                c = i - PAIR_V
                nc.vector.tensor_tensor(cv[:, c, PADC + META:], ps[:, 1, 0:SEQ], sg[:, 0:SEQ], ALU.mult)\
                    .then_inc(conv_done, 1)
                nc.vector.tensor_tensor(cv[:, c, PADC:PADC + META], ps[:, 1, LIVE:NT], sg[:, LIVE:NT], ALU.mult)\
                    .then_inc(conv_done, 1)
                nc.vector.tensor_tensor(st[:, c, :, PADC], ps[:, 1, SEQ:LIVE], sg[:, SEQ:LIVE], ALU.mult)\
                    .then_inc(conv_done, 1)
                dve.wait_ge(conv_done, 3 * (i - PAIR_V) + 3)
                dve.sem_inc(glu_done, 1)
                dve.sem_inc(tile_free[1], 1)
            dve.wait_ge(const_ready, 5 + KC)

            def tap(j, k):
                return nc.vector.scalar_tensor_tensor(out=yc[:, j, 0:SEQ], in0=cv[:, j, bass.ds(k + META, SEQ)],
                                                      scalar=dw[:, j, bass.ds(k, 1)], in1=yc[:, j, 0:SEQ],
                                                      op0=ALU.mult, op1=ALU.add)
            for j in range(KC):
                nc.vector.tensor_scalar(yc[:, j, 0:SEQ], cv[:, j, META:META + SEQ], dw[:, j, 0:1], cvec[:, 0, j:j + 1],
                                        ALU.mult, ALU.add).then_inc(tap_done, 1)
            with dve.Fori(PAIR_GLU, PAIR_IN - 1) as i:
                for k in range(1, 5):
                    split_lo(dve, 4 * i + k, k)
                    for j in range(4 * ((k - 1) % 2), 4 * ((k - 1) % 2) + 4):
                        dve.wait_ge(tap_done, 2 * KC * (i - PAIR_GLU) + KC * ((k - 1) // 2) + j + 1)
                        tap(j, 2 * (i - PAIR_GLU) + (k - 1) // 2 + 1).then_inc(tap_done, 1)
            for k in range(1, 5):
                split_lo(dve, 4 * (PAIR_IN - 1) + k, k)
            for j in range(KC):
                vchain(nc.vector.tensor_tensor(stp[:], st[:, j], spread(dw[:, j], 1, DEC), ALU.mult))
                vwait(dve)
                vchain(nc.vector.tensor_reduce(yc[:, j, SEQ:LIVE], stp[:], AX_X, ALU.add))
                vwait(dve)
                vchain(nc.vector.tensor_scalar(yc[:, j, SEQ:LIVE], yc[:, j, SEQ:LIVE], cvec[:, 0, j:j + 1],
                                               None, ALU.add))
            vwait(dve)

    page_in = [sem(f"page_in{s}") for s in range(4)]
    page_used, dg_ready, qb_ready, zd_done = sem("page_used"), sem("dg_ready"), sem("qb_ready"), sem("zd_done")
    vt_ready, vn_ready = sem("vt_ready"), sem("vn_ready")
    d_act, d_vec, d_pe, d_vec2 = sem("d_act"), sem("d_vec"), sem("d_pe"), sem("d_vec2")
    aexp_done, z_kept = sem("aexp_done"), sem("z_kept")
    z_ready, relu_done, abs_done, ln_done = sem("z_ready"), sem("relu_done"), sem("abs_done"), sem("ln_done")
    sp_ready, t_ready, e_done = sem("sp_ready"), sem("t_ready"), sem("e_done")
    o_ready, o_done = sem("o_ready"), sem("o_done")
    mu_ready, cen_done, silu_done, nrm_done = sem("mu_ready"), sem("cen_done"), sem("silu_done"), sem("nrm_done")
    NG = HEADS // GH
    NP = DEC * PAGES

    with nc.Block() as block:
        @block.sync
        def _(sp):
            sp.dma_start(kvT.rearrange("(j p) t -> p j t", p=P), qkv[:, KA:3 * KA, :]).then_inc(kv_done, 16)
            sp.dma_start(conv_p.rearrange("(j p) t -> p j t", p=P), cv[:, :, META + SEQ:]).then_inc(kv_done, 16)
            for j in range(KC):
                sp.dma_start(conv_s[:, j], st[:, j, :, 1:TAPS]).then_inc(kv_done, 16)
            sp.wait_ge(kv_done, 16 * (2 + KC))

        @block.gpsimd
        def _(pool):
            pool.wait_ge(rows_ready, 1)
            pool.wait_ge(kv_done, 16 * (2 + KC))
            for n in range(2 * NP):
                if n >= 4:
                    pool.wait_ge(page_used, n - 3)
                cache = cache_k if n < NP else cache_v
                nc.gpsimd.indirect_dma_start(
                    ring[:, n % 4, :], None, cache,
                    bass.IndirectOffsetOnAxis(ap=rows[:, n % NP:n % NP + 1], axis=0)).then_inc(page_in[n % 4], 16)

        @block.tensor
        def _(pe):
            for blk in range(3):
                at_col, n = ((0, P), (P, P), (LIVE, META))[blk]
                for j in range(KA):
                    m = pe.transpose(ps[0:n, 2 * blk + j // 4, P * (j % 4):P * (j % 4) + P],
                                     qkv[:, 2 * KA + j, at_col:at_col + n], ident[:])
                m.then_inc(vt_ready, 1)
            pe.wait_ge(vn_ready, 3)
            for b in range(DEC):
                pe.wait_ge(dg_ready, b + 1)
                if b >= 2:
                    pe.wait_ge(page_used, 2 * (b - 1))
                for c in range(2):
                    m = pe.matmul(ps[:, 2 * (b % 2) + c, :], ones[:], dg[:, b % 2, 4 * c:4 * c + 4, :],
                                  start=True, stop=True)
                m.then_inc(qb_ready, 1)
            pe.wait_ge(d_vec, 2)
            pe.matmul(ps[:, 4, 0:256], neg_tri[:], sd[:], start=True, stop=False)
            pe.matmul(ps[:, 4, 0:256].rearrange("p (b g h) -> p b g h", b=DEC, g=PAGES)[:, :, 0, :], neg_ones[:],
                      sd[:, :, 1, :], start=False, stop=True).then_inc(d_pe, 1)
            for b in range(DEC):
                pe.wait_ge(d_act, 4)
                for g in range(PAGES):
                    n = NP + 2 * b + g
                    pe.wait_ge(page_in[n % 4], 16 * (n // 4 + 1))
                for j in range(KA):
                    for g in range(PAGES):
                        n = NP + 2 * b + g
                        m = pe.matmul(ps[:, 5, 16 * j + 2 * b:16 * j + 2 * b + 2], ring[:, n % 4, P * j:P * j + P],
                                      ed[:, b, g, 2 * j:2 * j + 2], start=g == 0, stop=g == 1)
                m.then_inc(page_used, 2)

            def scores(h0, out_ab, out_m, stop):
                j, r = h0 // 2, HD * (h0 % 2)
                q, k = qkv[r:r + HD, j], qkv[r:r + HD, KA + j]
                return (out_ab, k[:, 0:P], q[:, 0:SEQ]), (out_ab, k[:, P:SEQ], q[:, P:SEQ]), \
                    (out_m, k[:, LIVE:NT], q[:, 0:SEQ])

            pe.wait_ge(d_vec, 3)
            for g in range(NG):
                if g >= 1:
                    pe.wait_ge(o_done, g)
                for i in range(GH):
                    a, b, c = scores(GH * g + i, i, 4 + i, True)
                    pe.matmul(ps[:, i, 0:256], a[1], a[2], start=True, stop=True)
                    pe.matmul(ps[:, i, 256:384], b[1], b[2], start=True, stop=True)
                    pe.matmul(ps[0:META, 4 + i, 0:256], c[1], c[2], start=True, stop=True).then_inc(z_ready, 1)
                pe.wait_ge(sp_ready, g + 1)
                for i in range(GH):
                    a, b, c = scores(GH * g + i, i, 4 + i, False)
                    pe.matmul(ps[:, i, 0:256], a[1], a[2], start=True, stop=False)
                    pe.matmul(ps[:, i, 0:256], neg_tri[:], sab[:, i, 0:256], start=False, stop=False)
                    pe.matmul(ps[:, i, 0:P], ident[:], pen[:], start=False, stop=False)
                    pe.matmul(ps[:, i, P:256], neg_ones[:], sab[:, i, 256:384], start=False, stop=True)
                    pe.matmul(ps[:, i, 256:384], b[1], b[2], start=True, stop=False)
                    pe.matmul(ps[:, i, 256:384], ident[:], pen[:], start=False, stop=False)
                    pe.matmul(ps[:, i, 256:384], neg_tri[:], sab[:, i, 256:384], start=False, stop=True)
                    o = ps[0:META, 4 + i, 0:256]
                    pe.matmul(o, c[1], c[2], start=True, stop=False)
                    pe.matmul(o, neg_tri[0:META, 0:META], sm[:, i, :], start=False, stop=False)
                    pe.matmul(o, neg_ones[:, 0:META], sab[:, i, 0:256], start=False, stop=False)
                    pe.matmul(ps[0:META, 4 + i, P:256], neg_ones[:, 0:META], sab[:, i, 256:384], start=False,
                              stop=True).then_inc(t_ready, 1)
                pe.wait_ge(aexp_done, 2 * GH * (g + 1))
                for i in range(GH):
                    h0 = GH * g + i
                    r = HD * (i % 2)
                    o = ps[r:r + HD, i // 2, 0:256]
                    pe.matmul(o, vn[:, 0, HD * h0:HD * h0 + HD], eab[:, i, 0:256], start=True, stop=False)
                    pe.matmul(ps[r:r + HD, i // 2, P:256], vn[:, 1, HD * h0:HD * h0 + HD], eab[:, i, 256:384],
                              start=False, stop=False)
                    m = pe.matmul(o, vn[0:META, 2, HD * h0:HD * h0 + HD], em[:, i, :], start=False, stop=True)
                m.then_inc(o_ready, 1)
            for j in range(KC):
                m = pe.matmul(ps[:, 6, 0:LIVE], ones[:], yc[:, j, :], start=j == 0, stop=j == KC - 1)
            m.then_inc(mu_ready, 1)
            pe_norm(pe, KC, LIVE, work, KD)

        @block.scalar
        def _(act):
            for blk in range(3):
                n = (P, P, META)[blk]
                act.wait_ge(vt_ready, blk + 1)
                nc.scalar.copy(vn[0:n, blk, :], ps[0:n, 2 * blk:2 * blk + 2, :].rearrange("p a b -> p (a b)"))\
                    .then_inc(vn_ready, 1)
            act.wait_ge(d_vec, 1)
            nc.scalar.activation(ed[:], zd[:], ACT.Abs).then_inc(d_act, 1)
            act.wait_ge(d_act, 1)
            nc.scalar.activation(ed[:], ed[:], ACT.Exp, scale=-1.0).then_inc(d_act, 1)
            act.wait_ge(d_act, 2)
            nc.scalar.activation(ed[:], ed[:], ACT.Ln, bias=1.0).then_inc(d_act, 1)
            act.wait_ge(d_vec2, 1)
            nc.scalar.activation(ed[:], zd[:], ACT.Exp).then_inc(d_act, 1)
            for g in range(NG):
                for i in range(GH):
                    b = bias[:, GH * g + i:GH * g + i + 1]
                    act.wait_ge(z_ready, GH * g + i + 1)
                    nc.scalar.activation(eab[:, i, :], ps[:, i, 0:384], ACT.Identity, bias=b).then_inc(z_kept, 1)
                    nc.scalar.activation(em[:, i, :], ps[0:META, 4 + i, 0:256], ACT.Identity, bias=b[0:META])\
                        .then_inc(z_kept, 1)
                act.wait_ge(relu_done, 2 * g + 2)
                nc.scalar.activation(eab[:], eab[:], ACT.Abs).then_inc(abs_done, 1)
                nc.scalar.activation(em[:], em[:], ACT.Abs).then_inc(abs_done, 1)
                act.wait_ge(abs_done, 2 * g + 2)
                nc.scalar.activation(eab[:], eab[:], ACT.Exp, scale=-1.0).then_inc(e_done, 1)
                nc.scalar.activation(em[:], em[:], ACT.Exp, scale=-1.0).then_inc(e_done, 1)
                act.wait_ge(e_done, 2 * g + 2)
                nc.scalar.activation(eab[:], eab[:], ACT.Ln, bias=1.0).then_inc(ln_done, 1)
                nc.scalar.activation(em[:], em[:], ACT.Ln, bias=1.0).then_inc(ln_done, 1)
                for i in range(GH):
                    b = bias[:, GH * g + i:GH * g + i + 1]
                    act.wait_ge(t_ready, GH * g + i + 1)
                    nc.scalar.activation(eab[:, i, :], ps[:, i, 0:384], ACT.Exp, bias=b).then_inc(aexp_done, 1)
                    nc.scalar.activation(em[:, i, :], ps[0:META, 4 + i, 0:256], ACT.Exp, bias=b[0:META])\
                        .then_inc(aexp_done, 1)
            act.wait_ge(cen_done, KC)
            act_norm(act, yc, KC, LIVE, work, root, KD, DC, 1)
            for j in range(KC):
                act.wait_ge(nrm_done, j + 1)
                nc.scalar.activation(yc[:, j, :], yc[:, j, :], ACT.Silu, bias=cvec[:, 2, j:j + 1],
                                     scale=cvec[:, 1, j:j + 1]).then_inc(silu_done, 1)

        @block.vector
        def _(dve):
            def diag(b):
                if b >= 2:
                    dve.wait_ge(qb_ready, b - 1)
                nc.vector.tensor_tensor(dg[:, b % 2], spread(ident[:], 1, KA),
                                        spread(qkv[:, 0:KA, SEQ + b], 2, P), ALU.mult).then_inc(dg_ready, 1)
            dve.wait_ge(const_ready, 10 + KC)
            dve.wait_ge(kv_done, 16 * (2 + KC))
            diag(0)
            for b in range(DEC):
                if b + 1 < DEC:
                    diag(b + 1)
                dve.wait_ge(qb_ready, b + 1)
                for g in range(PAGES):
                    n = 2 * b + g
                    dve.wait_ge(page_in[n % 4], 16 * (n // 4 + 1))
                    if n >= 1:
                        vwait(dve)
                    nc.vector.tensor_tensor(prod[:], ring[:, n % 4, :],
                                            ps[:, 2 * (b % 2):2 * (b % 2) + 2, :].rearrange("p a b -> p (a b)"),
                                            ALU.mult).then_inc(page_used, 1)
                    dve.wait_ge(page_used, n + 1)
                    vchain(nc.vector.tensor_reduce(zd[:, b, g, :], prod[:].rearrange("p (h d) -> p h d", h=HEADS),
                                                   AX_X, ALU.add))
            vwait(dve)
            vchain(nc.vector.tensor_tensor(zd[:], zd[:], spread(spread(bias[:], 1, PAGES), 1, DEC), ALU.add))
            vwait(dve)
            nc.vector.tensor_scalar(sd[:], zd[:], 0.0, None, ALU.max).then_inc(d_vec, 1)
            dve.wait_ge(d_act, 3)
            dve.wait_ge(d_vec, 1)
            nc.vector.tensor_tensor(sd[:], sd[:], ed[:], ALU.add).then_inc(d_vec, 1)
            dve.wait_ge(d_pe, 1)
            nc.vector.tensor_tensor(zd[:].rearrange("p b g h -> p (b g h)"), ps[:, 4, 0:256],
                                    zd[:].rearrange("p b g h -> p (b g h)"), ALU.add).then_inc(d_vec2, 1)
            dve.wait_ge(page_used, 2 * NP)
            for r in range(2):
                ins = nc.vector.tensor_copy(
                    attn[HD * r:HD * r + HD, :, SEQ:LIVE],
                    ps[HD * r:HD * r + HD, 5, 0:P].rearrange("p (j b r) -> p j b r", j=KA, b=DEC)[:, :, :, r])
                if r == 0:
                    vchain(ins)
            ins.then_inc(d_vec, 1)
            for g in range(NG):
                dve.wait_ge(z_kept, 2 * GH * (g + 1))
                nc.vector.tensor_scalar(sab[:], eab[:], 0.0, None, ALU.max).then_inc(relu_done, 1)
                nc.vector.tensor_scalar(sm[:], em[:], 0.0, None, ALU.max).then_inc(relu_done, 1)
                dve.wait_ge(relu_done, 2 * g + 2)
                dve.wait_ge(ln_done, 2 * g + 2)
                vchain(nc.vector.tensor_tensor(sm[:], sm[:], em[:], ALU.add))
                vchain(nc.vector.tensor_tensor(sab[:], sab[:], eab[:], ALU.add))
                vwait(dve)
                for c in (0, 256):
                    vchain(nc.vector.tensor_tensor(sab[:, :, c:c + P], sab[:, :, c:c + P], spread(mask[:], 1, GH),
                                                   ALU.mult))
                vwait(dve)
                dve.sem_inc(sp_ready, 1)
                dve.wait_ge(o_ready, g + 1)
                nc.vector.tensor_copy(attn[:, GH // 2 * g:GH // 2 * (g + 1), 0:SEQ], ps[:, 0:2, 0:256])\
                    .then_inc(o_done, 1)
            dve.wait_ge(mu_ready, 1)
            for j in range(KC):
                nc.vector.scalar_tensor_tensor(out=yc[:, j, :], in0=ps[:, 6, 0:LIVE], scalar=-1.0 / DC,
                                               in1=yc[:, j, :], op0=ALU.mult, op1=ALU.add).then_inc(cen_done, 1)
            dve.wait_ge(cen_done, KC)
            dve_rstd(dve, LIVE, root, rstd, tmp, 2, DC, 1)
            for j in range(KC):
                nc.vector.tensor_tensor(yc[:, j, :], yc[:, j, :], rstd[:, 0:LIVE], ALU.mult).then_inc(nrm_done, 1)

    br_hi, br_lo, t1_done, mixed_done, mx_hi = (sem("br_hi"), sem("br_lo"), sem("t1_done"), sem("mixed_done"),
                                                sem("mx_hi"))
    mx_lo, x2_done, h2_ready, spill_done = sem("mx_lo"), sem("x2_done"), sem("h2_ready"), sem("spill_done")
    with nc.Block() as block:
        @block.sync
        def _(sp):
            with sp.Fori(PAIR_IN + 1, PAIR_OUT + 1) as i:
                for s in range(RAW):
                    load_half(sp, 4 * i + s, s, a_halves[4 * i + s])
            sp.wait_ge(x2_done, KD)
            sp.dma_start(x2_dram, x[:, :, 0:LIVE]).then_inc(spill_done, 16)
            sp.wait_ge(spill_done, 16)

        @block.scalar
        def _(act):
            nc.scalar.copy(at_p[0][:], attn[:]).then_inc(br_hi, 1)
            nc.scalar.copy(cv_p[0][:], yc[:]).then_inc(br_hi, 1)

            def mixed_hi(b):
                def f(i):
                    t = 2 * (i - PAIR_IN) + b
                    act.wait_ge(mixed_done, t + 1)
                    nc.scalar.copy(mx[0][:, t, :], gates[:, t, :]).then_inc(mx_hi, 1)
                return f
            act_pairs(act, PAIR_IN, PAIR_BR, mixed_hi(0), mixed_hi(1))
            act_pairs(act, PAIR_BR, PAIR_OUT, None, None)
            act.wait_ge(x2_done, KD)
            act_norm(act, x, KD, LIVE, work2, root, KD + KC, D, 0)
            act_norm_split(act, h2, LIVE, work2, KD)

        @block.tensor
        def _(pe):
            pe.wait_ge(br_lo, 2)
            with pe.Fori(PAIR_IN, PAIR_BR) as i:
                for b in range(2):
                    pe.wait_ge(tile_free[b], i + 1)
                    half_products(pe, 4 * i + 2 * b, 2 * b, ps[:, 2 * b, 0:LIVE], at_p, 0, LIVE, True, True)
                    half_products(pe, 4 * i + 2 * b + 1, 2 * b + 1, ps[:, 2 * b + 1, 0:LIVE], cv_p, 0, LIVE,
                                  True, True)
            pe.wait_ge(mx_lo, KD)
            pe_pairs(pe, PAIR_BR, PAIR_OUT, mx, LIVE)
            pe_norm(pe, KD, LIVE, work2, KD + KC)

        @block.vector
        def _(dve):
            dve.wait_ge(br_hi, 1)
            nc.vector.tensor_tensor(at_p[1][:], attn[:], at_p[0][:].bitcast(F32), ALU.subtract).then_inc(br_lo, 1)
            dve.wait_ge(br_hi, 2)
            nc.vector.tensor_tensor(cv_p[1][:], yc[:], cv_p[0][:].bitcast(F32), ALU.subtract).then_inc(br_lo, 1)
            with dve.Fori(PAIR_IN, PAIR_BR) as i:
                for b in range(2):
                    split_lo(dve, 4 * i + 2 * b + 1, 2 * b + 1)
                    split_lo(dve, 4 * i + 2 * b + 2, 2 * b + 2)
                    t = 2 * (i - PAIR_IN) + b
                    dve.wait_ge(mm_done, 4 * i + 2 * b + 4)
                    nc.vector.tensor_tensor(t2[:, 0], gates[:, t, :], ps[:, 2 * b, 0:LIVE], ALU.mult)\
                        .then_inc(t1_done, 1)
                    nc.vector.tensor_tensor(t2[:, 1], gates[:, KD + t, :], ps[:, 2 * b + 1, 0:LIVE], ALU.mult)\
                        .then_inc(t1_done, 1)
                    dve.wait_ge(t1_done, 4 * (i - PAIR_IN) + 2 * b + 2)
                    nc.vector.tensor_tensor(gates[:, t, :], t2[:, 0], t2[:, 1], ALU.add).then_inc(mixed_done, 1)
                    dve.sem_inc(tile_free[b], 1)
                    dve.wait_ge(mx_hi, 2 * (i - PAIR_IN) + b + 1)
                    nc.vector.tensor_tensor(mx[1][:, t, :], gates[:, t, :], mx[0][:, t, :].bitcast(F32),
                                            ALU.subtract).then_inc(mx_lo, 1)
            with dve.Fori(PAIR_BR, PAIR_OUT) as i:
                for b in range(2):
                    split_lo(dve, 4 * i + 2 * b + 1, 2 * b + 1)
                    split_lo(dve, 4 * i + 2 * b + 2, 2 * b + 2)
                    t = 2 * (i - PAIR_BR) + b
                    dve.wait_ge(mm_done, 4 * i + 2 * b + 4)
                    nc.vector.tensor_tensor(x[:, t, 0:LIVE], x[:, t, 0:LIVE], ps[:, b, 0:LIVE], ALU.add)\
                        .then_inc(x2_done, 1)
                    dve.wait_ge(x2_done, 2 * (i - PAIR_BR) + b + 1)
                    dve.sem_inc(tile_free[b], 1)
            dve.wait_ge(x2_done, KD)
            dve_rstd(dve, LIVE, root, rstd, tmp, 3, D, 0)
            dve_norm_split(dve, x, h2, LIVE, work2, rstd, 1, KD)
            vwait(dve)

    sk_in, qry_done, sc_ready, sc_done, zero_done = (sem("sk_in"), sem("qry_done"), sem("sc_ready"),
                                                     sem("sc_done"), sem("zero_done"))
    half_scores = sem("half_scores")
    with nc.Block() as block:
        @block.sync
        def _(sp):
            sp.dma_start(skT, sub_keysT).then_inc(sk_in, 16)
            with sp.Fori(PAIR_OUT + 1, PAIR_QRY) as i:
                for s in range(RAW):
                    load_half(sp, 4 * i + s, s, a_halves[4 * i + s])
            for s in range(RAW):
                load_half(sp, 4 * PAIR_QRY + s, s, u_tiles[s])

        @block.gpsimd
        def _(pool):
            nc.gpsimd.memset(sc_all[:, 2], 0.0).then_inc(zero_done, 1)

        @block.scalar
        def _(act):
            def keep(b):
                def f(i):
                    nc.scalar.copy(qry[:, b, :], ps[:, b, 0:LIVE]).then_inc(tile_free[b], 1)
                return f
            act_pairs(act, PAIR_OUT, PAIR_QRY, keep(0), keep(1))

        @block.tensor
        def _(pe):
            pe.wait_ge(sk_in, 16)
            with pe.Fori(PAIR_OUT, PAIR_QRY) as i:
                for b in range(2):
                    for hf in range(2):
                        half_products(pe, 4 * i + 2 * b + hf, 2 * b + hf, ps[:, b, 0:LIVE], h2, HALF * hf, LIVE,
                                      hf == 0, hf == 1)
                    pe.wait_ge(tile_free[b], i + 2)
                    pe.wait_ge(sc_done, 2 * (i - PAIR_OUT) + b + 1)
                    for t in range(TT):
                        n = (P, P, DEC)[t]
                        m = pe.matmul(ps[0:n, 2 + b, P * t:P * t + P], qry[:, b, P * t:P * t + n], skT[:, b, :],
                                      start=True, stop=True)
                    m.then_inc(sc_ready, 1)

        @block.vector
        def _(dve):
            dve.sem_inc(sc_done, 2)
            dve.wait_ge(zero_done, 1)

            def keep_scores(i, b):
                q = 2 * (i - PAIR_OUT) + b
                dve.wait_ge(sc_ready, q + 1)
                vq = nc.vector.tensor_copy(sc_all[:, 0:2, q, :], ps[:, 2 + b, 0:256])
                vq.then_inc(half_scores, 1)
                nc.vector.tensor_copy(sc_all[0:DEC, 2, q, :], ps[0:DEC, 2 + b, 256:384]).then_inc(half_scores, 1)
                dve.wait_ge(half_scores, 2 * q + 2)
                dve.sem_inc(sc_done, 1)
            with dve.Fori(PAIR_OUT, PAIR_QRY) as i:
                split_lo(dve, 4 * i + 1, 1)
                split_lo(dve, 4 * i + 2, 2)
                keep_scores(i, 0)
                split_lo(dve, 4 * i + 3, 3)
                split_lo(dve, 4 * i + 4, 4)
                keep_scores(i, 1)

    route, route_seen = sem("route"), sem("route_seen")
    with nc.Block() as block:
        @block.sync
        def _(sp):
            with sp.Fori(PAIR_QRY + 1, PAIR_U) as i:
                for s in range(RAW):
                    load_half(sp, 4 * i + s, s, u_tiles[4 * (i - PAIR_QRY) + s])
            for s in range(RAW):
                load_half(sp, 4 * PAIR_U + s, s, expert_v[0, s])

        @block.scalar
        def _(act):
            def gelu(b):
                def f(i):
                    nc.scalar.activation(W[:, 2 * (i - PAIR_QRY) + b, :], ps[:, b, 0:LIVE],
                                         ACT.Gelu_apprx_tanh).then_inc(tile_free[b], 1)
                return f
            act_pairs(act, PAIR_QRY, PAIR_U, gelu(0), gelu(1))

        @block.tensor
        def _(pe):
            pe_pairs(pe, PAIR_QRY, PAIR_U, h2, LIVE)

        @block.vector
        def _(dve):
            STEPS = 1 + TT * 2 * 5 + 2 + TT * 5 + 4 + 2 * 3
            with dve.Fori(0, PH) as hd:
                count = [0]

                def step(ins):
                    count[0] += 1
                    ins.then_inc(route, 1)

                def after():
                    dve.wait_ge(route, STEPS * hd + count[0])
                    dve.sem_inc(route_seen, 1)

                def lo_part(k):
                    split_lo(dve, 4 * PAIR_QRY + 4 * HEAD_PAIRS * hd + k, k)

                def top8(dst, idx, src):
                    step(nc.vector.max(dst, src))
                    after()
                    step(nc.vector.max_index(idx.bitcast(U32), dst, src))

                def drop8(dst, src):
                    step(nc.vector.match_replace(src, dst, src, NEG_BIG))
                    after()

                k = 0
                step(nc.vector.tensor_copy(sh, sc_all[:, :, bass.ds(2 * hd, 2), :]))
                after()
                for t in range(TT):
                    for q in range(2):
                        s, v, ix = sh[:, t, q, :], top1[:, t, q, :], idx1[:, t, q, :]
                        k += 1
                        lo_part(k)
                        top8(v[:, 0:8], ix[:, 0:8], s)
                        drop8(v[:, 0:8], s)
                        k += 1
                        lo_part(k)
                        top8(v[:, 8:16], ix[:, 8:16], s)
                after()
                k += 1
                lo_part(k)
                step(nc.vector.tensor_tensor(cand, spread(top1[:, :, 0, :], 3, PK), spread(top1[:, :, 1, :], 2, PK),
                                             ALU.add))
                step(nc.vector.tensor_copy(idx1f, idx1.bitcast(U32)))
                after()
                for t in range(TT):
                    s = cand[:, t].rearrange("p a b -> p (a b)")
                    top8(top2[:, t, 0:8], pos2[:, t, 0:8], s)
                    drop8(top2[:, t, 0:8], s)
                    k += 1
                    lo_part(k)
                    top8(top2[:, t, 8:16], pos2[:, t, 8:16], s)
                after()
                step(nc.vector.tensor_scalar(pab[:, 0].bitcast(U32), pos2.bitcast(U32), 4, None,
                                             ALU.logical_shift_right))
                step(nc.vector.tensor_scalar(pab[:, 1].bitcast(U32), pos2.bitcast(U32), 15, None,
                                             ALU.bitwise_and))
                after()
                step(nc.vector.tensor_copy(pabf, pab.bitcast(U32)))
                step(nc.vector.tensor_copy(chosen[:, 2, :, bass.ds(hd, 1), :],
                                           top2.rearrange("p t (o k) -> p t o k", o=1)))
                after()
                for q in range(2):
                    k += 1
                    lo_part(k)
                    after()
                    ranks = spread(spread(iota[:, 0:PK], 1, PK), 1, TT)
                    step(nc.vector.tensor_tensor(eq, spread(pabf[:, q], 3, PK), ranks, ALU.is_equal))
                    after()
                    step(nc.vector.tensor_tensor(eq, eq, spread(idx1f[:, :, q, :], 2, PK), ALU.mult))
                    after()
                    step(nc.vector.tensor_reduce(chosen[:, q, :, bass.ds(hd, 1), :].rearrange("p t o k -> p t (o k)"),
                                                 eq, AX_X, ALU.add))
                after()
                while k < 4 * HEAD_PAIRS:
                    k += 1
                    lo_part(k)
                assert k == 4 * HEAD_PAIRS and count[0] == STEPS, (k, count[0], STEPS)
            with dve.Fori(PAIR_QRY + PH * HEAD_PAIRS, PAIR_U) as i:
                for k in range(1, 5):
                    split_lo(dve, 4 * i + k, k)

    soft = sem("soft")
    soft_act, tr_ready, ch_done = sem("soft_act"), sem("tr_ready"), sem("ch_done")
    l_ready, r_ready, g_ready, g_used = sem("l_ready"), sem("r_ready"), sem("g_ready"), sem("g_used")
    left_one, diff_done, diff_seen = sem("left_one"), sem("diff_done"), sem("diff_seen")
    with nc.Block() as block:
        @block.scalar
        def _(act):
            act.wait_ge(soft, 2)
            nc.scalar.activation(chosen[:, 2], chosen[:, 2], ACT.Exp).then_inc(soft_act, 1)

        @block.gpsimd
        def _(pool):
            pool.sem_inc(g_used, 2)
            pool.wait_ge(ch_done, 3)
            with pool.Fori(0, LIVE // 8) as i:
                for b in range(2):
                    pool.wait_ge(g_ready, 2 * i + b + 1)
                    nc.gpsimd.tensor_tensor(rdiff[:, b], spread(iota[:], 1, 4),
                                            spread(chT[:, 1, bass.ds(8 * i + 4 * b, 4)], 2, NK),
                                            ALU.subtract).then_inc(diff_done, 1)
                    pool.wait_ge(diff_done, 2 * i + b + 1)
                    pool.sem_inc(diff_seen, 1)
                    nc.gpsimd.tensor_scalar(rhot[:, b], rdiff[:, b], 0.0, None, ALU.is_equal).then_inc(r_ready, 1)

        @block.tensor
        def _(pe):
            pe.sem_inc(g_ready, 2)
            pe.wait_ge(soft, 5)
            for t in range(TT):
                n = (P, P, DEC)[t]
                for q in range(3):
                    m = pe.transpose(ps[:, q, P * t:P * t + n],
                                     chosen[0:n, q, t].rearrange("p h k -> p (h k)"), ident[0:n, 0:n])
            m.then_inc(tr_ready, 1)
            with pe.Fori(0, LIVE // 8) as i:
                for b in range(2):
                    pe.wait_ge(l_ready, 2 * i + b + 1)
                    pe.wait_ge(r_ready, 2 * i + b + 1)
                    pe.wait_ge(g_used, 2 * i + b + 1)
                    for t in range(4):
                        m = pe.matmul(ps[:, 4 + b, NK * t:NK * t + NK], lhot[:, b, t], rhot[:, b, t],
                                      start=True, stop=True)
                    m.then_inc(g_ready, 1)

        @block.vector
        def _(dve):
            sc = chosen[:, 2]
            nc.vector.tensor_copy(sums[:, 0], sc[:, :, :, 0]).then_inc(soft, 1)
            dve.wait_ge(soft, 1)
            nc.vector.tensor_tensor(sc, sc, spread(sums[:, 0], 3, PK), ALU.subtract).then_inc(soft, 1)
            dve.wait_ge(soft_act, 1)
            nc.vector.tensor_reduce(sums[:, 0], sc, AX_X, ALU.add).then_inc(soft, 1)
            dve.wait_ge(soft, 3)
            nc.vector.reciprocal(sums[:, 1], sums[:, 0]).then_inc(soft, 1)
            dve.wait_ge(soft, 4)
            nc.vector.tensor_tensor(sc, sc, spread(sums[:, 1], 3, PK), ALU.mult).then_inc(soft, 1)
            dve.wait_ge(tr_ready, 1)
            for q in range(3):
                nc.vector.tensor_copy(chT[:, q, :], ps[:, q, 0:LIVE]).then_inc(ch_done, 1)
            dve.wait_ge(ch_done, 3)

            def left(tok, b, t):
                return nc.vector.tensor_scalar(lhot[:, b, t], iota[:], chT[:, 0, bass.ds(tok, 1)],
                                               chT[:, 2, bass.ds(tok, 1)], ALU.is_equal, ALU.mult)
            for b in range(2):
                for t in range(4):
                    left(4 * b + t, b, t).then_inc(left_one, 1)
                dve.wait_ge(left_one, 4 * b + 4)
                dve.sem_inc(l_ready, 1)

            def weigh(i, b):
                dve.wait_ge(g_ready, 2 + 2 * i + b + 1)
                wv = W[:, :, bass.ds(8 * i + 4 * b, 4)]
                nc.vector.tensor_tensor(wv, wv, ps[:, 4 + b, :].rearrange("p (t n) -> p n t", t=4),
                                        ALU.mult).then_inc(g_used, 1)
            with dve.Fori(0, LIVE // 8 - 1) as i:
                for b in range(2):
                    dve.wait_ge(g_ready, 2 + 2 * i + b + 1)
                    for t in range(4):
                        left(8 * i + 8 + 4 * b + t, b, t).then_inc(left_one, 1)
                    weigh(i, b)
                    dve.wait_ge(left_one, 8 * i + 4 * b + 12)
                    dve.sem_inc(l_ready, 1)
            for b in range(2):
                weigh(LIVE // 8 - 1, b)

    x2_in, whi_done, wlo_done, acc_done = sem("x2_in"), sem("whi_done"), sem("wlo_done"), sem("acc_done")
    C0 = 4 * PAIR_U
    with nc.Block() as block:
        @block.sync
        def _(sp):
            sp.dma_start(x2[:], x2_dram).then_inc(x2_in, 16)
            with sp.Fori(1, NK // 4) as i:
                for s in range(RAW):
                    load_half(sp, C0 + 4 * i + s, s, expert_v[0, 4 * i + s])
            with sp.Fori(0, NK // 4) as i:
                for s in range(RAW):
                    load_half(sp, C0 + NK + 4 * i + s, s, expert_v[1, 4 * i + s])

        @block.scalar
        def _(act):
            def f(c, n, k, v=True):
                if v:
                    split_hi(act, C0 + c, k)
                act.wait_ge(mm_done, C0 + c + 1)
                nc.scalar.copy(w_hi[k % 2][:], W[:, n, :]).then_inc(whi_done, 1)
            for p in range(2):
                if p == 0:
                    f(0, 0, 0, False)
                    for k in range(1, 4):
                        f(k, k, k)
                with act.Fori(1 - p, NK // 4) as i:
                    for k in range(4):
                        f(NK * p + 4 * i + k, 4 * i + k, k)

        @block.vector
        def _(dve):
            def f(c, n, k, v=True):
                if v:
                    split_lo(dve, C0 + c, k)
                dve.wait_ge(whi_done, c + 1)
                dve.wait_ge(mm_done, C0 + c + 1)
                nc.vector.tensor_tensor(w_lo[k % 2][:], W[:, n, :], w_hi[k % 2][:].bitcast(F32),
                                        ALU.subtract).then_inc(wlo_done, 1)
            dve.wait_ge(x2_in, 16)
            for p in range(2):
                if p == 0:
                    f(0, 0, 0, False)
                    for k in range(1, 4):
                        f(k, k, k)
                with dve.Fori(1 - p, NK // 4) as i:
                    for k in range(4):
                        f(NK * p + 4 * i + k, 4 * i + k, k)
                dve.wait_ge(mm_done, C0 + NK * (p + 1) + 2)
                nc.vector.tensor_tensor(x2[:, HALF * p:HALF * (p + 1), :], x2[:, HALF * p:HALF * (p + 1), :],
                                        ps[:, :, 0:LIVE], ALU.add).then_inc(acc_done, 1)

        @block.tensor
        def _(pe):
            def f(c, k, start, stop):
                pe.wait_ge(lo_done, C0 + c + RAW + 1)
                pe.wait_ge(wlo_done, c + 1)
                for j in range(HALF):
                    o = ps[:, j, 0:LIVE]
                    pe.matmul(o, hi[k % 2][:, j], w_hi[k % 2][:], start=start, stop=False, skip_group_check=True)
                    pe.matmul(o, hi[k % 2][:, j], w_lo[k % 2][:], start=False, stop=False, skip_group_check=True)
                    m = pe.matmul(o, lo[k % 2][:, j], w_hi[k % 2][:], start=False, stop=stop, skip_group_check=True)
                m.then_inc(mm_done, 1)
            for p in range(2):
                if p == 1:
                    pe.wait_ge(acc_done, 1)
                for k in range(4):
                    f(NK * p + k, k, k == 0, False)
                with pe.Fori(1, NK // 4 - 1) as i:
                    for k in range(4):
                        f(NK * p + 4 * i + k, k, False, False)
                for k in range(4):
                    f(NK * p + NK - 4 + k, k, False, k == 3)

    y_done = sem("y_done")
    with nc.Block() as block:
        @block.scalar
        def _(act):
            act_norm(act, x2, KD, LIVE, fin, fin_r[:, 0], 2 * KD + KC, D, 0)

        @block.tensor
        def _(pe):
            pe_norm(pe, KD, LIVE, fin, 2 * KD + KC)

        @block.vector
        def _(dve):
            dve_rstd(dve, LIVE, fin_r[:, 0], fin_r[:, 1], fin_r[:, 2], 4, D, 0)
            for j in range(KD):
                nc.vector.scalar_tensor_tensor(out=x2[:, j, :], in0=x2[:, j, :], scalar=gain[:, 2, j:j + 1],
                                               in1=fin_r[:, 1], op0=ALU.mult, op1=ALU.mult).then_inc(y_done, 1)

        @block.sync
        def _(sp):
            for q in range(4):
                sp.wait_ge(y_done, 4 * q + 4)
                sp.dma_start(yT[:, 4 * q:4 * q + 4], x2[:, 4 * q:4 * q + 4, :]).then_inc(out_done, 16)
            sp.wait_ge(out_done, 64)


def build(nc, arrays):
    args = {}
    for name, v in arrays.items():
        args[name] = nc.dram_tensor(name, v.shape, mybir.dt.from_np(v.dtype), kind="ExternalInput").ap()
    args["expert_v"] = args["expert_v"].rearrange("(a n) (h d) -> h n a d", a=NK, h=2)
    outs = {"yT": (P, KD, LIVE), "kvT": (2 * DA, NT), "conv_p": (DC, TAPS - 1), "conv_s": (P, KC, DEC, TAPS - 1)}
    for name, shape in outs.items():
        args[name] = nc.dram_tensor(name, shape, F32, kind="ExternalOutput").ap()
    trunk(nc, *args.values())


def kernel(**inputs):
    import numpy as np
    import concourse.bacc as bacc
    from concourse.bass_utils import run_bass_kernel_spmd

    def tiles(w):
        k, c = w.shape
        return w.reshape(k // (HALF * P), HALF, P, c // P, P).transpose(3, 0, 2, 1, 4)

    def columns(v):
        v = v.reshape(v.shape[:-1] + (v.shape[-1] // P, P))
        return np.moveaxis(v, -1, 0)

    a = {k: np.asarray(v) for k, v in inputs.items()}
    tokens = np.concatenate([a["x_prompt"][0], a["x_sample"][:, 0], a["meta_tokens"]], axis=0)
    w_in = tiles(a["w_in"][0])
    order = list(range(3 * KA))
    for c in range(KC):
        order += [3 * KA + KC + c, 3 * KA + c]
    order += list(range(3 * KA + 2 * KC, T_IN))
    w_br = np.concatenate([tiles(a["w_branch_attn"][0]), tiles(a["w_branch_conv"][0])], axis=1)
    weights = np.concatenate([w_in[order], w_br, tiles(a["w_out"][0]), tiles(a["w_query"][0])], axis=0)
    u = a["expert_u"][0].reshape(NK, NK, 2, HALF, P).transpose(1, 2, 4, 3, 0)
    arrays = {
        "weights": weights.reshape(-1, P, HALF * P),
        "xT": columns(tokens).transpose(0, 2, 1),
        "gains": columns(np.stack([a["norm_mix_g"][0], a["norm_ffn_g"][0], a["norm_final_g"]])),
        "u_tiles": u.reshape(-1, P, HALF * P),
        "expert_v": a["expert_v"][0],
        "cache_k": a["cache_k"][0].reshape(-1, DA),
        "cache_v": a["cache_v"][0].reshape(-1, DA),
        "stateT": columns(a["state_conv"][0]).transpose(0, 3, 1, 2),
        "page_table": np.broadcast_to(a["page_table"].reshape(1, -1), (P, DEC * PAGES)),
        "sb_bias": np.broadcast_to(a["sb_bias"], (P, HEADS)),
        "w_dwT": columns(a["w_dw"][0]).transpose(0, 2, 1),
        "conv_vecs": columns(np.stack([a["b_dw"][0], a["conv_ln_g"][0], a["conv_ln_b"][0]])),
        "sub_keysT": a["sub_keys"][0].transpose(2, 0, 1),
    }
    arrays = {k: np.ascontiguousarray(v) for k, v in arrays.items()}
    nc = bacc.Bacc("TRN2", target_bir_lowering=False, num_devices=1)
    build(nc, arrays)
    r = run_bass_kernel_spmd(nc, [arrays], core_ids=[0]).results[0]
    y = np.transpose(r["yT"], (2, 1, 0)).reshape(LIVE, D)
    kv = np.transpose(r["kvT"].reshape(2, HEADS, HD, NT), (0, 3, 1, 2))
    prompt = np.concatenate([kv[:, LIVE:], kv[:, :SEQ]], axis=1)[:, None, None]
    sample = kv[:, SEQ:LIVE][:, None, :, None]
    conv_prompt = np.transpose(r["conv_p"], (1, 0))[None, None]
    conv_sample = np.transpose(r["conv_s"], (2, 3, 1, 0)).reshape(1, DEC, TAPS - 1, DC)
    return (y[None, :SEQ], y[SEQ:, None], prompt[0], prompt[1], conv_prompt, sample[0], sample[1], conv_sample)
```

```python
from contextlib import ExitStack

import concourse.bass as bass
from concourse import mybir

F32 = mybir.dt.float32
F32R = mybir.dt.float32r
U32 = mybir.dt.uint32
I32 = mybir.dt.int32
ACT = mybir.ActivationFunctionType
ALU = mybir.AluOpType
AX_X = mybir.AxisListType.X

P = 128
D = 2048
KD = D // P
SEQ, DEC, META = 256, 8, 16
LIVE = SEQ + DEC
NT = LIVE + META
HEADS, HD = 16, 64
DA = HEADS * HD
KA = DA // P
DC = 1024
KC = DC // P
TAPS = 31
PAGES = 2
PH, PK = 8, 16
NK = 128
RMS_EPS, LN_EPS = 1e-6, 1e-5

HALF = 8
QT = HALF // 2
RAW, SPLIT = 4, 4
AHEAD = 3
T_IN, T_BR, T_OUT, T_QRY = 72, 16, 16, 16
PAIR_ATT = 24
PAIR_Q, PAIR_V, PAIR_GLU, PAIR_IN = 4, 12, 20, T_IN // 2
PAIR_BR = PAIR_IN + T_BR // 2
PAIR_OUT = PAIR_BR + T_OUT // 2
PAIR_QRY = PAIR_OUT + T_QRY // 2
PAIR_U = PAIR_QRY + NK // 2
HEAD_PAIRS = 5
SPARE_TILE = PH * HEAD_PAIRS * 2
GS = 6
TT = 3
NEG_BIG = -3.0e38
MASKED = -1.0e30


def spread(ap, at, count):
    wide = ap.unsqueeze(at)
    shape = list(wide.shape)
    shape[at] = count
    return wide.broadcast_to(shape)


def trunk(nc, *args):
    with ExitStack() as ctx:
        program(nc, ctx, *args)


def program(nc, ctx, weights, xT, gains, u_tiles, expert_v, cache_k, cache_v, stateT, page_table, sb_bias,
          w_dwT, conv_vecs, sub_keysT, yT, kvT, conv_p, conv_s):
    at = {}
    base = 16512

    def place(name, offset, shape, dt=F32):
        size = 4
        for n in shape[1:]:
            size *= n
        t = nc.alloc_sbuf_tensor_at(name, shape, dt, offset=base + offset)
        at[name] = -(-(offset + size) // 32) * 32
        return t

    raw = place("raw", 0, [P, RAW, HALF, P])
    hi = [place(f"hi{s}", at["raw"] + 2048 * s, [P, QT, P], F32R) for s in range(SPLIT)]
    lo = [place(f"lo{s}", at["hi3"] + 2048 * s, [P, QT, P], F32R) for s in range(SPLIT)]
    ident = place("ident", at["lo3"], [P, P])
    ones = place("ones", at["ident"], [P, P])
    neg_tri = place("neg_tri", at["ones"], [P, P])
    neg_ones = place("neg_ones", at["neg_tri"], [P, P])
    mask = place("mask", at["neg_ones"], [P, P])
    pen = place("pen", at["mask"], [P, P])
    iota = place("iota", at["pen"], [P, P])
    gain = place("gain", at["iota"], [P, 3, KD])
    dw = place("dw", at["gain"], [P, KC, TAPS])
    cvec = place("cvec", at["dw"], [P, 3, KC])
    bias = place("bias", at["cvec"], [P, HEADS])
    eps = place("eps", at["bias"], [P, 2])
    pages = place("pages", at["eps"], [P, DEC * PAGES], I32)
    page_f = place("page_f", at["pages"], [P, DEC * PAGES])
    part = place("part", at["page_f"], [P, 2])
    rows = place("rows", at["part"], [P, DEC * PAGES], I32)
    X = 38400
    assert at["rows"] <= X
    gates = place("gates", X, [P, 2 * KD, LIVE])
    h2 = [place("h2_hi", X, [P, KD, LIVE], F32R), place("h2_lo", X + 16896, [P, KD, LIVE], F32R)]
    Y = X + 33792
    x = place("x", Y, [P, KD, NT])
    yc = place("yc", at["x"], [P, KC, LIVE])
    attn = place("attn", at["yc"], [P, KA, LIVE])
    qkv = place("qkv", at["attn"], [P, 3 * KA, NT])
    work = place("work", at["qkv"], [P, 4, NT])
    rstd = place("rstd", at["work"], [P, NT])
    root = place("root", at["rstd"], [P, NT])
    tmp = place("tmp", at["root"], [P, NT])
    Z = at["tmp"]
    h = [place("h_hi", Z, [P, KD, NT], F32R), place("h_lo", Z + 17920, [P, KD, NT], F32R)]
    PADC = TAPS - 1
    cv = place("cv", at["h_lo"], [P, KC, PADC + META + SEQ])
    st = place("st", at["cv"], [P, KC, DEC, TAPS])
    sg = place("sg", at["st"], [P, NT])
    stp = place("stp", at["sg"], [P, DEC, TAPS])
    dg = place("dg", X, [P, KA, P])
    prod = place("prod", at["dg"], [P, DA])
    zd = place("zd", X + 8 * 1056, [P, DEC, PAGES, HEADS])
    ed = place("ed", at["zd"], [P, DEC, PAGES, HEADS])
    sd = place("sd", at["ed"], [P, DEC, PAGES, HEADS])
    ring = place("ring", X + 16 * 1056, [P, 4, DA])
    assert at["ring"] <= Y
    GH = 4
    eab = place("eab", Y, [P, GH, 384])
    sab = place("sab", at["eab"], [P, GH, 384])
    em = place("em", at["sab"], [META, GH, 256])
    assert at["em"] <= at["x"]
    sm = place("sm", at["stp"], [META, GH, 256])
    vn = place("vn", at["sm"], [P, 3, GH * HD])
    qg = place("qg", at["vn"], [P, 3, GH // 2, NT])
    assert at["qg"] <= 212800
    QK = at["attn"]
    at_p = [place("at_hi", QK, [P, KA, LIVE], F32R), place("at_lo", QK + 8448, [P, KA, LIVE], F32R)]
    cv_p = [place("cv_hi", QK + 16896, [P, KC, LIVE], F32R), place("cv_lo", QK + 25344, [P, KC, LIVE], F32R)]
    mx = [place("mx_hi", QK + 33792, [P, KD, LIVE], F32R), place("mx_lo", QK + 50688, [P, KD, LIVE], F32R)]
    t2 = place("t2", at["mx_lo"], [P, 2, LIVE])
    work2 = place("work2", at["t2"], [P, 4, LIVE])
    W = place("W", Y, [P, NK, LIVE])
    Wf = W[:].rearrange("p a b -> p (a b)")
    spare = SPARE_TILE * LIVE
    offs = [spare]

    def carve(n):
        a = offs[0]
        offs[0] += n
        return Wf[:, a:a + n]

    sc_all = carve(TT * 2 * PH * NK).rearrange("p (t q n) -> p t q n", t=TT, q=2 * PH)
    sh = carve(TT * 2 * NK).rearrange("p (t q n) -> p t q n", t=TT, q=2)
    cand = carve(TT * PK * PK).rearrange("p (t a b) -> p t a b", t=TT, a=PK)
    eq = carve(TT * PK * PK).rearrange("p (t a b) -> p t a b", t=TT, a=PK)
    top1 = carve(TT * 2 * PK).rearrange("p (t q k) -> p t q k", t=TT, q=2)
    idx1 = carve(TT * 2 * PK).rearrange("p (t q k) -> p t q k", t=TT, q=2)
    idx1f = carve(TT * 2 * PK).rearrange("p (t q k) -> p t q k", t=TT, q=2)
    top2 = carve(TT * PK).rearrange("p (t k) -> p t k", t=TT)
    pos2 = carve(TT * PK).rearrange("p (t k) -> p t k", t=TT)
    pab = carve(2 * TT * PK).rearrange("p (q t k) -> p q t k", q=2, t=TT)
    pabf = carve(2 * TT * PK).rearrange("p (q t k) -> p q t k", q=2, t=TT)
    assert offs[0] <= NK * LIVE
    qry = W[:, 30:32, :]
    skT = W[:, 32, 0:2 * NK].rearrange("p (q n) -> p q n", q=2)
    chosen = place("chosen", at["W"], [P, 3, TT, PH, PK])
    lhot = place("lhot", X, [P, GS, 4, NK])
    rhot = place("rhot", at["lhot"], [P, GS, 4, NK])
    rdiff = place("rdiff", at["rhot"], [P, 4, NK])
    ldiff = place("ldiff", at["rdiff"], [P, 2, 2, NK])
    chT = place("chT", at["ldiff"], [P, 4, LIVE])
    sums = place("sums", at["chT"], [P, 2, TT, PH])
    x2 = place("x2", X, [P, KD, LIVE])
    w_hi = [place(f"w_hi{s}", at["x2"] + 1056 * s, [P, LIVE], F32R) for s in range(2)]
    w_lo = [place(f"w_lo{s}", at["w_hi1"] + 1056 * s, [P, LIVE], F32R) for s in range(2)]
    fin = place("fin", Y, [P, 4, LIVE])
    fin_r = place("fin_r", at["fin"], [P, 3, LIVE])

    ps = ctx.enter_context(nc.psum_tensor("ps", [P, 8, 512], F32))
    x2_dram = nc.dram_tensor("x2_spill", [P, KD, LIVE], F32, kind="Internal").ap()

    def sem(name):
        return ctx.enter_context(nc.semaphore(name))

    raw_in = [sem(f"raw_in{s}") for s in range(RAW)]
    hi_done, lo_done, mm_done = sem("hi_done"), sem("lo_done"), sem("mm_done")
    tile_free = [sem("tile_free0"), sem("tile_free1")]
    vec_step = sem("vec_step")
    act_step = sem("act_step")
    steps = {"vec": 0, "act": 0}

    def vchain(ins):
        steps["vec"] += 1
        ins.then_inc(vec_step, 1)

    def vwait(dve):
        dve.wait_ge(vec_step, steps["vec"])

    a_halves = weights

    def load_half(sp, c, s, src):
        sp.wait_ge(hi_done, 2 * c + 2)
        sp.wait_ge(lo_done, 2 * c + 2)
        sp.dma_start(raw[:, s].rearrange("p a b -> p (a b)"), src).then_inc(raw_in[s], 16)

    def raw_quarter(k):
        return raw[:, k // 2 % RAW, QT * (k % 2):QT * (k % 2) + QT]

    def split_hi(act, q0, k):
        act.wait_ge(raw_in[k // 2 % RAW], 2 * q0 + 16 * (k // (2 * RAW)) + 16)
        act.wait_ge(mm_done, q0 + k + 1)
        nc.scalar.copy(hi[k % SPLIT][:], raw_quarter(k)).then_inc(hi_done, 1)

    def split_lo(dve, q0, k):
        dve.wait_ge(hi_done, q0 + k + 2 * RAW + 1)
        dve.wait_ge(mm_done, q0 + k + 1)
        nc.vector.tensor_tensor(lo[k % SPLIT][:], raw_quarter(k), hi[k % SPLIT][:].bitcast(F32),
                                ALU.subtract).then_inc(lo_done, 1)

    def tile_done(eng, i, b):
        eng.wait_ge(mm_done, 8 * i + 4 * b + 4 + SPLIT)

    def quarter_products(pe, q0, k, out, rhs, first, n, start, stop):
        pe.wait_ge(lo_done, q0 + k + 2 * RAW + 1)
        for j in range(QT):
            a, b = hi[k % SPLIT][:, j], lo[k % SPLIT][:, j]
            rh, rl = rhs[0][:, first + j, 0:n], rhs[1][:, first + j, 0:n]
            pe.matmul(out, a, rh, start=start and j == 0, stop=False)
            pe.matmul(out, a, rl, start=False, stop=False)
            m = pe.matmul(out, b, rh, start=False, stop=stop and j == QT - 1)
        m.then_inc(mm_done, 1)

    def pe_tile(pe, i, b, rhs, n):
        for r in range(4):
            quarter_products(pe, 8 * i, 4 * b + r, ps[:, b, 0:n], rhs, QT * r, n, r == 0, r == 3)

    def pe_pairs(pe, first, last, rhs, n):
        with pe.Fori(first, last) as i:
            for b in range(2):
                pe.wait_ge(tile_free[b], i + 1)
                pe_tile(pe, i, b, rhs, n)

    def four(split, eng, i, b):
        for k in range(4 * b + AHEAD, 4 * b + AHEAD + 4):
            split(eng, 8 * i, k)

    def act_pairs(act, first, last, even, odd):
        with act.Fori(first, last) as i:
            for b, read in ((0, even), (1, odd)):
                four(split_hi, act, i, b)
                if read:
                    tile_done(act, i, b)
                    read(i)

    sq_ready, sq_used, root_ready = sem("sq_ready"), sem("sq_used"), sem("root_ready")
    norm_ready, norm_hi = sem("norm_ready"), sem("norm_hi")

    def act_norm(act, src, tiles, n, slots, rt, call, dim, e):
        for j in range(tiles):
            if call + j >= 4:
                act.wait_ge(sq_used, call + j - 3)
            nc.scalar.square(slots[:, j % 4, 0:n], src[:, j, 0:n]).then_inc(sq_ready, 1)
        act.wait_ge(sq_used, call + tiles)
        nc.scalar.activation(rt[:, 0:n], ps[:, 7, 0:n], ACT.Sqrt, bias=eps[:, e:e + 1],
                             scale=1.0 / dim).then_inc(root_ready, 1)

    def pe_norm(pe, tiles, n, slots, call):
        for j in range(tiles):
            pe.wait_ge(sq_ready, call + j + 1)
            pe.matmul(ps[:, 7, 0:n], ones[:], slots[:, j % 4, 0:n], start=j == 0,
                      stop=j == tiles - 1).then_inc(sq_used, 1)

    def dve_rstd(dve, n, rt, rs, tp, nth, dim, e):
        dve.wait_ge(root_ready, nth)
        vchain(nc.vector.reciprocal(rs[:, 0:n], rt[:, 0:n]))
        vwait(dve)
        vchain(nc.vector.tensor_scalar(rt[:, 0:n], ps[:, 7, 0:n], 1.0 / dim, eps[:, e:e + 1], ALU.mult, ALU.add))
        vchain(nc.vector.tensor_tensor(tp[:, 0:n], rs[:, 0:n], rs[:, 0:n], ALU.mult))
        vwait(dve)
        vchain(nc.vector.tensor_tensor(tp[:, 0:n], tp[:, 0:n], rt[:, 0:n], ALU.mult))
        vwait(dve)
        vchain(nc.vector.tensor_scalar(tp[:, 0:n], tp[:, 0:n], -0.5, 1.5, ALU.mult, ALU.add))
        vwait(dve)
        vchain(nc.vector.tensor_tensor(rs[:, 0:n], rs[:, 0:n], tp[:, 0:n], ALU.mult))
        vwait(dve)

    def dve_norm_split(dve, src, parts, n, slots, rs, g, call):
        def scaled(j):
            nc.vector.scalar_tensor_tensor(out=slots[:, j % 4, 0:n], in0=src[:, j, 0:n],
                                           scalar=gain[:, g, j:j + 1], in1=rs[:, 0:n],
                                           op0=ALU.mult, op1=ALU.mult).then_inc(norm_ready, 1)
        scaled(0)
        scaled(1)
        for j in range(KD):
            dve.wait_ge(norm_hi, call + j + 1)
            vchain(nc.vector.tensor_tensor(parts[1][:, j, 0:n], slots[:, j % 4, 0:n],
                                           parts[0][:, j, 0:n].bitcast(F32), ALU.subtract))
            if j + 2 < KD:
                scaled(j + 2)

    def act_norm_split(act, parts, n, slots, call):
        for j in range(KD):
            act.wait_ge(norm_ready, call + j + 1)
            nc.scalar.copy(parts[0][:, j, 0:n], slots[:, j % 4, 0:n]).then_inc(norm_hi, 1)

    x_in, vec_in, const_ready = sem("x_in"), sem("vec_in"), sem("const_ready")
    fill0, glu_done = sem("fill0"), sem("glu_done")
    rows_ready, part_ready, out_done, kv_done = sem("rows_ready"), sem("part_ready"), sem("out_done"), sem("kv_done")
    conv_done, norm_split0, tap_done = sem("conv_done"), sem("norm_split0"), sem("tap_done")

    page_in = [sem(f"page_in{s}") for s in range(4)]
    page_used, dg_ready, qb_ready, zd_done = sem("page_used"), sem("dg_ready"), sem("qb_ready"), sem("zd_done")
    vt_ready, vn_ready, qg_ready = sem("vt_ready"), sem("vn_ready"), sem("qg_ready")
    d_act, d_vec, d_pe, d_vec2 = sem("d_act"), sem("d_vec"), sem("d_pe"), sem("d_vec2")
    z_ready, zm_ready, z_kept, relu_done = sem("z_ready"), sem("zm_ready"), sem("z_kept"), sem("relu_done")
    abs_done, e_done, ln_done, sp_step = sem("abs_done"), sem("e_done"), sem("ln_done"), sem("sp_step")
    sp_ready, t_ready, m_ready, aexp_done = sem("sp_ready"), sem("t_ready"), sem("m_ready"), sem("aexp_done")
    o_ready, o_done = sem("o_ready"), sem("o_done")
    act_go, pe_go = sem("act_go"), sem("pe_go")
    NG = HEADS // GH
    NP = DEC * PAGES

    def meta_bank(i):
        return ps[0:META, 6 + i % 2, 256 * (i // 2):256 * (i // 2) + 256]

    with nc.Block() as block:
        @block.sync
        def _(sp):
            sp.dma_start(x[:], xT).then_inc(x_in, 16)
            for t, src in ((gain, gains), (dw, w_dwT), (cvec, conv_vecs), (bias, sb_bias), (pages, page_table)):
                sp.dma_start(t[:], src).then_inc(vec_in, 16)
            for j in range(KC):
                sp.dma_start(st[:, j, :, 0:PADC], stateT[:, j]).then_inc(vec_in, 16)
            for s in range(RAW):
                sp.dma_start(raw[:, s].rearrange("p a b -> p (a b)"), a_halves[s]).then_inc(raw_in[s], 16)
            with sp.Fori(1, PAIR_IN + 1) as i:
                for s in range(RAW):
                    load_half(sp, 4 * i + s, s, a_halves[4 * i + s])

        @block.gpsimd
        def _(pool):
            pool.sem_inc(tile_free[0], 1)
            pool.sem_inc(tile_free[1], 1)
            nc.gpsimd.memset(ones[:], 1.0).then_inc(fill0, 1)
            nc.gpsimd.memset(eps[:, 0:1], RMS_EPS).then_inc(fill0, 1)
            nc.gpsimd.memset(eps[:, 1:2], LN_EPS).then_inc(fill0, 1)
            nc.gpsimd.memset(ident[:], 0.0).then_inc(const_ready, 1)
            nc.gpsimd.memset(neg_tri[:], -1.0).then_inc(const_ready, 1)
            nc.gpsimd.memset(mask[:], 1.0).then_inc(const_ready, 1)
            nc.gpsimd.memset(neg_ones[:], -1.0).then_inc(const_ready, 1)
            nc.gpsimd.memset(pen[:], 0.0).then_inc(const_ready, 1)
            for j in range(KC):
                nc.gpsimd.memset(cv[:, j, 0:PADC], 0.0).then_inc(const_ready, 1)
            pool.wait_ge(const_ready, 5 + KC)
            nc.gpsimd.affine_select(out=ident[:], in_=ident[:], compare_op=ALU.not_equal, fill=1.0, base=0,
                                    pattern=[[-1, P]], channel_multiplier=1).then_inc(const_ready, 1)
            nc.gpsimd.affine_select(out=neg_tri[:], in_=neg_tri[:], compare_op=ALU.is_ge, fill=0.0, base=0,
                                    pattern=[[-1, P]], channel_multiplier=1).then_inc(const_ready, 1)
            nc.gpsimd.affine_select(out=mask[:], in_=mask[:], compare_op=ALU.is_gt, fill=0.0, base=0,
                                    pattern=[[1, P]], channel_multiplier=-1).then_inc(const_ready, 1)
            nc.gpsimd.affine_select(out=pen[:], in_=pen[:], compare_op=ALU.is_gt, fill=MASKED, base=0,
                                    pattern=[[1, P]], channel_multiplier=-1).then_inc(const_ready, 1)
            nc.gpsimd.iota(iota[:], pattern=[[1, P]], base=0, channel_multiplier=0,
                           allow_small_or_imprecise_dtypes=True).then_inc(const_ready, 1)
            nc.gpsimd.iota(part[:], pattern=[[0, 2]], base=0, channel_multiplier=1,
                           allow_small_or_imprecise_dtypes=True).then_inc(part_ready, 1)

            pool.wait_ge(rows_ready, 1)
            for n in range(2 * NP):
                if n >= 4:
                    pool.wait_ge(page_used, n - 3)
                cache = cache_k if n < NP else cache_v
                nc.gpsimd.indirect_dma_start(
                    ring[:, n % 4, :], None, cache,
                    bass.IndirectOffsetOnAxis(ap=rows[:, n % NP:n % NP + 1], axis=0)).then_inc(page_in[n % 4], 16)
            pool.wait_ge(page_used, 2 * NP)
            with pool.Fori(0, NG) as g:
                pool.wait_ge(m_ready, g + 1)
                nc.gpsimd.tensor_copy(qg[:], qkv[:].rearrange("p (s j) t -> p s j t", s=3)[:, :, bass.ds(2 * g, 2), :])\
                    .then_inc(qg_ready, 1)

        @block.scalar
        def _(act):
            act.sem_inc(hi_done, 2 * RAW)
            act.wait_ge(x_in, 16)
            act.wait_ge(fill0, 3)
            act_norm(act, x, KD, NT, work, root, 0, D, 0)
            act_norm_split(act, h, NT, work, 0)
            for k in range(AHEAD):
                split_hi(act, 0, k)

            def copy_out(b):
                def f(i):
                    nc.scalar.copy(qkv[:, 2 * i + b, :], ps[:, b, 0:NT]).then_inc(tile_free[b], 1)
                return f

            def q_out(b):
                def f(i):
                    nc.scalar.mul(qkv[:, 2 * i + b, :], ps[:, b, 0:NT], HD ** -0.5).then_inc(tile_free[b], 1)
                return f

            def glu_gate(i):
                act.wait_ge(glu_done, i - PAIR_V + 1)
                nc.scalar.activation(sg[:], ps[:, 0, 0:NT], ACT.Sigmoid).then_inc(tile_free[0], 1)

            def gate_out(i, b):
                nc.scalar.copy(gates[:, 2 * (i - PAIR_GLU) + b, :], ps[:, b, 0:LIVE]).then_inc(tile_free[b], 1)

            def gate_tile(i, b):
                four(split_hi, act, i, b)
                tile_done(act, i, b)
                gate_out(i, b)

            act_pairs(act, 0, PAIR_Q, q_out(0), q_out(1))
            act_pairs(act, PAIR_Q, PAIR_V, copy_out(0), copy_out(1))
            act_pairs(act, PAIR_V, PAIR_GLU, glu_gate, None)
            act.wait_ge(d_vec, 1)
            nc.scalar.activation(ed[:], zd[:], ACT.Abs).then_inc(d_act, 1)
            act.wait_ge(d_act, 1)
            nc.scalar.activation(ed[:], ed[:], ACT.Exp, scale=-1.0).then_inc(d_act, 1)
            act.wait_ge(d_act, 2)
            nc.scalar.activation(ed[:], ed[:], ACT.Ln, bias=1.0).then_inc(d_act, 1)
            gate_tile(PAIR_GLU, 0)
            gate_tile(PAIR_GLU, 1)
            act.wait_ge(d_vec2, 1)
            nc.scalar.activation(ed[:], zd[:], ACT.Exp).then_inc(d_act, 1)
            for i in range(PAIR_GLU + 1, PAIR_ATT - 1):
                gate_tile(i, 0)
                gate_tile(i, 1)
            gate_tile(PAIR_GLU + 3, 0)
            act.wait_ge(d_vec, 3)
            gate_tile(PAIR_GLU + 3, 1)
            with act.Fori(0, NG) as g:
                def hi_one(tile, r):
                    split_hi(act, 8 * (PAIR_ATT + 3 * g + tile // 2), 4 * (tile % 2) + AHEAD + r)

                def out(tile):
                    tile_done(act, PAIR_ATT + 3 * g + tile // 2, tile % 2)
                    gate_out(PAIR_ATT + 3 * g + tile // 2, tile % 2)

                for i in range(GH):
                    act.wait_ge(z_ready, GH * g + i + 1)
                    act.sem_inc(act_go, 1)
                    nc.scalar.activation(eab[:, i, :], ps[:, 2 + i, 0:384], ACT.Identity,
                                         bias=bias[:, bass.ds(GH * g + i, 1)]).then_inc(z_kept, 1)
                act.wait_ge(zm_ready, g + 1)
                act.sem_inc(act_go, 1)
                for i in range(GH):
                    nc.scalar.activation(em[:, i, :], meta_bank(i), ACT.Identity,
                                         bias=bias[0:META, bass.ds(GH * g + i, 1)]).then_inc(z_kept, 1)
                hi_one(0, 0)
                act.wait_ge(relu_done, 2 * g + 1)
                nc.scalar.activation(eab[:], eab[:], ACT.Abs).then_inc(abs_done, 1)
                hi_one(0, 1)
                act.wait_ge(relu_done, 2 * g + 2)
                nc.scalar.activation(em[:], em[:], ACT.Abs).then_inc(abs_done, 1)
                hi_one(0, 2)
                act.wait_ge(abs_done, 2 * g + 1)
                nc.scalar.activation(eab[:], eab[:], ACT.Exp, scale=-1.0).then_inc(e_done, 1)
                act.wait_ge(abs_done, 2 * g + 2)
                nc.scalar.activation(em[:], em[:], ACT.Exp, scale=-1.0).then_inc(e_done, 1)
                hi_one(0, 3)
                out(0)
                act.wait_ge(e_done, 2 * g + 1)
                nc.scalar.activation(eab[:], eab[:], ACT.Ln, bias=1.0).then_inc(ln_done, 1)
                act.wait_ge(e_done, 2 * g + 2)
                nc.scalar.activation(em[:], em[:], ACT.Ln, bias=1.0).then_inc(ln_done, 1)
                for r in range(4):
                    hi_one(1, r)
                out(1)
                for r in range(4):
                    hi_one(2, r)
                out(2)
                for i in range(GH):
                    act.wait_ge(t_ready, GH * g + i + 1)
                    act.sem_inc(act_go, 1)
                    nc.scalar.activation(eab[:, i, :], ps[:, 2 + i, 0:384], ACT.Exp,
                                         bias=bias[:, bass.ds(GH * g + i, 1)]).then_inc(aexp_done, 1)
                act.wait_ge(m_ready, g + 2)
                act.sem_inc(act_go, 1)
                for i in range(GH):
                    nc.scalar.activation(em[:, i, :], meta_bank(i), ACT.Exp,
                                         bias=bias[0:META, bass.ds(GH * g + i, 1)]).then_inc(aexp_done, 1)
                for tile in range(3, 6):
                    for r in range(4):
                        hi_one(tile, r)
                    out(tile)

        @block.tensor
        def _(pe):
            pe.sem_inc(o_done, 1)
            pe.sem_inc(m_ready, 1)
            pe.sem_inc(mm_done, SPLIT)
            pe.wait_ge(fill0, 3)
            pe_norm(pe, KD, NT, work, 0)
            pe.wait_ge(norm_split0, 1)
            pe_pairs(pe, 0, PAIR_V, h, NT)
            with pe.Fori(PAIR_V, PAIR_GLU) as i:
                pe.wait_ge(tile_free[0], i + 1)
                pe_tile(pe, i, 0, h, NT)
                pe.wait_ge(dg_ready, i - PAIR_V + 1)
                for c in range(2):
                    m = pe.matmul(ps[:, 2 + c, :], ones[:], dg[:, 4 * c:4 * c + 4, :], start=True, stop=True)
                m.then_inc(qb_ready, 1)
                pe.wait_ge(tile_free[1], i + 1)
                pe_tile(pe, i, 1, h, NT)
            def gate_tile(t):
                pe.wait_ge(tile_free[t % 2], PAIR_GLU + t // 2 + 1)
                pe_tile(pe, PAIR_GLU + t // 2, t % 2, h, LIVE)

            gate_tile(0)
            pe.wait_ge(d_vec, 2)
            pe.matmul(ps[:, 4, 0:256], neg_tri[:], sd[:], start=True, stop=False)
            pe.matmul(ps[:, 4, 0:256].rearrange("p (b g h) -> p b g h", b=DEC, g=PAGES)[:, :, 0, :], neg_ones[:],
                      sd[:, :, 1, :], start=False, stop=True).then_inc(d_pe, 1)
            gate_tile(1)
            gate_tile(2)
            pe.wait_ge(d_act, 4)
            for b in range(DEC):
                for g in range(PAGES):
                    n = NP + 2 * b + g
                    pe.wait_ge(page_in[n % 4], 16 * (n // 4 + 1))
                for j in range(KA):
                    for g in range(PAGES):
                        n = NP + 2 * b + g
                        m = pe.matmul(ps[:, 5, 16 * j + 2 * b:16 * j + 2 * b + 2], ring[:, n % 4, P * j:P * j + P],
                                      ed[:, b, g, 2 * j:2 * j + 2], start=g == 0, stop=g == 1)
                m.then_inc(page_used, 2)
                if b % 2 == 1:
                    gate_tile(3 + b // 2)
            gate_tile(7)
            pe.wait_ge(d_vec, 3)
            with pe.Fori(0, NG) as g:
                def tile(t):
                    i = PAIR_ATT + 3 * g + t // 2
                    pe.wait_ge(tile_free[t % 2], i + 1)
                    pe_tile(pe, i, t % 2, h, LIVE)

                def q_of(i):
                    r = HD * (i % 2)
                    return qg[r:r + HD, 0, i // 2]

                def k_of(i):
                    r = HD * (i % 2)
                    return qg[r:r + HD, 1, i // 2]

                pe.wait_ge(qg_ready, g + 1)
                pe.wait_ge(o_done, g + 1)
                for blk in range(3):
                    at_col, n = ((0, P), (P, P), (LIVE, META))[blk]
                    for j in range(GH // 2):
                        o = ps[0:n, 6 + blk // 2, 256 * (blk % 2) + P * j:256 * (blk % 2) + P * j + P]
                        m = pe.transpose(o, qg[:, 2, j, at_col:at_col + n], ident[:])
                m.then_inc(vt_ready, 1)
                for i in range(GH):
                    q, k = q_of(i), k_of(i)
                    pe.matmul(ps[:, 2 + i, 0:256], k[:, 0:P], q[:, 0:SEQ], start=True, stop=True)
                    pe.matmul(ps[:, 2 + i, 256:384], k[:, P:SEQ], q[:, P:SEQ], start=True, stop=True)\
                        .then_inc(z_ready, 1)
                pe.wait_ge(vn_ready, g + 1)
                pe.sem_inc(pe_go, 1)
                for i in range(GH):
                    m = pe.matmul(meta_bank(i), k_of(i)[:, LIVE:NT], q_of(i)[:, 0:SEQ], start=True, stop=True)
                m.then_inc(zm_ready, 1)
                tile(0)
                tile(1)
                tile(2)
                pe.wait_ge(sp_ready, g + 1)
                for i in range(GH):
                    q, k = q_of(i), k_of(i)
                    pe.matmul(ps[:, 2 + i, 0:256], k[:, 0:P], q[:, 0:SEQ], start=True, stop=False)
                    pe.matmul(ps[:, 2 + i, 0:256], neg_tri[:], sab[:, i, 0:256], start=False, stop=False)
                    pe.matmul(ps[:, 2 + i, 0:P], ident[:], pen[:], start=False, stop=False)
                    pe.matmul(ps[:, 2 + i, P:256], neg_ones[:], sab[:, i, 256:384], start=False, stop=True)
                    pe.matmul(ps[:, 2 + i, 256:384], k[:, P:SEQ], q[:, P:SEQ], start=True, stop=False)
                    pe.matmul(ps[:, 2 + i, 256:384], ident[:], pen[:], start=False, stop=False)
                    pe.matmul(ps[:, 2 + i, 256:384], neg_tri[:], sab[:, i, 256:384], start=False, stop=True)\
                        .then_inc(t_ready, 1)
                for i in range(GH):
                    o = meta_bank(i)
                    pe.matmul(o, k_of(i)[:, LIVE:NT], q_of(i)[:, 0:SEQ], start=True, stop=False)
                    pe.matmul(o, neg_tri[0:META, 0:META], sm[:, i, :], start=False, stop=False)
                    pe.matmul(o, neg_ones[:, 0:META], sab[:, i, 0:256], start=False, stop=False)
                    m = pe.matmul(o[:, P:256], neg_ones[:, 0:META], sab[:, i, 256:384], start=False, stop=True)
                m.then_inc(m_ready, 1)
                tile(3)
                tile(4)
                pe.wait_ge(aexp_done, 2 * GH * (g + 1))
                for i in range(GH):
                    r = HD * (i % 2)
                    o = ps[r:r + HD, 2 + i // 2, 0:256]
                    pe.matmul(o, vn[:, 0, HD * i:HD * i + HD], eab[:, i, 0:256], start=True, stop=False)
                    pe.matmul(o[:, P:256], vn[:, 1, HD * i:HD * i + HD], eab[:, i, 256:384],
                              start=False, stop=False)
                    m = pe.matmul(o, vn[0:META, 2, HD * i:HD * i + HD], em[:, i, :], start=False, stop=True)
                m.then_inc(o_ready, 1)
                tile(5)

        @block.vector
        def _(dve):
            dve.sem_inc(lo_done, 2 * RAW)
            dve.sem_inc(glu_done, 1)
            dve.wait_ge(vec_in, 16 * (5 + KC))
            dve_rstd(dve, NT, root, rstd, tmp, 1, D, 0)
            dve_norm_split(dve, x, h, NT, work, rstd, 0, 0)
            vwait(dve)
            dve.sem_inc(norm_split0, 1)
            dve.wait_ge(part_ready, 1)
            vchain(nc.vector.tensor_copy(page_f[:], pages[:]))
            vwait(dve)
            nc.vector.tensor_scalar(rows[:], page_f[:], float(P), part[:, 0:1], ALU.mult,
                                    ALU.add).then_inc(rows_ready, 1)
            for k in range(AHEAD):
                split_lo(dve, 0, k)
            with dve.Fori(0, PAIR_V) as i:
                four(split_lo, dve, i, 0)
                four(split_lo, dve, i, 1)
            def diag(b):
                nc.vector.tensor_tensor(dg[:], spread(ident[:], 1, KA),
                                        spread(qkv[:, 0:KA, bass.ds(b + SEQ, 1)].rearrange("p j o -> p (j o)"), 2, P),
                                        ALU.mult).then_inc(dg_ready, 1)

            def page_products(b, u, g):
                dve.wait_ge(page_in[2 * u + g], 8 * (b - u) + 16)
                nc.vector.tensor_tensor(prod[:], ring[:, 2 * u + g, :],
                                        ps[:, 2:4, :].rearrange("p a b -> p (a b)"), ALU.mult).then_inc(page_used, 1)

            def page_sums(b, g):
                dve.wait_ge(page_used, 2 * b + g + 1)
                nc.vector.tensor_reduce(zd[:, bass.ds(b, 1), g, :].rearrange("p o h -> p (o h)"),
                                        prod[:].rearrange("p (h d) -> p h d", h=HEADS), AX_X,
                                        ALU.add).then_inc(zd_done, 1)

            dve.sem_inc(zd_done, 1)
            dve.wait_ge(const_ready, 10 + KC)
            dve.wait_ge(tile_free[0], PAIR_Q + 1)
            dve.wait_ge(tile_free[1], PAIR_Q + 1)
            with dve.Fori(0, DEC // 2) as m:
                for u in range(2):
                    b = 2 * m + u
                    i = b + PAIR_V
                    diag(b)
                    four(split_lo, dve, i, 0)
                    split_lo(dve, 8 * i, 4 + AHEAD)
                    dve.wait_ge(qb_ready, b + 1)
                    dve.wait_ge(zd_done, 2 * b + 1)
                    page_products(b, u, 0)
                    split_lo(dve, 8 * i, 5 + AHEAD)
                    page_sums(b, 0)
                    split_lo(dve, 8 * i, 6 + AHEAD)
                    dve.wait_ge(zd_done, 2 * b + 2)
                    page_products(b, u, 1)
                    split_lo(dve, 8 * i, 7 + AHEAD)
                    page_sums(b, 1)
                    tile_done(dve, i, 1)
                    dve.wait_ge(tile_free[0], i + 2)
                    nc.vector.tensor_tensor(cv[:, b, PADC + META:], ps[:, 1, 0:SEQ], sg[:, 0:SEQ], ALU.mult)\
                        .then_inc(conv_done, 1)
                    nc.vector.tensor_tensor(cv[:, b, PADC:PADC + META], ps[:, 1, LIVE:NT], sg[:, LIVE:NT], ALU.mult)\
                        .then_inc(conv_done, 1)
                    nc.vector.tensor_tensor(st[:, b, :, PADC], ps[:, 1, SEQ:LIVE], sg[:, SEQ:LIVE], ALU.mult)\
                        .then_inc(conv_done, 1)
                    dve.wait_ge(conv_done, 3 * b + 3)
                    dve.sem_inc(glu_done, 1)
                    dve.sem_inc(tile_free[1], 1)
            dve.wait_ge(const_ready, 5 + KC)

            def tap(j, k):
                return nc.vector.scalar_tensor_tensor(out=yc[:, j, 0:SEQ], in0=cv[:, j, bass.ds(k + META, SEQ)],
                                                      scalar=dw[:, j, bass.ds(k, 1)], in1=yc[:, j, 0:SEQ],
                                                      op0=ALU.mult, op1=ALU.add)
            for j in range(KC):
                nc.vector.tensor_scalar(yc[:, j, 0:SEQ], cv[:, j, META:META + SEQ], dw[:, j, 0:1], cvec[:, 0, j:j + 1],
                                        ALU.mult, ALU.add).then_inc(tap_done, 1)
            def tap_tile(i, b, number):
                for k in range(4):
                    split_lo(dve, 8 * i, 4 * b + AHEAD + k)
                    for o in range(6 * number + (0, 2, 3, 5)[k], 6 * number + (2, 3, 5, 6)[k]):
                        dve.wait_ge(tap_done, o + 1)
                        tap(o % KC, 1 + o // KC).then_inc(tap_done, 1)

            dve.wait_ge(zd_done, NP + 1)
            vchain(nc.vector.tensor_tensor(zd[:], zd[:], spread(spread(bias[:], 1, PAGES), 1, DEC), ALU.add))
            vwait(dve)
            nc.vector.tensor_scalar(sd[:], zd[:], 0.0, None, ALU.max).then_inc(d_vec, 1)
            dve.wait_ge(d_act, 3)
            dve.wait_ge(d_vec, 1)
            nc.vector.tensor_tensor(sd[:], sd[:], ed[:], ALU.add).then_inc(d_vec, 1)
            tap_tile(PAIR_GLU, 0, 0)
            tap_tile(PAIR_GLU, 1, 1)
            dve.wait_ge(d_pe, 1)
            nc.vector.tensor_tensor(zd[:].rearrange("p b g h -> p (b g h)"), ps[:, 4, 0:256],
                                    zd[:].rearrange("p b g h -> p (b g h)"), ALU.add).then_inc(d_vec2, 1)
            for t in range(2, 6):
                tap_tile(PAIR_GLU + t // 2, t % 2, t)
            for j in range(KC):
                vchain(nc.vector.tensor_tensor(stp[:], st[:, j], spread(dw[:, j], 1, DEC), ALU.mult))
                vwait(dve)
                vchain(nc.vector.tensor_reduce(yc[:, j, SEQ:LIVE], stp[:], AX_X, ALU.add))
                vwait(dve)
                vchain(nc.vector.tensor_scalar(yc[:, j, SEQ:LIVE], yc[:, j, SEQ:LIVE], cvec[:, 0, j:j + 1],
                                               None, ALU.add))
                if j == 3:
                    tap_tile(PAIR_GLU + 3, 0, 6)
            dve.wait_ge(page_used, 2 * NP)
            for r in range(2):
                ins = nc.vector.tensor_copy(
                    attn[HD * r:HD * r + HD, :, SEQ:LIVE],
                    ps[HD * r:HD * r + HD, 5, 0:P].rearrange("p (j b r) -> p j b r", j=KA, b=DEC)[:, :, :, r])
            ins.then_inc(d_vec, 1)
            tap_tile(PAIR_GLU + 3, 1, 7)
            with dve.Fori(0, NG) as g:
                def tile(t, between=(None,) * 4):
                    for k in range(4):
                        split_lo(dve, 8 * (PAIR_ATT + 3 * g + t // 2), 4 * (t % 2) + AHEAD + k)
                        for o in (8 * t + 2 * k, 8 * t + 2 * k + 1):
                            dve.wait_ge(tap_done, 6 * KC * (g + 1) + o + 1)
                            tap(o % KC, 6 * g + 7 + o // KC).then_inc(tap_done, 1)
                        if between[k]:
                            between[k]()

                dve.wait_ge(vt_ready, g + 1)
                nc.vector.tensor_copy(vn[:, 0:2, :].rearrange("p a b -> p (a b)"), ps[:, 6, :])
                nc.vector.tensor_copy(vn[0:META, 2, :], ps[0:META, 7, 0:GH * HD]).then_inc(vn_ready, 1)
                dve.wait_ge(z_kept, 2 * GH * g + GH)
                nc.vector.tensor_scalar(sab[:], eab[:], 0.0, None, ALU.max).then_inc(relu_done, 1)
                dve.wait_ge(z_kept, 2 * GH * g + 2 * GH)
                nc.vector.tensor_scalar(sm[:], em[:], 0.0, None, ALU.max).then_inc(relu_done, 1)
                tile(0)

                def add_ab():
                    dve.wait_ge(relu_done, 2 * g + 2)
                    dve.wait_ge(ln_done, 2 * g + 1)
                    nc.vector.tensor_tensor(sab[:], sab[:], eab[:], ALU.add).then_inc(sp_step, 1)

                def masked(c, n):
                    def f():
                        dve.wait_ge(sp_step, 3 * g + n)
                        nc.vector.tensor_tensor(sab[:, :, c:c + P], sab[:, :, c:c + P], spread(mask[:], 1, GH),
                                                ALU.mult).then_inc(sp_step, 1)
                    return f

                def add_m():
                    dve.wait_ge(ln_done, 2 * g + 2)
                    nc.vector.tensor_tensor(sm[:], sm[:], em[:], ALU.add).then_inc(sp_ready, 1)
                tile(1, (None, None, add_ab, masked(0, 1)))
                tile(2, (masked(256, 1), add_m, None, None))
                tile(3)
                tile(4)
                tile(5)
                dve.wait_ge(o_ready, g + 1)
                nc.vector.tensor_copy(attn[:, bass.ds(GH // 2 * g, GH // 2), 0:SEQ], ps[:, 2:4, 0:256])\
                    .then_inc(o_done, 1)

    mu_ready, cen_done, silu_done, nrm_done = sem("mu_ready"), sem("cen_done"), sem("silu_done"), sem("nrm_done")
    sig_done, x_back = sem("sig_done"), sem("x_back")
    with nc.Block() as block:
        @block.sync
        def _(sp):
            sp.dma_start(x[:], xT).then_inc(x_back, 16)
            sp.dma_start(kvT.rearrange("(j p) t -> p j t", p=P), qkv[:, KA:3 * KA, :]).then_inc(kv_done, 16)
            sp.dma_start(conv_p.rearrange("(j p) t -> p j t", p=P), cv[:, :, META + SEQ:]).then_inc(kv_done, 16)
            for j in range(KC):
                sp.dma_start(conv_s[:, j], st[:, j, :, 1:TAPS]).then_inc(kv_done, 16)
            sp.wait_ge(kv_done, 16 * (2 + KC))
            sp.wait_ge(x_back, 16)

        @block.tensor
        def _(pe):
            for j in range(KC):
                m = pe.matmul(ps[:, 6, 0:LIVE], ones[:], yc[:, j, :], start=j == 0, stop=j == KC - 1)
            m.then_inc(mu_ready, 1)
            pe_norm(pe, KC, LIVE, work, KD)

        @block.scalar
        def _(act):
            for q in range(4):
                nc.scalar.activation(gates[:, 8 * q:8 * q + 8, :], gates[:, 8 * q:8 * q + 8, :], ACT.Sigmoid)\
                    .then_inc(sig_done, 1)
            act.wait_ge(cen_done, KC)
            act_norm(act, yc, KC, LIVE, work, root, KD, DC, 1)
            for j in range(KC):
                act.wait_ge(nrm_done, j + 1)
                nc.scalar.activation(yc[:, j, :], yc[:, j, :], ACT.Silu, bias=cvec[:, 2, j:j + 1],
                                     scale=cvec[:, 1, j:j + 1]).then_inc(silu_done, 1)

        @block.vector
        def _(dve):
            dve.wait_ge(mu_ready, 1)
            for j in range(KC):
                nc.vector.scalar_tensor_tensor(out=yc[:, j, :], in0=ps[:, 6, 0:LIVE], scalar=-1.0 / DC,
                                               in1=yc[:, j, :], op0=ALU.mult, op1=ALU.add).then_inc(cen_done, 1)
            dve.wait_ge(cen_done, KC)
            dve_rstd(dve, LIVE, root, rstd, tmp, 2, DC, 1)
            for j in range(KC):
                nc.vector.tensor_tensor(yc[:, j, :], yc[:, j, :], rstd[:, 0:LIVE], ALU.mult).then_inc(nrm_done, 1)

    br_hi, br_lo, t1_done, mixed_done, mx_hi = (sem("br_hi"), sem("br_lo"), sem("t1_done"), sem("mixed_done"),
                                                sem("mx_hi"))
    mx_lo, x2_done, h2_ready, spill_done = sem("mx_lo"), sem("x2_done"), sem("h2_ready"), sem("spill_done")
    with nc.Block() as block:
        @block.sync
        def _(sp):
            with sp.Fori(PAIR_IN + 1, PAIR_OUT + 1) as i:
                for s in range(RAW):
                    load_half(sp, 4 * i + s, s, a_halves[4 * i + s])
            sp.wait_ge(x2_done, KD)
            sp.dma_start(x2_dram, x[:, :, 0:LIVE]).then_inc(spill_done, 16)
            sp.wait_ge(spill_done, 16)

        @block.scalar
        def _(act):
            nc.scalar.copy(at_p[0][:], attn[:]).then_inc(br_hi, 1)
            nc.scalar.copy(cv_p[0][:], yc[:]).then_inc(br_hi, 1)

            def mixed_hi(b):
                def f(i):
                    t = 2 * (i - PAIR_IN) + b
                    act.wait_ge(mixed_done, t + 1)
                    nc.scalar.copy(mx[0][:, t, :], gates[:, t, :]).then_inc(mx_hi, 1)
                return f
            act_pairs(act, PAIR_IN, PAIR_BR, mixed_hi(0), mixed_hi(1))
            act_pairs(act, PAIR_BR, PAIR_OUT, None, None)
            act.wait_ge(x2_done, KD)
            act_norm(act, x, KD, LIVE, work2, root, KD + KC, D, 0)
            act_norm_split(act, h2, LIVE, work2, KD)

        @block.tensor
        def _(pe):
            pe.wait_ge(br_lo, 2)
            with pe.Fori(PAIR_IN, PAIR_BR) as i:
                for b in range(2):
                    pe.wait_ge(tile_free[b], i + 1)
                    for r in range(4):
                        quarter_products(pe, 8 * i, 4 * b + r, ps[:, 2 * b + r // 2, 0:LIVE], (at_p, cv_p)[r // 2],
                                         QT * (r % 2), LIVE, r % 2 == 0, r % 2 == 1)
            pe.wait_ge(mx_lo, KD)
            pe_pairs(pe, PAIR_BR, PAIR_OUT, mx, LIVE)
            pe_norm(pe, KD, LIVE, work2, KD + KC)

        @block.vector
        def _(dve):
            dve.wait_ge(br_hi, 1)
            nc.vector.tensor_tensor(at_p[1][:], attn[:], at_p[0][:].bitcast(F32), ALU.subtract).then_inc(br_lo, 1)
            dve.wait_ge(br_hi, 2)
            nc.vector.tensor_tensor(cv_p[1][:], yc[:], cv_p[0][:].bitcast(F32), ALU.subtract).then_inc(br_lo, 1)
            with dve.Fori(PAIR_IN, PAIR_BR) as i:
                for b in range(2):
                    four(split_lo, dve, i, b)
                    t = 2 * (i - PAIR_IN) + b
                    tile_done(dve, i, b)
                    nc.vector.tensor_tensor(t2[:, 0], gates[:, t, :], ps[:, 2 * b, 0:LIVE], ALU.mult)\
                        .then_inc(t1_done, 1)
                    nc.vector.tensor_tensor(t2[:, 1], gates[:, KD + t, :], ps[:, 2 * b + 1, 0:LIVE], ALU.mult)\
                        .then_inc(t1_done, 1)
                    dve.wait_ge(t1_done, 4 * (i - PAIR_IN) + 2 * b + 2)
                    nc.vector.tensor_tensor(gates[:, t, :], t2[:, 0], t2[:, 1], ALU.add).then_inc(mixed_done, 1)
                    dve.sem_inc(tile_free[b], 1)
                    dve.wait_ge(mx_hi, 2 * (i - PAIR_IN) + b + 1)
                    nc.vector.tensor_tensor(mx[1][:, t, :], gates[:, t, :], mx[0][:, t, :].bitcast(F32),
                                            ALU.subtract).then_inc(mx_lo, 1)
            with dve.Fori(PAIR_BR, PAIR_OUT) as i:
                for b in range(2):
                    four(split_lo, dve, i, b)
                    t = 2 * (i - PAIR_BR) + b
                    tile_done(dve, i, b)
                    nc.vector.tensor_tensor(x[:, t, 0:LIVE], x[:, t, 0:LIVE], ps[:, b, 0:LIVE], ALU.add)\
                        .then_inc(x2_done, 1)
                    dve.wait_ge(x2_done, 2 * (i - PAIR_BR) + b + 1)
                    dve.sem_inc(tile_free[b], 1)
            dve.wait_ge(x2_done, KD)
            dve_rstd(dve, LIVE, root, rstd, tmp, 3, D, 0)
            dve_norm_split(dve, x, h2, LIVE, work2, rstd, 1, KD)
            vwait(dve)

    sk_in, qry_done, sc_ready, sc_done, zero_done = (sem("sk_in"), sem("qry_done"), sem("sc_ready"),
                                                     sem("sc_done"), sem("zero_done"))
    half_scores = sem("half_scores")
    with nc.Block() as block:
        @block.sync
        def _(sp):
            sp.dma_start(skT, sub_keysT).then_inc(sk_in, 16)
            with sp.Fori(PAIR_OUT + 1, PAIR_QRY) as i:
                for s in range(RAW):
                    load_half(sp, 4 * i + s, s, a_halves[4 * i + s])
            for s in range(RAW):
                load_half(sp, 4 * PAIR_QRY + s, s, u_tiles[s])

        @block.gpsimd
        def _(pool):
            nc.gpsimd.memset(sc_all[:, 2], 0.0).then_inc(zero_done, 1)

        @block.scalar
        def _(act):
            def keep(b):
                def f(i):
                    nc.scalar.copy(qry[:, b, :], ps[:, b, 0:LIVE]).then_inc(tile_free[b], 1)
                return f
            act_pairs(act, PAIR_OUT, PAIR_QRY, keep(0), keep(1))

        @block.tensor
        def _(pe):
            pe.wait_ge(sk_in, 16)
            with pe.Fori(PAIR_OUT, PAIR_QRY) as i:
                for b in range(2):
                    pe_tile(pe, i, b, h2, LIVE)
                    pe.wait_ge(tile_free[b], i + 2)
                    pe.wait_ge(sc_done, 2 * (i - PAIR_OUT) + b + 1)
                    for t in range(TT):
                        n = (P, P, DEC)[t]
                        m = pe.matmul(ps[0:n, 2 + b, P * t:P * t + P], qry[:, b, P * t:P * t + n], skT[:, b, :],
                                      start=True, stop=True)
                    m.then_inc(sc_ready, 1)

        @block.vector
        def _(dve):
            dve.sem_inc(sc_done, 2)
            dve.wait_ge(zero_done, 1)

            def keep_scores(i, b):
                q = 2 * (i - PAIR_OUT) + b
                dve.wait_ge(sc_ready, q + 1)
                vq = nc.vector.tensor_copy(sc_all[:, 0:2, q, :], ps[:, 2 + b, 0:256])
                vq.then_inc(half_scores, 1)
                nc.vector.tensor_copy(sc_all[0:DEC, 2, q, :], ps[0:DEC, 2 + b, 256:384]).then_inc(half_scores, 1)
                dve.wait_ge(half_scores, 2 * q + 2)
                dve.sem_inc(sc_done, 1)
            with dve.Fori(PAIR_OUT, PAIR_QRY) as i:
                for b in range(2):
                    four(split_lo, dve, i, b)
                    keep_scores(i, b)

    route, route_seen = sem("route"), sem("route_seen")
    with nc.Block() as block:
        @block.sync
        def _(sp):
            with sp.Fori(PAIR_QRY + 1, PAIR_U) as i:
                for s in range(RAW):
                    load_half(sp, 4 * i + s, s, u_tiles[4 * (i - PAIR_QRY) + s])
            for s in range(RAW):
                load_half(sp, 4 * PAIR_U + s, s, expert_v[0, s])

        @block.scalar
        def _(act):
            def gelu(b):
                def f(i):
                    nc.scalar.activation(W[:, 2 * (i - PAIR_QRY) + b, :], ps[:, b, 0:LIVE],
                                         ACT.Gelu_apprx_tanh).then_inc(tile_free[b], 1)
                return f
            act_pairs(act, PAIR_QRY, PAIR_U, gelu(0), gelu(1))

        @block.tensor
        def _(pe):
            pe_pairs(pe, PAIR_QRY, PAIR_U, h2, LIVE)

        @block.vector
        def _(dve):
            STEPS = 1 + TT * 2 * 5 + 2 + TT * 5 + 4 + 2 * 3
            with dve.Fori(0, PH) as hd:
                count = [0]

                def step(ins):
                    count[0] += 1
                    ins.then_inc(route, 1)

                def after():
                    dve.wait_ge(route, STEPS * hd + count[0])
                    dve.sem_inc(route_seen, 1)

                split = [0]

                def lo_next(n=1):
                    for _ in range(n):
                        split_lo(dve, 8 * PAIR_QRY + 8 * HEAD_PAIRS * hd, AHEAD + split[0])
                        split[0] += 1

                def best8(dst, idx, src):
                    lo_next()
                    step(nc.vector.max(dst, src))
                    lo_next()
                    after()
                    step(nc.vector.max_index(idx.bitcast(U32), dst, src))

                def drop8(dst, src):
                    step(nc.vector.match_replace(src, dst, src, NEG_BIG))
                    after()

                lo_next()
                step(nc.vector.tensor_copy(sh, sc_all[:, :, bass.ds(2 * hd, 2), :]))
                after()
                for t in range(TT):
                    for q in range(2):
                        s, v, ix = sh[:, t, q, :], top1[:, t, q, :], idx1[:, t, q, :]
                        best8(v[:, 0:8], ix[:, 0:8], s)
                        drop8(v[:, 0:8], s)
                        best8(v[:, 8:16], ix[:, 8:16], s)
                lo_next()
                after()
                step(nc.vector.tensor_tensor(cand, spread(top1[:, :, 0, :], 3, PK), spread(top1[:, :, 1, :], 2, PK),
                                             ALU.add))
                step(nc.vector.tensor_copy(idx1f, idx1.bitcast(U32)))
                for t in range(TT):
                    s = cand[:, t].rearrange("p a b -> p (a b)")
                    lo_next()
                    after()
                    step(nc.vector.max(top2[:, t, 0:8], s))
                    after()
                    step(nc.vector.max_index(pos2[:, t, 0:8].bitcast(U32), top2[:, t, 0:8], s))
                    drop8(top2[:, t, 0:8], s)
                    lo_next()
                    step(nc.vector.max(top2[:, t, 8:16], s))
                    after()
                    step(nc.vector.max_index(pos2[:, t, 8:16].bitcast(U32), top2[:, t, 8:16], s))
                lo_next()
                after()
                step(nc.vector.tensor_scalar(pab[:, 0].bitcast(U32), pos2.bitcast(U32), 4, None,
                                             ALU.logical_shift_right))
                step(nc.vector.tensor_scalar(pab[:, 1].bitcast(U32), pos2.bitcast(U32), 15, None,
                                             ALU.bitwise_and))
                after()
                step(nc.vector.tensor_copy(pabf, pab.bitcast(U32)))
                step(nc.vector.tensor_copy(chosen[:, 2, :, bass.ds(hd, 1), :],
                                           top2.rearrange("p t (o k) -> p t o k", o=1)))
                for q in range(2):
                    lo_next()
                    after()
                    ranks = spread(spread(iota[:, 0:PK], 1, PK), 1, TT)
                    step(nc.vector.tensor_tensor(eq, spread(pabf[:, q], 3, PK), ranks, ALU.is_equal))
                    lo_next()
                    after()
                    step(nc.vector.tensor_tensor(eq, eq, spread(idx1f[:, :, q, :], 2, PK), ALU.mult))
                    lo_next()
                    after()
                    step(nc.vector.tensor_reduce(chosen[:, q, :, bass.ds(hd, 1), :].rearrange("p t o k -> p t (o k)"),
                                                 eq, AX_X, ALU.add))
                lo_next(8 * HEAD_PAIRS - split[0])
                after()
                assert split[0] == 8 * HEAD_PAIRS and count[0] == STEPS, (split[0], count[0], STEPS)
            with dve.Fori(PAIR_QRY + PH * HEAD_PAIRS, PAIR_U) as i:
                four(split_lo, dve, i, 0)
                four(split_lo, dve, i, 1)

    soft = sem("soft")
    soft_act, tr_ready, ch_done = sem("soft_act"), sem("tr_ready"), sem("ch_done")
    l_ready, r_ready, g_ready, g_used = sem("l_ready"), sem("r_ready"), sem("g_ready"), sem("g_used")
    l_act, sq_done, diff_done, diff_seen = sem("l_act"), sem("sq_done"), sem("diff_done"), sem("diff_seen")
    GROUPS = LIVE // 4

    def by_vector(b):
        return 3 if b % 3 == 2 else 2
    SQ = sum(4 - by_vector(b) for b in range(GS))
    with nc.Block() as block:
        @block.scalar
        def _(act):
            act.wait_ge(soft, 2)
            nc.scalar.activation(chosen[:, 2], chosen[:, 2], ACT.Exp).then_inc(soft_act, 1)
            act.wait_ge(ch_done, 4)
            with act.Fori(0, GROUPS // GS) as i:
                for b in range(GS):
                    act.wait_ge(g_ready, GS * i + b + 1)
                    toks = range(by_vector(b), 4)
                    for t in toks:
                        nc.scalar.activation(ldiff[:, b % 2, t - 2], iota[:], ACT.Square,
                                             bias=chT[:, 3, bass.ds(4 * GS * i + 4 * b + t, 1)]).then_inc(sq_done, 1)
                    for t in toks:
                        act.wait_ge(sq_done, SQ * i + sum(4 - by_vector(k) for k in range(b)) + t - toks[0] + 1)
                        m = nc.scalar.activation(lhot[:, b, t], ldiff[:, b % 2, t - 2], ACT.Relu, scale=-2.0,
                                                 bias=chT[:, 2, bass.ds(4 * GS * i + 4 * b + t, 1)])
                    m.then_inc(l_act, 1)

        @block.gpsimd
        def _(pool):
            pool.sem_inc(g_used, GS)
            pool.wait_ge(ch_done, 3)
            with pool.Fori(0, GROUPS // GS) as i:
                for b in range(0, GS, 2):
                    n = (GS // 2) * i + b // 2
                    pool.wait_ge(g_ready, GS * i + b + 1)
                    pool.wait_ge(r_ready, n + 1)
                    pool.sem_inc(diff_seen, 1)
                    nc.gpsimd.tensor_tensor(rdiff[:], spread(iota[:], 1, 4),
                                            spread(chT[:, 1, bass.ds(4 * GS * i + 4 * b, 4)], 2, NK),
                                            ALU.subtract).then_inc(diff_done, 1)
                    pool.wait_ge(diff_done, n + 1)
                    pool.sem_inc(diff_seen, 1)
                    nc.gpsimd.tensor_scalar(rhot[:, b], rdiff[:], 0.0, None, ALU.is_equal).then_inc(r_ready, 1)

        @block.tensor
        def _(pe):
            pe.sem_inc(g_ready, GS)
            pe.sem_inc(r_ready, 1)
            pe.wait_ge(soft, 5)
            for t in range(TT):
                n = (P, P, DEC)[t]
                for q in range(3):
                    m = pe.transpose(ps[:, q, P * t:P * t + n],
                                     chosen[0:n, q, t].rearrange("p h k -> p (h k)"), ident[0:n, 0:n])
            m.then_inc(tr_ready, 1)
            with pe.Fori(0, GROUPS // GS) as i:
                for b in range(GS):
                    pe.wait_ge(l_ready, GS * i + b + 1)
                    pe.wait_ge(l_act, GS * i + b + 1)
                    if b % 2 == 0:
                        pe.wait_ge(r_ready, (GS // 2) * i + b // 2 + 2)
                    pe.wait_ge(g_used, GS * i + b + 1)
                    for t in range(4):
                        m = pe.matmul(ps[:, 2 + b, NK * t:NK * t + NK], lhot[:, b, t], rhot[:, b, t],
                                      start=True, stop=True)
                    m.then_inc(g_ready, 1)

        @block.vector
        def _(dve):
            sc = chosen[:, 2]
            nc.vector.tensor_copy(sums[:, 0], sc[:, :, :, 0]).then_inc(soft, 1)
            dve.wait_ge(soft, 1)
            nc.vector.tensor_tensor(sc, sc, spread(sums[:, 0], 3, PK), ALU.subtract).then_inc(soft, 1)
            dve.wait_ge(soft_act, 1)
            nc.vector.tensor_reduce(sums[:, 0], sc, AX_X, ALU.add).then_inc(soft, 1)
            dve.wait_ge(soft, 3)
            nc.vector.reciprocal(sums[:, 1], sums[:, 0]).then_inc(soft, 1)
            dve.wait_ge(soft, 4)
            nc.vector.tensor_tensor(sc, sc, spread(sums[:, 1], 3, PK), ALU.mult).then_inc(soft, 1)
            dve.wait_ge(tr_ready, 1)
            for q in range(3):
                nc.vector.tensor_copy(chT[:, q, :], ps[:, q, 0:LIVE]).then_inc(ch_done, 1)
            dve.wait_ge(ch_done, 3)
            nc.vector.tensor_scalar(chT[:, 3, :], chT[:, 0, :], -1.0, None, ALU.mult).then_inc(ch_done, 1)

            def left(tok, b, t):
                return nc.vector.tensor_scalar(lhot[:, b, t], iota[:], chT[:, 0, bass.ds(tok, 1)],
                                               chT[:, 2, bass.ds(tok, 1)], ALU.is_equal, ALU.mult)
            def hots(i, b):
                tok = 4 * GS * i + 4 * b
                if b % 2:
                    nc.vector.tensor_tensor(rhot[:, b], spread(iota[:], 1, 4),
                                            spread(chT[:, 1, bass.ds(tok, 4)], 2, NK), ALU.is_equal)
                for t in range(by_vector(b)):
                    m = left(tok + t, b, t)
                m.then_inc(l_ready, 1)

            def weigh(i, b):
                dve.wait_ge(g_ready, GS + GS * i + b + 1)
                wv = W[:, :, bass.ds(4 * GS * i + 4 * b, 4)]
                nc.vector.tensor_tensor(wv, wv, ps[:, 2 + b, :].rearrange("p (t n) -> p n t", t=4),
                                        ALU.mult).then_inc(g_used, 1)

            for b in range(GS):
                hots(0, b)
            with dve.Fori(0, GROUPS // GS - 1) as i:
                for b in range(GS):
                    weigh(i, b)
                    hots(i + 1, b)
            for b in range(GS):
                weigh(GROUPS // GS - 1, b)

    x2_in, whi_done, wlo_done, acc_done = sem("x2_in"), sem("whi_done"), sem("wlo_done"), sem("acc_done")
    C0 = 4 * PAIR_U
    with nc.Block() as block:
        @block.sync
        def _(sp):
            sp.dma_start(x2[:], x2_dram).then_inc(x2_in, 16)
            with sp.Fori(1, NK // 4) as i:
                for s in range(RAW):
                    load_half(sp, C0 + 4 * i + s, s, expert_v[0, 4 * i + s])
            with sp.Fori(0, NK // 4) as i:
                for s in range(RAW):
                    load_half(sp, C0 + NK + 4 * i + s, s, expert_v[1, 4 * i + s])

        def halves(eng, w_part, split, after_pass):
            def half(c, n, k, last=2):
                w_part(c + 1, n, k + 1)
                for r in range(last):
                    split(eng, C0 * 2 + 2 * (c - k), 2 * k + AHEAD + r)
            w_part(0, 0, 0)
            for p in range(2):
                with eng.Fori(0, NK // 4 - 1) as i:
                    for k in range(4):
                        half(NK * p + 4 * i + k, 4 * i + k + 1, k)
                for k in range(4):
                    if p == 0 or k < 2:
                        half(NK * p + NK - 4 + k, (NK - 3 + k) % NK, k)
                    elif k == 2:
                        half(NK * p + NK - 4 + k, NK - 3 + k, k, 1)
                after_pass(p)

        @block.scalar
        def _(act):
            def w_part(c, n, k):
                act.wait_ge(mm_done, 2 * C0 + 2 * c + 2)
                nc.scalar.copy(w_hi[k % 2][:], W[:, n, :]).then_inc(whi_done, 1)
            halves(act, w_part, split_hi, lambda p: None)

        @block.vector
        def _(dve):
            def w_part(c, n, k):
                dve.wait_ge(whi_done, c + 1)
                dve.wait_ge(mm_done, 2 * C0 + 2 * c + 2)
                nc.vector.tensor_tensor(w_lo[k % 2][:], W[:, n, :], w_hi[k % 2][:].bitcast(F32),
                                        ALU.subtract).then_inc(wlo_done, 1)

            def after_pass(p):
                dve.wait_ge(mm_done, 2 * C0 + 2 * NK * (p + 1) + SPLIT)
                nc.vector.tensor_tensor(x2[:, HALF * p:HALF * (p + 1), :], x2[:, HALF * p:HALF * (p + 1), :],
                                        ps[:, :, 0:LIVE], ALU.add).then_inc(acc_done, 1)
            dve.wait_ge(x2_in, 16)
            halves(dve, w_part, split_lo, after_pass)

        @block.tensor
        def _(pe):
            def f(c, k, start, stop):
                pe.wait_ge(wlo_done, c + 1)
                for r in range(2):
                    pe.wait_ge(lo_done, 2 * C0 + 2 * c + r + 2 * RAW + 1)
                    a, b = hi[(2 * k + r) % SPLIT], lo[(2 * k + r) % SPLIT]
                    for j in range(QT):
                        o = ps[:, QT * r + j, 0:LIVE]
                        pe.matmul(o, a[:, j], w_hi[k % 2][:], start=start, stop=False, skip_group_check=True)
                        pe.matmul(o, a[:, j], w_lo[k % 2][:], start=False, stop=False, skip_group_check=True)
                        m = pe.matmul(o, b[:, j], w_hi[k % 2][:], start=False, stop=stop, skip_group_check=True)
                    m.then_inc(mm_done, 1)
            for p in range(2):
                if p == 1:
                    pe.wait_ge(acc_done, 1)
                for k in range(4):
                    f(NK * p + k, k, k == 0, False)
                with pe.Fori(1, NK // 4 - 1) as i:
                    for k in range(4):
                        f(NK * p + 4 * i + k, k, False, False)
                for k in range(4):
                    f(NK * p + NK - 4 + k, k, False, k == 3)

    y_done = sem("y_done")
    with nc.Block() as block:
        @block.scalar
        def _(act):
            act_norm(act, x2, KD, LIVE, fin, fin_r[:, 0], 2 * KD + KC, D, 0)

        @block.tensor
        def _(pe):
            pe_norm(pe, KD, LIVE, fin, 2 * KD + KC)

        @block.vector
        def _(dve):
            dve_rstd(dve, LIVE, fin_r[:, 0], fin_r[:, 1], fin_r[:, 2], 4, D, 0)
            for j in range(KD):
                nc.vector.scalar_tensor_tensor(out=x2[:, j, :], in0=x2[:, j, :], scalar=gain[:, 2, j:j + 1],
                                               in1=fin_r[:, 1], op0=ALU.mult, op1=ALU.mult).then_inc(y_done, 1)

        @block.sync
        def _(sp):
            for q in range(4):
                sp.wait_ge(y_done, 4 * q + 4)
                sp.dma_start(yT[:, 4 * q:4 * q + 4], x2[:, 4 * q:4 * q + 4, :]).then_inc(out_done, 16)
            sp.wait_ge(out_done, 64)


def build(nc, arrays):
    args = {}
    for name, v in arrays.items():
        args[name] = nc.dram_tensor(name, v.shape, mybir.dt.from_np(v.dtype), kind="ExternalInput").ap()
    args["expert_v"] = args["expert_v"].rearrange("(a n) (h d) -> h n a d", a=NK, h=2)
    outs = {"yT": (P, KD, LIVE), "kvT": (2 * DA, NT), "conv_p": (DC, TAPS - 1), "conv_s": (P, KC, DEC, TAPS - 1)}
    for name, shape in outs.items():
        args[name] = nc.dram_tensor(name, shape, F32, kind="ExternalOutput").ap()
    trunk(nc, *args.values())


def kernel(**inputs):
    import numpy as np
    import concourse.bacc as bacc
    from concourse.bass_utils import run_bass_kernel_spmd

    def tiles(w):
        k, c = w.shape
        return w.reshape(k // (HALF * P), HALF, P, c // P, P).transpose(3, 0, 2, 1, 4)

    def columns(v):
        v = v.reshape(v.shape[:-1] + (v.shape[-1] // P, P))
        return np.moveaxis(v, -1, 0)

    a = {k: np.asarray(v) for k, v in inputs.items()}
    tokens = np.concatenate([a["x_prompt"][0], a["x_sample"][:, 0], a["meta_tokens"]], axis=0)
    w_in = tiles(a["w_in"][0])
    order = list(range(3 * KA))
    for c in range(KC):
        order += [3 * KA + KC + c, 3 * KA + c]
    order += list(range(3 * KA + 2 * KC, T_IN))
    w_br = np.concatenate([tiles(a["w_branch_attn"][0]), tiles(a["w_branch_conv"][0])], axis=1)
    weights = np.concatenate([w_in[order], w_br, tiles(a["w_out"][0]), tiles(a["w_query"][0])], axis=0)
    u = a["expert_u"][0].reshape(NK, NK, 2, HALF, P).transpose(1, 2, 4, 3, 0)
    arrays = {
        "weights": weights.reshape(-1, P, HALF * P),
        "xT": columns(tokens).transpose(0, 2, 1),
        "gains": columns(np.stack([a["norm_mix_g"][0], a["norm_ffn_g"][0], a["norm_final_g"]])),
        "u_tiles": u.reshape(-1, P, HALF * P),
        "expert_v": a["expert_v"][0],
        "cache_k": a["cache_k"][0].reshape(-1, DA),
        "cache_v": a["cache_v"][0].reshape(-1, DA),
        "stateT": columns(a["state_conv"][0]).transpose(0, 3, 1, 2),
        "page_table": np.broadcast_to(a["page_table"].reshape(1, -1), (P, DEC * PAGES)),
        "sb_bias": np.broadcast_to(a["sb_bias"], (P, HEADS)),
        "w_dwT": columns(a["w_dw"][0]).transpose(0, 2, 1),
        "conv_vecs": columns(np.stack([a["b_dw"][0], a["conv_ln_g"][0], a["conv_ln_b"][0]])),
        "sub_keysT": a["sub_keys"][0].transpose(2, 0, 1),
    }
    arrays = {k: np.ascontiguousarray(v) for k, v in arrays.items()}
    nc = bacc.Bacc("TRN2", target_bir_lowering=False, num_devices=1)
    build(nc, arrays)
    r = run_bass_kernel_spmd(nc, [arrays], core_ids=[0]).results[0]
    y = np.transpose(r["yT"], (2, 1, 0)).reshape(LIVE, D)
    kv = np.transpose(r["kvT"].reshape(2, HEADS, HD, NT), (0, 3, 1, 2))
    prompt = np.concatenate([kv[:, LIVE:], kv[:, :SEQ]], axis=1)[:, None, None]
    sample = kv[:, SEQ:LIVE][:, None, :, None]
    conv_prompt = np.transpose(r["conv_p"], (1, 0))[None, None]
    conv_sample = np.transpose(r["conv_s"], (2, 3, 1, 0)).reshape(1, DEC, TAPS - 1, DC)
    return (y[None, :SEQ], y[SEQ:, None], prompt[0], prompt[1], conv_prompt, sample[0], sample[1], conv_sample)
```

```python
from contextlib import ExitStack

import concourse.bass as bass
from concourse import mybir

F32 = mybir.dt.float32
F32R = mybir.dt.float32r
U32 = mybir.dt.uint32
I32 = mybir.dt.int32
ACT = mybir.ActivationFunctionType
ALU = mybir.AluOpType
AX_X = mybir.AxisListType.X

P = 128
D = 2048
KD = D // P
SEQ, DEC, META = 256, 8, 16
LIVE = SEQ + DEC
NT = LIVE + META
HEADS, HD = 16, 64
DA = HEADS * HD
KA = DA // P
DC = 1024
KC = DC // P
TAPS = 31
PAGES = 2
PH, PK = 8, 16
NK = 128
RMS_EPS, LN_EPS = 1e-6, 1e-5

HALF = 8
QT = HALF // 2
RAW, SPLIT = 4, 4
AHEAD = 3
T_IN, T_BR, T_OUT, T_QRY = 72, 16, 16, 16
PAIR_ATT = 24
PAIR_Q, PAIR_V, PAIR_GLU, PAIR_IN = 4, 12, 20, T_IN // 2
PAIR_BR = PAIR_IN + T_BR // 2
PAIR_OUT = PAIR_BR + T_OUT // 2
PAIR_QRY = PAIR_OUT + T_QRY // 2
PAIR_U = PAIR_QRY + NK // 2
HEAD_PAIRS = 5
SPARE_TILE = PH * HEAD_PAIRS * 2
GS = 6
TT = 3
NEG_BIG = -3.0e38
MASKED = -1.0e30


def spread(ap, at, count):
    wide = ap.unsqueeze(at)
    shape = list(wide.shape)
    shape[at] = count
    return wide.broadcast_to(shape)


def trunk(nc, *args):
    with ExitStack() as ctx:
        program(nc, ctx, *args)


def program(nc, ctx, weights, xT, gains, u_tiles, expert_v, cache_k, cache_v, stateT, page_table, sb_bias,
          w_dwT, conv_vecs, sub_keysT, yT, kvT, conv_p, conv_s):
    at = {}
    base = 16512

    def place(name, offset, shape, dt=F32):
        size = 4
        for n in shape[1:]:
            size *= n
        t = nc.alloc_sbuf_tensor_at(name, shape, dt, offset=base + offset)
        at[name] = -(-(offset + size) // 32) * 32
        return t

    raw = place("raw", 0, [P, RAW, HALF, P])
    hi = [place(f"hi{s}", at["raw"] + 2048 * s, [P, QT, P], F32R) for s in range(SPLIT)]
    lo = [place(f"lo{s}", at["hi3"] + 2048 * s, [P, QT, P], F32R) for s in range(SPLIT)]
    ident = place("ident", at["lo3"], [P, P])
    ones = place("ones", at["ident"], [P, P])
    neg_tri = place("neg_tri", at["ones"], [P, P])
    neg_ones = place("neg_ones", at["neg_tri"], [P, P])
    mask = place("mask", at["neg_ones"], [P, P])
    pen = place("pen", at["mask"], [P, P])
    iota = place("iota", at["pen"], [P, P])
    gain = place("gain", at["iota"], [P, 3, KD])
    dw = place("dw", at["gain"], [P, KC, TAPS])
    cvec = place("cvec", at["dw"], [P, 3, KC])
    bias = place("bias", at["cvec"], [P, HEADS])
    eps = place("eps", at["bias"], [P, 2])
    pages = place("pages", at["eps"], [P, DEC * PAGES], I32)
    page_f = place("page_f", at["pages"], [P, DEC * PAGES])
    part = place("part", at["page_f"], [P, 2])
    rows = place("rows", at["part"], [P, DEC * PAGES], I32)
    X = 38400
    assert at["rows"] <= X
    gates = place("gates", X, [P, 2 * KD, LIVE])
    h2 = [place("h2_hi", X, [P, KD, LIVE], F32R), place("h2_lo", X + 16896, [P, KD, LIVE], F32R)]
    Y = X + 33792
    x = place("x", Y, [P, KD, NT])
    yc = place("yc", at["x"], [P, KC, LIVE])
    attn = place("attn", at["yc"], [P, KA, LIVE])
    qkv = place("qkv", at["attn"], [P, 3 * KA, NT])
    work = place("work", at["qkv"], [P, 4, NT])
    rstd = place("rstd", at["work"], [P, NT])
    root = place("root", at["rstd"], [P, NT])
    tmp = place("tmp", at["root"], [P, NT])
    Z = at["tmp"]
    h = [place("h_hi", Z, [P, KD, NT], F32R), place("h_lo", Z + 17920, [P, KD, NT], F32R)]
    PADC = TAPS - 1
    cv = place("cv", at["h_lo"], [P, KC, PADC + META + SEQ])
    st = place("st", at["cv"], [P, KC, DEC, TAPS])
    sg = place("sg", at["st"], [P, NT])
    stp = place("stp", at["sg"], [P, DEC, TAPS])
    dg = place("dg", X, [P, KA, P])
    prod = place("prod", at["dg"], [P, DA])
    zd = place("zd", X + 8 * 1056, [P, DEC, PAGES, HEADS])
    ed = place("ed", at["zd"], [P, DEC, PAGES, HEADS])
    sd = place("sd", at["ed"], [P, DEC, PAGES, HEADS])
    ring = place("ring", X + 16 * 1056, [P, 4, DA])
    assert at["ring"] <= Y
    GH = 4
    eab = place("eab", Y, [P, GH, 384])
    sab = place("sab", at["eab"], [P, GH, 384])
    em = place("em", at["sab"], [META, GH, 256])
    assert at["em"] <= at["x"]
    sm = place("sm", at["stp"], [META, GH, 256])
    vn = place("vn", at["sm"], [P, 3, GH * HD])
    qg = place("qg", at["vn"], [P, 3, GH // 2, NT])
    assert at["qg"] <= 212800
    QK = at["attn"]
    at_p = [place("at_hi", QK, [P, KA, LIVE], F32R), place("at_lo", QK + 8448, [P, KA, LIVE], F32R)]
    cv_p = [place("cv_hi", QK + 16896, [P, KC, LIVE], F32R), place("cv_lo", QK + 25344, [P, KC, LIVE], F32R)]
    mx = [place("mx_hi", QK + 33792, [P, KD, LIVE], F32R), place("mx_lo", QK + 50688, [P, KD, LIVE], F32R)]
    t2 = place("t2", at["mx_lo"], [P, 2, LIVE])
    W2 = Y + 110592
    work2 = place("work2", W2, [P, 4, LIVE])
    acc2 = place("acc2", at["work2"], [P, LIVE])
    rstd2 = place("rstd2", at["acc2"], [P, LIVE])
    root2 = place("root2", at["rstd2"], [P, LIVE])
    tmp2 = place("tmp2", at["root2"], [P, LIVE])
    raw2 = [place("raw2_hi", QK, [P, KD, LIVE], F32R), place("raw2_lo", QK + 16896, [P, KD, LIVE], F32R)]
    acc = place("acc", at["vn"] - 4 * 3 * GH * HD, [P, NT])
    W = place("W", Y, [P, NK, LIVE])
    Wf = W[:].rearrange("p a b -> p (a b)")
    spare = SPARE_TILE * LIVE
    offs = [spare]

    def carve(n):
        a = offs[0]
        offs[0] += n
        return Wf[:, a:a + n]

    sc_all = carve(TT * 2 * PH * NK).rearrange("p (t q n) -> p t q n", t=TT, q=2 * PH)
    sh = carve(TT * 2 * NK).rearrange("p (t q n) -> p t q n", t=TT, q=2)
    cand = carve(TT * PK * PK).rearrange("p (t a b) -> p t a b", t=TT, a=PK)
    eq = carve(TT * PK * PK).rearrange("p (t a b) -> p t a b", t=TT, a=PK)
    top1 = carve(TT * 2 * PK).rearrange("p (t q k) -> p t q k", t=TT, q=2)
    idx1 = carve(TT * 2 * PK).rearrange("p (t q k) -> p t q k", t=TT, q=2)
    idx1f = carve(TT * 2 * PK).rearrange("p (t q k) -> p t q k", t=TT, q=2)
    top2 = carve(TT * PK).rearrange("p (t k) -> p t k", t=TT)
    pos2 = carve(TT * PK).rearrange("p (t k) -> p t k", t=TT)
    pab = carve(2 * TT * PK).rearrange("p (q t k) -> p q t k", q=2, t=TT)
    pabf = carve(2 * TT * PK).rearrange("p (q t k) -> p q t k", q=2, t=TT)
    assert offs[0] <= NK * LIVE
    qry = W[:, 26:28, :]
    skT = W[:, 28, 0:2 * NK].rearrange("p (q n) -> p q n", q=2)
    chosen = place("chosen", at["W"], [P, 3, TT, PH, PK])
    lhot = place("lhot", X, [P, GS, 4, NK])
    rhot = place("rhot", at["lhot"], [P, GS, 4, NK])
    rdiff = place("rdiff", at["rhot"], [P, 4, NK])
    ldiff = place("ldiff", at["rdiff"], [P, 2, 2, NK])
    chT = place("chT", at["ldiff"], [P, 4, LIVE])
    sums = place("sums", at["chT"], [P, 2, TT, PH])
    x2 = place("x2", X, [P, KD, LIVE])
    w_hi = [place(f"w_hi{s}", at["x2"] + 1056 * s, [P, LIVE], F32R) for s in range(2)]
    w_lo = [place(f"w_lo{s}", at["w_hi1"] + 1056 * s, [P, LIVE], F32R) for s in range(2)]
    fin = place("fin", at["w_lo1"], [P, 4, LIVE])
    fin_r = place("fin_r", at["fin"], [P, 4, LIVE])
    assert at["fin_r"] <= Y

    ps = ctx.enter_context(nc.psum_tensor("ps", [P, 8, 512], F32))
    x2_dram = nc.dram_tensor("x2_spill", [P, KD, LIVE], F32, kind="Internal").ap()

    def sem(name):
        return ctx.enter_context(nc.semaphore(name))

    raw_in = [sem(f"raw_in{s}") for s in range(RAW)]
    hi_done, lo_done, mm_done = sem("hi_done"), sem("lo_done"), sem("mm_done")
    tile_free = [sem("tile_free0"), sem("tile_free1")]
    vec_step = sem("vec_step")
    act_step = sem("act_step")
    steps = {"vec": 0, "act": 0}

    def vchain(ins):
        steps["vec"] += 1
        ins.then_inc(vec_step, 1)

    def vwait(dve):
        dve.wait_ge(vec_step, steps["vec"])

    a_halves = weights

    def load_half(sp, c, s, src):
        sp.wait_ge(hi_done, 2 * c + 2)
        sp.wait_ge(lo_done, 2 * c + 2)
        sp.dma_start(raw[:, s].rearrange("p a b -> p (a b)"), src).then_inc(raw_in[s], 16)

    def raw_quarter(k):
        return raw[:, k // 2 % RAW, QT * (k % 2):QT * (k % 2) + QT]

    def split_hi(act, q0, k):
        act.wait_ge(raw_in[k // 2 % RAW], 2 * q0 + 16 * (k // (2 * RAW)) + 16)
        act.wait_ge(mm_done, q0 + k + 1)
        nc.scalar.copy(hi[k % SPLIT][:], raw_quarter(k)).then_inc(hi_done, 1)

    def split_lo(dve, q0, k):
        dve.wait_ge(hi_done, q0 + k + 2 * RAW + 1)
        dve.wait_ge(mm_done, q0 + k + 1)
        nc.vector.tensor_tensor(lo[k % SPLIT][:], raw_quarter(k), hi[k % SPLIT][:].bitcast(F32),
                                ALU.subtract).then_inc(lo_done, 1)

    def tile_done(eng, i, b):
        eng.wait_ge(mm_done, 8 * i + 4 * b + 4 + SPLIT)

    def quarter_products(pe, q0, k, out, rhs, first, n, start, stop):
        pe.wait_ge(lo_done, q0 + k + 2 * RAW + 1)
        for j in range(QT):
            a, b = hi[k % SPLIT][:, j], lo[k % SPLIT][:, j]
            rh, rl = rhs[0][:, first + j, 0:n], rhs[1][:, first + j, 0:n]
            pe.matmul(out, a, rh, start=start and j == 0, stop=False)
            pe.matmul(out, a, rl, start=False, stop=False)
            m = pe.matmul(out, b, rh, start=False, stop=stop and j == QT - 1)
        m.then_inc(mm_done, 1)

    def pe_tile(pe, i, b, rhs, n):
        for r in range(4):
            quarter_products(pe, 8 * i, 4 * b + r, ps[:, b, 0:n], rhs, QT * r, n, r == 0, r == 3)

    def pe_pairs(pe, first, last, rhs, n):
        with pe.Fori(first, last) as i:
            for b in range(2):
                pe.wait_ge(tile_free[b], i + 1)
                pe_tile(pe, i, b, rhs, n)

    def four(split, eng, i, b):
        for k in range(4 * b + AHEAD, 4 * b + AHEAD + 4):
            split(eng, 8 * i, k)

    def act_pairs(act, first, last, even, odd):
        with act.Fori(first, last) as i:
            for b, read in ((0, even), (1, odd)):
                four(split_hi, act, i, b)
                if read:
                    tile_done(act, i, b)
                    read(i)

    sq_ready, sq_used, sum_ready, root_ready = sem("sq_ready"), sem("sq_used"), sem("sum_ready"), sem("root_ready")
    norm_ready, norm_hi, norm_lo = sem("norm_ready"), sem("norm_hi"), sem("norm_lo")
    CALL = (0, KD, KD + KC, KD + KC + KD)
    CALL_N = KD

    def pool_sum(pool, total, slots, j, call, n):
        pool.wait_ge(sq_ready, call + j + 1)
        if j >= 2:
            pool.wait_ge(sq_used, call + j)
        nc.gpsimd.tensor_tensor(total[:, 0:n], slots[:, 0, 0:n] if j == 1 else total[:, 0:n], slots[:, j % 4, 0:n],
                                ALU.add).then_inc(sq_used, 2 if j == 1 else 1)

    def pe_sum(pe, total, call, tiles, n):
        pe.wait_ge(sq_used, call + tiles)
        pe.matmul(ps[:, 7, 0:n], ones[:], total[:, 0:n], start=True, stop=True).then_inc(sum_ready, 1)

    def act_root(act, rt, nth, dim, e, n):
        act.wait_ge(sum_ready, nth)
        nc.scalar.activation(rt[:, 0:n], ps[:, 7, 0:n], ACT.Sqrt, bias=eps[:, e:e + 1],
                             scale=1.0 / dim).then_inc(root_ready, 1)

    def dve_rstd(dve, n, rt, rs, tp, nth, dim, e):
        dve.wait_ge(root_ready, nth)
        vchain(nc.vector.reciprocal(rs[:, 0:n], rt[:, 0:n]))
        vwait(dve)
        vchain(nc.vector.tensor_scalar(rt[:, 0:n], ps[:, 7, 0:n], 1.0 / dim, eps[:, e:e + 1], ALU.mult, ALU.add))
        vchain(nc.vector.tensor_tensor(tp[:, 0:n], rs[:, 0:n], rs[:, 0:n], ALU.mult))
        vwait(dve)
        vchain(nc.vector.tensor_tensor(tp[:, 0:n], tp[:, 0:n], rt[:, 0:n], ALU.mult))
        vwait(dve)
        vchain(nc.vector.tensor_scalar(tp[:, 0:n], tp[:, 0:n], -0.5, 1.5, ALU.mult, ALU.add))
        vwait(dve)
        vchain(nc.vector.tensor_tensor(rs[:, 0:n], rs[:, 0:n], tp[:, 0:n], ALU.mult))
        vwait(dve)

    def norm_scaled(src, slots, s, j, g, rs, n):
        nc.vector.scalar_tensor_tensor(out=slots[:, s, 0:n], in0=src[:, j, 0:n],
                                       scalar=gain[:, g, j:j + 1] if isinstance(j, int) else gain[:, g, bass.ds(j, 1)],
                                       in1=rs[:, 0:n], op0=ALU.mult, op1=ALU.mult).then_inc(norm_ready, 1)

    def norm_hi_part(act, parts, slots, s, j, count, n):
        act.wait_ge(norm_ready, count + 1)
        nc.scalar.copy(parts[0][:, j, 0:n], slots[:, s, 0:n]).then_inc(norm_hi, 1)

    def norm_lo_part(dve, parts, slots, s, j, count, n):
        dve.wait_ge(norm_hi, count + 1)
        nc.vector.tensor_tensor(parts[1][:, j, 0:n], slots[:, s, 0:n], parts[0][:, j, 0:n].bitcast(F32),
                                ALU.subtract).then_inc(norm_lo, 1)

    def pe_tile_follow(pe, i, b, rhs, n, ready, count):
        for r in range(4):
            pe.wait_ge(ready, count + QT * (r + 1))
            quarter_products(pe, 8 * i, 4 * b + r, ps[:, b, 0:n], rhs, QT * r, n, r == 0, r == 3)

    x_in = [sem(f"x_in{c}") for c in range(4)]
    gain_in, vec_in, const_ready = sem("gain_in"), sem("vec_in"), sem("const_ready")
    raw_h_hi, raw_h_lo = sem("raw_h_hi"), sem("raw_h_lo")
    fill0, glu_done = sem("fill0"), sem("glu_done")
    rows_ready, part_ready, out_done, kv_done = sem("rows_ready"), sem("part_ready"), sem("out_done"), sem("kv_done")
    conv_done, tap_done = sem("conv_done"), sem("tap_done")

    page_in = [sem(f"page_in{s}") for s in range(4)]
    page_used, dg_ready, qb_ready, zd_done = sem("page_used"), sem("dg_ready"), sem("qb_ready"), sem("zd_done")
    vt_ready, vn_ready, qg_ready = sem("vt_ready"), sem("vn_ready"), sem("qg_ready")
    d_act, d_vec, d_pe, d_vec2 = sem("d_act"), sem("d_vec"), sem("d_pe"), sem("d_vec2")
    z_ready, zm_ready, z_kept, relu_done = sem("z_ready"), sem("zm_ready"), sem("z_kept"), sem("relu_done")
    abs_done, e_done, ln_done, sp_step = sem("abs_done"), sem("e_done"), sem("ln_done"), sem("sp_step")
    sp_ready, t_ready, m_ready, aexp_done = sem("sp_ready"), sem("t_ready"), sem("m_ready"), sem("aexp_done")
    o_ready, o_done = sem("o_ready"), sem("o_done")
    act_go, pe_go, dve_go = sem("act_go"), sem("pe_go"), sem("dve_go")
    NG = HEADS // GH
    NP = DEC * PAGES

    def norm_tiles(t):
        first = 3 * (t - 1) if t < 3 else 2 * t
        return range(first, first + (3 if t < 3 else 2))

    def meta_bank(i):
        return ps[0:META, 6 + i % 2, 256 * (i // 2):256 * (i // 2) + 256]

    with nc.Block() as block:
        @block.sync
        def _(sp):
            sp.dma_start(gain[:], gains).then_inc(gain_in, 16)
            for c in range(4):
                sp.dma_start(x[:, QT * c:QT * c + QT], xT[:, QT * c:QT * c + QT]).then_inc(x_in[c], 16)
                sp.dma_start(raw[:, c].rearrange("p a b -> p (a b)"), a_halves[c]).then_inc(raw_in[c], 16)
            for t, src in ((dw, w_dwT), (cvec, conv_vecs), (bias, sb_bias), (pages, page_table)):
                sp.dma_start(t[:], src).then_inc(vec_in, 16)
            for j in range(KC):
                sp.dma_start(st[:, j, :, 0:PADC], stateT[:, j]).then_inc(vec_in, 16)

            def stream(first, last):
                with sp.Fori(first, last) as i:
                    for s in range(RAW):
                        load_half(sp, 4 * i + s, s, a_halves[4 * i + s])
            stream(1, PAIR_V + 2)
            for b in range(2):
                sp.wait_ge(tile_free[b], PAIR_V + 1)
            sp.dma_start(kvT.rearrange("(j p) t -> p j t", p=P), qkv[:, KA:3 * KA, :]).then_inc(kv_done, 16)
            stream(PAIR_V + 2, PAIR_GLU + 2)
            sp.wait_ge(conv_done, 3 * KC)
            sp.dma_start(conv_p.rearrange("(j p) t -> p j t", p=P), cv[:, :, META + SEQ:]).then_inc(kv_done, 16)
            for j in range(KC):
                sp.dma_start(conv_s[:, j], st[:, j, :, 1:TAPS]).then_inc(kv_done, 16)
            stream(PAIR_GLU + 2, PAIR_IN + 1)
            sp.wait_ge(kv_done, 16 * (2 + KC))

        @block.gpsimd
        def _(pool):
            pool.sem_inc(tile_free[0], 1)
            pool.sem_inc(tile_free[1], 1)
            nc.gpsimd.memset(ones[:], 1.0).then_inc(fill0, 1)
            nc.gpsimd.memset(eps[:, 0:1], RMS_EPS).then_inc(fill0, 1)
            nc.gpsimd.memset(eps[:, 1:2], LN_EPS).then_inc(fill0, 1)
            nc.gpsimd.memset(ident[:], 0.0).then_inc(const_ready, 1)
            nc.gpsimd.memset(neg_tri[:], -1.0).then_inc(const_ready, 1)
            nc.gpsimd.memset(mask[:], 1.0).then_inc(const_ready, 1)
            nc.gpsimd.memset(neg_ones[:], -1.0).then_inc(const_ready, 1)
            nc.gpsimd.memset(pen[:], 0.0).then_inc(const_ready, 1)
            for j in range(KC):
                nc.gpsimd.memset(cv[:, j, 0:PADC], 0.0).then_inc(const_ready, 1)
            pool.wait_ge(const_ready, 5 + KC)
            nc.gpsimd.affine_select(out=ident[:], in_=ident[:], compare_op=ALU.not_equal, fill=1.0, base=0,
                                    pattern=[[-1, P]], channel_multiplier=1).then_inc(const_ready, 1)
            nc.gpsimd.affine_select(out=neg_tri[:], in_=neg_tri[:], compare_op=ALU.is_ge, fill=0.0, base=0,
                                    pattern=[[-1, P]], channel_multiplier=1).then_inc(const_ready, 1)
            nc.gpsimd.affine_select(out=mask[:], in_=mask[:], compare_op=ALU.is_gt, fill=0.0, base=0,
                                    pattern=[[1, P]], channel_multiplier=-1).then_inc(const_ready, 1)
            nc.gpsimd.affine_select(out=pen[:], in_=pen[:], compare_op=ALU.is_gt, fill=MASKED, base=0,
                                    pattern=[[1, P]], channel_multiplier=-1).then_inc(const_ready, 1)
            nc.gpsimd.iota(iota[:], pattern=[[1, P]], base=0, channel_multiplier=0,
                           allow_small_or_imprecise_dtypes=True).then_inc(const_ready, 1)
            nc.gpsimd.iota(part[:], pattern=[[0, 2]], base=0, channel_multiplier=1,
                           allow_small_or_imprecise_dtypes=True).then_inc(part_ready, 1)

            for j in range(1, KD):
                pool_sum(pool, acc, work, j, CALL[0], NT)
            pool.wait_ge(rows_ready, 1)
            pool.wait_ge(tile_free[0], PAIR_Q + 1)
            pool.wait_ge(tile_free[1], PAIR_Q + 1)
            for n in range(2 * NP):
                if n >= 4:
                    pool.wait_ge(page_used, n - 3)
                cache = cache_k if n < NP else cache_v
                nc.gpsimd.indirect_dma_start(
                    ring[:, n % 4, :], None, cache,
                    bass.IndirectOffsetOnAxis(ap=rows[:, n % NP:n % NP + 1], axis=0)).then_inc(page_in[n % 4], 16)
            pool.wait_ge(page_used, 2 * NP)
            with pool.Fori(0, NG) as g:
                pool.wait_ge(m_ready, g + 1)
                nc.gpsimd.tensor_copy(qg[:, 0, :, 0:LIVE], qkv[:, bass.ds(2 * g, 2), 0:LIVE]).then_inc(qg_ready, 1)
                nc.gpsimd.tensor_copy(
                    qg[:, 1:3], qkv[:, KA:3 * KA, :].rearrange("p (s j) t -> p s j t", s=2)[:, :, bass.ds(2 * g, 2), :])\
                    .then_inc(qg_ready, 1)

        @block.scalar
        def _(act):
            act.sem_inc(hi_done, 2 * RAW)
            act.wait_ge(gain_in, 16)
            for c in range(4):
                act.wait_ge(x_in[c], 16)
                for j in range(QT * c, QT * c + QT):
                    nc.scalar.activation(h2[0][:, j, :], x[:, j, 0:LIVE], ACT.Copy, scale=gain[:, 0, j:j + 1])\
                        .then_inc(raw_h_hi, 1)
                if c < AHEAD:
                    split_hi(act, 0, c)

            def copy_out(b):
                def f(i):
                    nc.scalar.copy(qkv[:, 2 * i + b, :], ps[:, b, 0:NT]).then_inc(tile_free[b], 1)
                return f

            def glu_gate(i):
                act.wait_ge(glu_done, i - PAIR_V + 1)
                nc.scalar.activation(sg[:], ps[:, 0, 0:NT], ACT.Sigmoid).then_inc(tile_free[0], 1)

            def gate_out(i, b):
                nc.scalar.copy(gates[:, 2 * (i - PAIR_GLU) + b, :], ps[:, b, 0:LIVE]).then_inc(tile_free[b], 1)

            def gate_tile(i, b):
                four(split_hi, act, i, b)
                tile_done(act, i, b)
                gate_out(i, b)

            four(split_hi, act, 0, 0)
            act_root(act, root, 1, D, 0, NT)
            for t in range(1, 2 * PAIR_Q):
                made = norm_tiles(t)
                for k in range(4):
                    split_hi(act, 8 * (t // 2), 4 * (t % 2) + AHEAD + k)
                    if k < len(made):
                        norm_hi_part(act, h, work, made[k] % 4, made[k], made[k], NT)
            act_pairs(act, PAIR_Q, PAIR_V, copy_out(0), copy_out(1))
            act_pairs(act, PAIR_V, PAIR_GLU, glu_gate, None)
            act.wait_ge(d_vec, 1)
            nc.scalar.activation(ed[:], zd[:], ACT.Abs).then_inc(d_act, 1)
            act.wait_ge(d_act, 1)
            nc.scalar.activation(ed[:], ed[:], ACT.Exp, scale=-1.0).then_inc(d_act, 1)
            act.wait_ge(d_act, 2)
            nc.scalar.activation(ed[:], ed[:], ACT.Ln, bias=1.0).then_inc(d_act, 1)
            gate_tile(PAIR_GLU, 0)
            gate_tile(PAIR_GLU, 1)
            act.wait_ge(d_vec2, 1)
            nc.scalar.activation(ed[:], zd[:], ACT.Exp).then_inc(d_act, 1)
            for i in range(PAIR_GLU + 1, PAIR_ATT - 1):
                gate_tile(i, 0)
                gate_tile(i, 1)
            gate_tile(PAIR_GLU + 3, 0)
            act.wait_ge(d_vec, 3)
            gate_tile(PAIR_GLU + 3, 1)
            with act.Fori(0, NG) as g:
                def hi_one(tile, r):
                    split_hi(act, 8 * (PAIR_ATT + 3 * g + tile // 2), 4 * (tile % 2) + AHEAD + r)

                def out(tile):
                    tile_done(act, PAIR_ATT + 3 * g + tile // 2, tile % 2)
                    gate_out(PAIR_ATT + 3 * g + tile // 2, tile % 2)

                for i in range(GH):
                    act.wait_ge(z_ready, GH * g + i + 1)
                    act.sem_inc(act_go, 1)
                    nc.scalar.activation(eab[:, i, :], ps[:, 2 + i, 0:384], ACT.Identity,
                                         bias=bias[:, bass.ds(GH * g + i, 1)]).then_inc(z_kept, 1)
                act.wait_ge(zm_ready, g + 1)
                act.sem_inc(act_go, 1)
                for i in range(GH):
                    nc.scalar.activation(em[:, i, :], meta_bank(i), ACT.Identity,
                                         bias=bias[0:META, bass.ds(GH * g + i, 1)]).then_inc(z_kept, 1)
                hi_one(0, 0)
                act.wait_ge(relu_done, 2 * g + 1)
                nc.scalar.activation(eab[:], eab[:], ACT.Abs).then_inc(abs_done, 1)
                hi_one(0, 1)
                act.wait_ge(relu_done, 2 * g + 2)
                nc.scalar.activation(em[:], em[:], ACT.Abs).then_inc(abs_done, 1)
                hi_one(0, 2)
                act.wait_ge(abs_done, 2 * g + 1)
                nc.scalar.activation(eab[:], eab[:], ACT.Exp, scale=-1.0).then_inc(e_done, 1)
                act.wait_ge(abs_done, 2 * g + 2)
                nc.scalar.activation(em[:], em[:], ACT.Exp, scale=-1.0).then_inc(e_done, 1)
                hi_one(0, 3)
                out(0)
                act.wait_ge(e_done, 2 * g + 1)
                nc.scalar.activation(eab[:], eab[:], ACT.Ln, bias=1.0).then_inc(ln_done, 1)
                act.wait_ge(e_done, 2 * g + 2)
                nc.scalar.activation(em[:], em[:], ACT.Ln, bias=1.0).then_inc(ln_done, 1)
                for r in range(4):
                    hi_one(1, r)
                out(1)
                for r in range(4):
                    hi_one(2, r)
                out(2)
                for i in range(GH):
                    act.wait_ge(t_ready, GH * g + i + 1)
                    act.sem_inc(act_go, 1)
                    nc.scalar.activation(eab[:, i, :], ps[:, 2 + i, 0:384], ACT.Exp,
                                         bias=bias[:, bass.ds(GH * g + i, 1)]).then_inc(aexp_done, 1)
                act.wait_ge(m_ready, g + 2)
                act.sem_inc(act_go, 1)
                for i in range(GH):
                    nc.scalar.activation(em[:, i, :], meta_bank(i), ACT.Exp,
                                         bias=bias[0:META, bass.ds(GH * g + i, 1)]).then_inc(aexp_done, 1)
                for tile in range(3, 6):
                    for r in range(4):
                        hi_one(tile, r)
                    out(tile)

        @block.tensor
        def _(pe):
            pe.sem_inc(o_done, 1)
            pe.sem_inc(m_ready, 1)
            pe.sem_inc(mm_done, SPLIT)
            pe.wait_ge(fill0, 3)
            pe_tile_follow(pe, 0, 0, h2, LIVE, raw_h_lo, 0)
            pe_sum(pe, acc, CALL[0], KD, NT)
            pe.wait_ge(tile_free[1], 1)
            pe_tile(pe, 0, 1, h2, LIVE)
            pe_pairs(pe, 1, PAIR_Q, h2, LIVE)
            pe.wait_ge(norm_lo, KD)
            pe_pairs(pe, PAIR_Q, PAIR_V, h, NT)
            with pe.Fori(PAIR_V, PAIR_GLU) as i:
                pe.wait_ge(tile_free[0], i + 1)
                pe_tile(pe, i, 0, h, NT)
                pe.wait_ge(dg_ready, i - PAIR_V + 1)
                for c in range(2):
                    m = pe.matmul(ps[:, 2 + c, :], ones[:], dg[:, 4 * c:4 * c + 4, :], start=True, stop=True)
                m.then_inc(qb_ready, 1)
                pe.wait_ge(tile_free[1], i + 1)
                pe_tile(pe, i, 1, h, NT)
            def gate_tile(t):
                pe.wait_ge(tile_free[t % 2], PAIR_GLU + t // 2 + 1)
                pe_tile(pe, PAIR_GLU + t // 2, t % 2, h, LIVE)

            gate_tile(0)
            pe.wait_ge(d_vec, 2)
            pe.matmul(ps[:, 4, 0:256], neg_tri[:], sd[:], start=True, stop=False)
            pe.matmul(ps[:, 4, 0:256].rearrange("p (b g h) -> p b g h", b=DEC, g=PAGES)[:, :, 0, :], neg_ones[:],
                      sd[:, :, 1, :], start=False, stop=True).then_inc(d_pe, 1)
            gate_tile(1)
            gate_tile(2)
            pe.wait_ge(d_act, 4)
            for b in range(DEC):
                for g in range(PAGES):
                    n = NP + 2 * b + g
                    pe.wait_ge(page_in[n % 4], 16 * (n // 4 + 1))
                for j in range(KA):
                    for g in range(PAGES):
                        n = NP + 2 * b + g
                        m = pe.matmul(ps[:, 5, 16 * j + 2 * b:16 * j + 2 * b + 2], ring[:, n % 4, P * j:P * j + P],
                                      ed[:, b, g, 2 * j:2 * j + 2], start=g == 0, stop=g == 1)
                m.then_inc(page_used, 2)
                if b % 2 == 1:
                    gate_tile(3 + b // 2)
            gate_tile(7)
            pe.wait_ge(d_vec, 3)
            with pe.Fori(0, NG) as g:
                def tile(t):
                    i = PAIR_ATT + 3 * g + t // 2
                    pe.wait_ge(tile_free[t % 2], i + 1)
                    pe_tile(pe, i, t % 2, h, LIVE)

                def q_of(i):
                    r = HD * (i % 2)
                    return qg[r:r + HD, 0, i // 2]

                def k_of(i):
                    r = HD * (i % 2)
                    return qg[r:r + HD, 1, i // 2]

                pe.wait_ge(qg_ready, 2 * g + 2)
                pe.wait_ge(o_done, g + 1)
                for blk in range(3):
                    at_col, n = ((0, P), (P, P), (LIVE, META))[blk]
                    for j in range(GH // 2):
                        o = ps[0:n, 6 + blk // 2, 256 * (blk % 2) + P * j:256 * (blk % 2) + P * j + P]
                        m = pe.transpose(o, qg[:, 2, j, at_col:at_col + n], ident[:])
                m.then_inc(vt_ready, 1)
                for i in range(GH):
                    q, k = q_of(i), k_of(i)
                    pe.matmul(ps[:, 2 + i, 0:256], k[:, 0:P], q[:, 0:SEQ], start=True, stop=True)
                    pe.matmul(ps[:, 2 + i, 256:384], k[:, P:SEQ], q[:, P:SEQ], start=True, stop=True)\
                        .then_inc(z_ready, 1)
                pe.wait_ge(vn_ready, g + 1)
                pe.sem_inc(pe_go, 1)
                for i in range(GH):
                    m = pe.matmul(meta_bank(i), k_of(i)[:, LIVE:NT], q_of(i)[:, 0:SEQ], start=True, stop=True)
                m.then_inc(zm_ready, 1)
                tile(0)
                tile(1)
                tile(2)
                pe.wait_ge(sp_ready, g + 1)
                for i in range(GH):
                    q, k = q_of(i), k_of(i)
                    pe.matmul(ps[:, 2 + i, 0:256], k[:, 0:P], q[:, 0:SEQ], start=True, stop=False)
                    pe.matmul(ps[:, 2 + i, 0:256], neg_tri[:], sab[:, i, 0:256], start=False, stop=False)
                    pe.matmul(ps[:, 2 + i, 0:P], ident[:], pen[:], start=False, stop=False)
                    pe.matmul(ps[:, 2 + i, P:256], neg_ones[:], sab[:, i, 256:384], start=False, stop=True)
                    pe.matmul(ps[:, 2 + i, 256:384], k[:, P:SEQ], q[:, P:SEQ], start=True, stop=False)
                    pe.matmul(ps[:, 2 + i, 256:384], ident[:], pen[:], start=False, stop=False)
                    pe.matmul(ps[:, 2 + i, 256:384], neg_tri[:], sab[:, i, 256:384], start=False, stop=True)\
                        .then_inc(t_ready, 1)
                for i in range(GH):
                    o = meta_bank(i)
                    pe.matmul(o, k_of(i)[:, LIVE:NT], q_of(i)[:, 0:SEQ], start=True, stop=False)
                    pe.matmul(o, neg_tri[0:META, 0:META], sm[:, i, :], start=False, stop=False)
                    pe.matmul(o, neg_ones[:, 0:META], sab[:, i, 0:256], start=False, stop=False)
                    m = pe.matmul(o[:, P:256], neg_ones[:, 0:META], sab[:, i, 256:384], start=False, stop=True)
                m.then_inc(m_ready, 1)
                tile(3)
                tile(4)
                pe.wait_ge(aexp_done, 2 * GH * (g + 1))
                for i in range(GH):
                    r = HD * (i % 2)
                    o = ps[r:r + HD, 2 + i // 2, 0:256]
                    pe.matmul(o, vn[:, 0, HD * i:HD * i + HD], eab[:, i, 0:256], start=True, stop=False)
                    pe.matmul(o[:, P:256], vn[:, 1, HD * i:HD * i + HD], eab[:, i, 256:384],
                              start=False, stop=False)
                    m = pe.matmul(o, vn[0:META, 2, HD * i:HD * i + HD], em[:, i, :], start=False, stop=True)
                m.then_inc(o_ready, 1)
                tile(5)

        @block.vector
        def _(dve):
            dve.sem_inc(lo_done, 2 * RAW)
            dve.sem_inc(glu_done, 1)
            dve.wait_ge(gain_in, 16)
            for c in range(4):
                dve.wait_ge(x_in[c], 16)
                for j in range(QT * c, QT * c + QT):
                    dve.wait_ge(raw_h_hi, j + 1)
                    nc.vector.scalar_tensor_tensor(out=h2[1][:, j, :], in0=x[:, j, 0:LIVE], scalar=gain[:, 0, j:j + 1],
                                                   in1=h2[0][:, j, :].bitcast(F32), op0=ALU.mult,
                                                   op1=ALU.subtract).then_inc(raw_h_lo, 1)
                    if j >= 4:
                        dve.wait_ge(sq_used, j - 3)
                    nc.vector.tensor_tensor(work[:, j % 4, :], x[:, j, :], x[:, j, :], ALU.mult).then_inc(sq_ready, 1)
                if c < AHEAD:
                    split_lo(dve, 0, c)

            def q_out(t):
                tile_done(dve, t // 2, t % 2)
                nc.vector.scalar_tensor_tensor(out=qkv[:, t, 0:LIVE], in0=ps[:, t % 2, 0:LIVE], scalar=HD ** -0.5,
                                               in1=rstd[:, 0:LIVE], op0=ALU.mult, op1=ALU.mult)\
                    .then_inc(tile_free[t % 2], 1)

            four(split_lo, dve, 0, 0)
            dve_rstd(dve, NT, root, rstd, tmp, 1, D, 0)
            q_out(0)
            for t in range(1, 2 * PAIR_Q):
                made = norm_tiles(t)
                for k in range(4):
                    split_lo(dve, 8 * (t // 2), 4 * (t % 2) + AHEAD + k)
                    if k < len(made):
                        if made[k] >= 4:
                            dve.wait_ge(norm_lo, made[k] - 3)
                            dve.wait_ge(norm_hi, made[k] - 3)
                        norm_scaled(x, work, made[k] % 4, made[k], 0, rstd, NT)
                    if 1 <= k <= len(made):
                        norm_lo_part(dve, h, work, made[k - 1] % 4, made[k - 1], made[k - 1], NT)
                q_out(t)
            dve.wait_ge(vec_in, 16 * (4 + KC))
            dve.wait_ge(part_ready, 1)
            vchain(nc.vector.tensor_copy(page_f[:], pages[:]))
            vwait(dve)
            nc.vector.tensor_scalar(rows[:], page_f[:], float(P), part[:, 0:1], ALU.mult,
                                    ALU.add).then_inc(rows_ready, 1)
            with dve.Fori(PAIR_Q, PAIR_V) as i:
                four(split_lo, dve, i, 0)
                four(split_lo, dve, i, 1)
            def diag(b):
                nc.vector.tensor_tensor(dg[:], spread(ident[:], 1, KA),
                                        spread(qkv[:, 0:KA, bass.ds(b + SEQ, 1)].rearrange("p j o -> p (j o)"), 2, P),
                                        ALU.mult).then_inc(dg_ready, 1)

            def page_products(b, u, g):
                dve.wait_ge(page_in[2 * u + g], 8 * (b - u) + 16)
                nc.vector.tensor_tensor(prod[:], ring[:, 2 * u + g, :],
                                        ps[:, 2:4, :].rearrange("p a b -> p (a b)"), ALU.mult).then_inc(page_used, 1)

            def page_sums(b, g):
                dve.wait_ge(page_used, 2 * b + g + 1)
                nc.vector.tensor_reduce(zd[:, bass.ds(b, 1), g, :].rearrange("p o h -> p (o h)"),
                                        prod[:].rearrange("p (h d) -> p h d", h=HEADS), AX_X,
                                        ALU.add).then_inc(zd_done, 1)

            dve.sem_inc(zd_done, 1)
            dve.wait_ge(const_ready, 10 + KC)
            dve.wait_ge(tile_free[0], PAIR_Q + 1)
            dve.wait_ge(tile_free[1], PAIR_Q + 1)
            with dve.Fori(0, DEC // 2) as m:
                for u in range(2):
                    b = 2 * m + u
                    i = b + PAIR_V
                    diag(b)
                    four(split_lo, dve, i, 0)
                    split_lo(dve, 8 * i, 4 + AHEAD)
                    dve.wait_ge(qb_ready, b + 1)
                    dve.wait_ge(zd_done, 2 * b + 1)
                    page_products(b, u, 0)
                    split_lo(dve, 8 * i, 5 + AHEAD)
                    page_sums(b, 0)
                    split_lo(dve, 8 * i, 6 + AHEAD)
                    dve.wait_ge(zd_done, 2 * b + 2)
                    page_products(b, u, 1)
                    split_lo(dve, 8 * i, 7 + AHEAD)
                    page_sums(b, 1)
                    tile_done(dve, i, 1)
                    dve.wait_ge(tile_free[0], i + 2)
                    nc.vector.tensor_tensor(cv[:, b, PADC + META:], ps[:, 1, 0:SEQ], sg[:, 0:SEQ], ALU.mult)\
                        .then_inc(conv_done, 1)
                    nc.vector.tensor_tensor(cv[:, b, PADC:PADC + META], ps[:, 1, LIVE:NT], sg[:, LIVE:NT], ALU.mult)\
                        .then_inc(conv_done, 1)
                    nc.vector.tensor_tensor(st[:, b, :, PADC], ps[:, 1, SEQ:LIVE], sg[:, SEQ:LIVE], ALU.mult)\
                        .then_inc(conv_done, 1)
                    dve.wait_ge(conv_done, 3 * b + 3)
                    dve.sem_inc(glu_done, 1)
                    dve.sem_inc(tile_free[1], 1)
            dve.wait_ge(const_ready, 5 + KC)

            def tap(j, k):
                return nc.vector.scalar_tensor_tensor(out=yc[:, j, 0:SEQ], in0=cv[:, j, bass.ds(k + META, SEQ)],
                                                      scalar=dw[:, j, bass.ds(k, 1)], in1=yc[:, j, 0:SEQ],
                                                      op0=ALU.mult, op1=ALU.add)

            def tap_tile(i, b, number):
                for k in range(4):
                    split_lo(dve, 8 * i, 4 * b + AHEAD + k)
                    for o in range(6 * number + (0, 2, 3, 5)[k], 6 * number + (2, 3, 5, 6)[k]):
                        dve.wait_ge(tap_done, o + 1)
                        tap(o % KC, 1 + o // KC).then_inc(tap_done, 1)

            dve.wait_ge(zd_done, NP + 1)
            vchain(nc.vector.tensor_tensor(zd[:], zd[:], spread(spread(bias[:], 1, PAGES), 1, DEC), ALU.add))
            vwait(dve)
            nc.vector.tensor_scalar(sd[:], zd[:], 0.0, None, ALU.max).then_inc(d_vec, 1)
            for k in range(4):
                split_lo(dve, 8 * PAIR_GLU, AHEAD + k)
                if k == 1:
                    dve.wait_ge(d_act, 3)
                    dve.wait_ge(d_vec, 1)
                    nc.vector.tensor_tensor(sd[:], sd[:], ed[:], ALU.add).then_inc(d_vec, 1)
                for j in (2 * k, 2 * k + 1):
                    nc.vector.tensor_scalar(yc[:, j, 0:SEQ], cv[:, j, META:META + SEQ], dw[:, j, 0:1],
                                            cvec[:, 0, j:j + 1], ALU.mult, ALU.add).then_inc(tap_done, 1)
            for o in range(6):
                dve.wait_ge(tap_done, o + 1)
                tap(o % KC, 1 + o // KC).then_inc(tap_done, 1)
            tap_tile(PAIR_GLU, 1, 1)
            dve.wait_ge(d_pe, 1)
            nc.vector.tensor_tensor(zd[:].rearrange("p b g h -> p (b g h)"), ps[:, 4, 0:256],
                                    zd[:].rearrange("p b g h -> p (b g h)"), ALU.add).then_inc(d_vec2, 1)
            for t in range(2, 6):
                tap_tile(PAIR_GLU + t // 2, t % 2, t)
            for j in range(KC):
                vchain(nc.vector.tensor_tensor(stp[:], st[:, j], spread(dw[:, j], 1, DEC), ALU.mult))
                vwait(dve)
                vchain(nc.vector.tensor_reduce(yc[:, j, SEQ:LIVE], stp[:], AX_X, ALU.add))
                vwait(dve)
                vchain(nc.vector.tensor_scalar(yc[:, j, SEQ:LIVE], yc[:, j, SEQ:LIVE], cvec[:, 0, j:j + 1],
                                               None, ALU.add))
                if j == 3:
                    tap_tile(PAIR_GLU + 3, 0, 6)
            dve.wait_ge(page_used, 2 * NP)
            for r in range(2):
                ins = nc.vector.tensor_copy(
                    attn[HD * r:HD * r + HD, :, SEQ:LIVE],
                    ps[HD * r:HD * r + HD, 5, 0:P].rearrange("p (j b r) -> p j b r", j=KA, b=DEC)[:, :, :, r])
            ins.then_inc(d_vec, 1)
            tap_tile(PAIR_GLU + 3, 1, 7)
            with dve.Fori(0, NG) as g:
                def tile(t, between=(None,) * 4):
                    for k in range(4):
                        split_lo(dve, 8 * (PAIR_ATT + 3 * g + t // 2), 4 * (t % 2) + AHEAD + k)
                        for o in (8 * t + 2 * k, 8 * t + 2 * k + 1):
                            dve.wait_ge(tap_done, 6 * KC * (g + 1) + o + 1)
                            tap(o % KC, 6 * g + 7 + o // KC).then_inc(tap_done, 1)
                        if between[k]:
                            between[k]()

                dve.wait_ge(vt_ready, g + 1)
                nc.vector.tensor_copy(vn[:, 0:2, :].rearrange("p a b -> p (a b)"), ps[:, 6, :])
                nc.vector.tensor_copy(vn[0:META, 2, :], ps[0:META, 7, 0:GH * HD]).then_inc(vn_ready, 1)
                dve.wait_ge(z_kept, 2 * GH * g + GH)
                nc.vector.tensor_scalar(sab[:], eab[:], 0.0, None, ALU.max).then_inc(relu_done, 1)
                dve.wait_ge(z_kept, 2 * GH * g + 2 * GH)
                nc.vector.tensor_scalar(sm[:], em[:], 0.0, None, ALU.max).then_inc(relu_done, 1)
                tile(0)

                def add_ab():
                    dve.wait_ge(relu_done, 2 * g + 2)
                    dve.wait_ge(ln_done, 2 * g + 1)
                    nc.vector.tensor_tensor(sab[:], sab[:], eab[:], ALU.add).then_inc(sp_step, 1)

                def masked(c, n):
                    def f():
                        dve.wait_ge(sp_step, 3 * g + n)
                        nc.vector.tensor_tensor(sab[:, :, c:c + P], sab[:, :, c:c + P], spread(mask[:], 1, GH),
                                                ALU.mult).then_inc(sp_step, 1)
                    return f

                def add_m():
                    dve.wait_ge(ln_done, 2 * g + 2)
                    nc.vector.tensor_tensor(sm[:], sm[:], em[:], ALU.add).then_inc(sp_ready, 1)
                tile(1, (None, None, add_ab, masked(0, 1)))
                tile(2, (masked(256, 1), add_m, None, None))
                tile(3)
                tile(4)
                tile(5)
                dve.wait_ge(o_ready, g + 1)
                nc.vector.tensor_copy(attn[:, bass.ds(GH // 2 * g, GH // 2), 0:SEQ], ps[:, 2:4, 0:256])\
                    .then_inc(o_done, 1)

    at_hi, at_lo, cv_hi, cv_lo = sem("at_hi"), sem("at_lo"), sem("cv_hi"), sem("cv_lo")
    sig_done, x_back = sem("sig_done"), sem("x_back")
    mean_step, mu_ready, cen_done, nrm_done = sem("mean_step"), sem("mu_ready"), sem("cen_done"), sem("nrm_done")
    silu_done, t1_done, mixed_done, mx_hi = sem("silu_done"), sem("t1_done"), sem("mixed_done"), sem("mx_hi")
    mx_lo, x2_done, spill_done, acc_zero = sem("mx_lo"), sem("x2_done"), sem("spill_done"), sem("acc_zero")
    raw2_hi, raw2_lo, pool_go = sem("raw2_hi"), sem("raw2_lo"), sem("pool_go")
    sk_in, sc_ready, sc_done, zero_done = sem("sk_in"), sem("sc_ready"), sem("sc_done"), sem("zero_done")
    half_scores = sem("half_scores")
    PAIR_CV = PAIR_IN + 4
    SIG = 4
    with nc.Block() as block:
        @block.sync
        def _(sp):
            sp.dma_start(x[:], xT).then_inc(x_back, 16)

            def stream(first, last):
                with sp.Fori(first, last) as i:
                    for s in range(RAW):
                        load_half(sp, 4 * i + s, s, a_halves[4 * i + s])
            stream(PAIR_IN + 1, PAIR_BR + 1)
            sp.wait_ge(at_lo, 2)
            sp.dma_start(skT, sub_keysT).then_inc(sk_in, 16)
            stream(PAIR_BR + 1, PAIR_OUT + 1)
            sp.wait_ge(x2_done, KD)
            sp.dma_start(x2_dram, x[:, :, 0:LIVE]).then_inc(spill_done, 16)
            stream(PAIR_OUT + 1, PAIR_QRY)
            for s in range(RAW):
                load_half(sp, 4 * PAIR_QRY + s, s, u_tiles[s])
            sp.wait_ge(spill_done, 16)

        @block.gpsimd
        def _(pool):
            for j in range(1, KC):
                if j >= 2:
                    pool.wait_ge(mean_step, j - 1)
                nc.gpsimd.tensor_tensor(acc2[:], yc[:, 0, :] if j == 1 else acc2[:], yc[:, j, :],
                                        ALU.add).then_inc(mean_step, 1)
            pool.wait_ge(mu_ready, 1)
            for j in range(1, KC):
                pool_sum(pool, acc2, work2, j, CALL[1], LIVE)
            pool.wait_ge(sum_ready, 2)
            nc.gpsimd.memset(acc2[:], 0.0).then_inc(acc_zero, 1)
            pool.wait_ge(acc_zero, 1)
            with pool.Fori(0, KD // 2) as i:
                for b in range(2):
                    pool.wait_ge(sq_ready, CALL[2] + 2 * i + b + 1)
                    pool.wait_ge(sq_used, CALL[2] + 2 * i + b)
                    pool.sem_inc(pool_go, 1)
                    nc.gpsimd.tensor_tensor(acc2[:], acc2[:], work2[:, b, :], ALU.add).then_inc(sq_used, 1)
            nc.gpsimd.memset(sc_all[:, 2], 0.0).then_inc(zero_done, 1)

        @block.scalar
        def _(act):
            for c in range(2):
                js = slice(KA // 2 * c, KA // 2 * (c + 1))
                nc.scalar.copy(at_p[0][:, js], attn[:, js]).then_inc(at_hi, 1)

            def sigmoid(q):
                t = slice(SIG * q, SIG * (q + 1))
                nc.scalar.activation(gates[:, t, :], gates[:, t, :], ACT.Sigmoid).then_inc(sig_done, 1)
            sigmoid(0)
            for m in range(32):
                split_hi(act, 8 * (PAIR_IN + m // 8), m % 8 + AHEAD)
                if m in (0, 1):
                    sigmoid(1 + m)
                if 4 <= m < 8:
                    for j in (2 * (m - 4), 2 * (m - 4) + 1):
                        act.wait_ge(cen_done, j + 1)
                        if j >= 4:
                            act.wait_ge(sq_used, CALL[1] + j - 3)
                        nc.scalar.square(work2[:, j % 4, :], yc[:, j, :]).then_inc(sq_ready, 1)
                if m == 12:
                    act_root(act, root2, 2, DC, 1, LIVE)
                if 13 <= m < 18:
                    sigmoid(3 + m - 13)
                if 18 <= m < 22:
                    for j in (2 * (m - 18), 2 * (m - 18) + 1):
                        act.wait_ge(nrm_done, j + 1)
                        nc.scalar.activation(yc[:, j, :], yc[:, j, :], ACT.Silu, bias=cvec[:, 2, j:j + 1],
                                             scale=cvec[:, 1, j:j + 1]).then_inc(silu_done, 1)
                if m in (23, 25):
                    js = slice(KC // 2 * ((m - 23) // 2), KC // 2 * ((m - 23) // 2 + 1))
                    act.wait_ge(silu_done, KC)
                    nc.scalar.copy(cv_p[0][:, js], yc[:, js]).then_inc(cv_hi, 1)
            with act.Fori(PAIR_CV, PAIR_BR) as i:
                for b in range(2):
                    four(split_hi, act, i, b)
                    n = 2 * (i - PAIR_CV) + b
                    act.wait_ge(mixed_done, n + 1)
                    nc.scalar.copy(mx[0][:, bass.ds(2 * n, 2), :], gates[:, bass.ds(2 * n, 2), :]).then_inc(mx_hi, 1)
            with act.Fori(PAIR_BR, PAIR_OUT) as i:
                for b in range(2):
                    four(split_hi, act, i, b)
                    t = 2 * (i - PAIR_BR) + b
                    act.wait_ge(x2_done, t + 1)
                    act.sem_inc(act_go, 1)
                    nc.scalar.activation(raw2[0][:, t, :], x[:, t, 0:LIVE], ACT.Copy, scale=gain[:, 1, bass.ds(t, 1)])\
                        .then_inc(raw2_hi, 1)
                    act.wait_ge(sq_used, CALL[2] + t - 1)
                    act.sem_inc(act_go, 1)
                    nc.scalar.square(work2[:, b, :], x[:, t, 0:LIVE]).then_inc(sq_ready, 1)
            four(split_hi, act, PAIR_OUT, 0)
            act_root(act, root2, 3, D, 0, LIVE)
            for k in range(4):
                split_hi(act, 8 * PAIR_OUT, 4 + AHEAD + k)
                if k < 2:
                    norm_hi_part(act, h2, work2, k, k, CALL_N + k, LIVE)
            with act.Fori(PAIR_OUT + 1, PAIR_QRY) as i:
                for b in range(2):
                    j = 2 * (i - PAIR_OUT) + b
                    for k in range(4):
                        split_hi(act, 8 * i, 4 * b + AHEAD + k)
                        if k == 0:
                            norm_hi_part(act, h2, work2, b, j, CALL_N + j, LIVE)

        @block.tensor
        def _(pe):
            def branch_tile(i, b, rhs):
                for r in range(4):
                    quarter_products(pe, 8 * i, 4 * b + r, ps[:, 2 * b + r // 2, 0:LIVE], rhs,
                                     QT * (r % 2), LIVE, r % 2 == 0, r % 2 == 1)
            for n in range(8):
                i, b = PAIR_IN + n // 2, n % 2
                pe.wait_ge(tile_free[b], i + 1)
                if n == 0:
                    for r in range(4):
                        pe.wait_ge(at_lo, min(r + 1, 2))
                        quarter_products(pe, 8 * i, r, ps[:, r // 2, 0:LIVE], at_p, QT * (r % 2), LIVE,
                                         r % 2 == 0, r % 2 == 1)
                    pe.wait_ge(mean_step, KC - 1)
                    pe.matmul(ps[:, 6, 0:LIVE], ones[:], acc2[:], start=True, stop=True).then_inc(mu_ready, 1)
                else:
                    branch_tile(i, b, at_p)
                if n == 2:
                    pe_sum(pe, acc2, CALL[1], KC, LIVE)
            pe.wait_ge(cv_lo, 2)
            with pe.Fori(PAIR_CV, PAIR_BR) as i:
                for b in range(2):
                    pe.wait_ge(tile_free[b], i + 1)
                    branch_tile(i, b, cv_p)
            pe.wait_ge(tile_free[0], PAIR_BR + 1)
            pe_tile_follow(pe, PAIR_BR, 0, mx, LIVE, mx_lo, 0)
            pe.wait_ge(tile_free[1], PAIR_BR + 1)
            pe_tile(pe, PAIR_BR, 1, mx, LIVE)
            pe_pairs(pe, PAIR_BR + 1, PAIR_OUT, mx, LIVE)

            def scores(i, b):
                pe.wait_ge(tile_free[b], i + 2)
                pe.wait_ge(sc_done, 2 * (i - PAIR_OUT) + b + 1)
                for t in range(TT):
                    n = (P, P, DEC)[t]
                    m = pe.matmul(ps[0:n, 2 + b, P * t:P * t + P], qry[:, b, P * t:P * t + n], skT[:, b, :],
                                  start=True, stop=True)
                m.then_inc(sc_ready, 1)
            pe.wait_ge(sk_in, 16)
            pe.wait_ge(tile_free[0], PAIR_OUT + 1)
            pe_tile_follow(pe, PAIR_OUT, 0, raw2, LIVE, raw2_lo, 0)
            pe_sum(pe, acc2, CALL[2], KD, LIVE)

            def query_tile(i, b):
                pe.wait_ge(tile_free[b], i + 1)
                for r in range(4):
                    if r == 2:
                        scores(i if b else i - 1, 1 - b)
                    quarter_products(pe, 8 * i, 4 * b + r, ps[:, b, 0:LIVE], raw2, QT * r, LIVE, r == 0, r == 3)
            query_tile(PAIR_OUT, 1)
            with pe.Fori(PAIR_OUT + 1, PAIR_QRY) as i:
                for b in range(2):
                    query_tile(i, b)
            scores(PAIR_QRY - 1, 1)

        @block.vector
        def _(dve):
            for c in range(2):
                js = slice(KA // 2 * c, KA // 2 * (c + 1))
                dve.wait_ge(at_hi, c + 1)
                nc.vector.tensor_tensor(at_p[1][:, js], attn[:, js], at_p[0][:, js].bitcast(F32),
                                        ALU.subtract).then_inc(at_lo, 1)
            for m in range(32):
                n = m // 4
                split_lo(dve, 8 * (PAIR_IN + m // 8), m % 8 + AHEAD)
                if m == 4:
                    dve.wait_ge(mu_ready, 1)
                if 4 <= m < 8:
                    for j in (2 * (m - 4), 2 * (m - 4) + 1):
                        nc.vector.scalar_tensor_tensor(out=yc[:, j, :], in0=ps[:, 6, 0:LIVE], scalar=-1.0 / DC,
                                                       in1=yc[:, j, :], op0=ALU.mult, op1=ALU.add)\
                            .then_inc(cen_done, 1)
                if m == 13:
                    dve_rstd(dve, LIVE, root2, rstd2, tmp2, 2, DC, 1)
                if 14 <= m < 18:
                    for j in (2 * (m - 14), 2 * (m - 14) + 1):
                        nc.vector.tensor_tensor(yc[:, j, :], yc[:, j, :], rstd2[:], ALU.mult).then_inc(nrm_done, 1)
                if m in (24, 26):
                    js = slice(KC // 2 * ((m - 24) // 2), KC // 2 * ((m - 24) // 2 + 1))
                    dve.wait_ge(cv_hi, (m - 24) // 2 + 1)
                    nc.vector.tensor_tensor(cv_p[1][:, js], yc[:, js], cv_p[0][:, js].bitcast(F32),
                                            ALU.subtract).then_inc(cv_lo, 1)
                if m % 4 == 3:
                    b = n % 2
                    tile_done(dve, PAIR_IN + n // 2, b)
                    dve.wait_ge(sig_done, 2 * n // SIG + 1)
                    nc.vector.tensor_tensor(gates[:, 2 * n:2 * n + 2, :], gates[:, 2 * n:2 * n + 2, :],
                                            ps[:, 2 * b:2 * b + 2, 0:LIVE], ALU.mult).then_inc(tile_free[b], 1)
            dve.wait_ge(sig_done, 2 * KD // SIG)
            dve.wait_ge(tile_free[0], PAIR_CV + 1)
            dve.wait_ge(tile_free[1], PAIR_CV + 1)
            with dve.Fori(PAIR_CV, PAIR_BR) as i:
                for b in range(2):
                    four(split_lo, dve, i, b)
                    n = 2 * (i - PAIR_CV) + b
                    tile_done(dve, i, b)
                    nc.vector.tensor_tensor(t2[:], gates[:, bass.ds(2 * n + KD, 2), :], ps[:, 2 * b:2 * b + 2, 0:LIVE],
                                            ALU.mult).then_inc(t1_done, 1)
                    dve.wait_ge(t1_done, n + 1)
                    nc.vector.tensor_tensor(gates[:, bass.ds(2 * n, 2), :], gates[:, bass.ds(2 * n, 2), :], t2[:],
                                            ALU.add).then_inc(mixed_done, 1)
                    dve.sem_inc(tile_free[b], 1)
                    dve.wait_ge(mx_hi, n + 1)
                    nc.vector.tensor_tensor(mx[1][:, bass.ds(2 * n, 2), :], gates[:, bass.ds(2 * n, 2), :],
                                            mx[0][:, bass.ds(2 * n, 2), :].bitcast(F32), ALU.subtract)\
                        .then_inc(mx_lo, 2)
            dve.wait_ge(x_back, 16)
            with dve.Fori(PAIR_BR, PAIR_OUT) as i:
                for b in range(2):
                    four(split_lo, dve, i, b)
                    t = 2 * (i - PAIR_BR) + b
                    tile_done(dve, i, b)
                    nc.vector.tensor_tensor(x[:, t, 0:LIVE], x[:, t, 0:LIVE], ps[:, b, 0:LIVE], ALU.add)\
                        .then_inc(x2_done, 1)
                    dve.wait_ge(x2_done, t + 1)
                    dve.sem_inc(tile_free[b], 1)
                    dve.wait_ge(raw2_hi, t + 1)
                    dve.sem_inc(dve_go, 1)
                    nc.vector.scalar_tensor_tensor(out=raw2[1][:, t, :], in0=x[:, t, 0:LIVE],
                                                   scalar=gain[:, 1, bass.ds(t, 1)],
                                                   in1=raw2[0][:, t, :].bitcast(F32), op0=ALU.mult,
                                                   op1=ALU.subtract).then_inc(raw2_lo, 1)
            dve.sem_inc(sc_done, 2)

            def query_out(i, b):
                tile_done(dve, i, b)
                nc.vector.tensor_tensor(qry[:, b, :], ps[:, b, 0:LIVE], rstd2[:], ALU.mult).then_inc(tile_free[b], 1)

            def keep_scores(q, b):
                dve.wait_ge(sc_ready, q + 1)
                nc.vector.tensor_copy(sc_all[:, 0:2, q, :], ps[:, 2 + b, 0:256]).then_inc(half_scores, 1)
                nc.vector.tensor_copy(sc_all[0:DEC, 2, q, :], ps[0:DEC, 2 + b, 256:384]).then_inc(half_scores, 1)
                dve.wait_ge(half_scores, 2 * q + 2)
                dve.sem_inc(sc_done, 1)

            four(split_lo, dve, PAIR_OUT, 0)
            dve_rstd(dve, LIVE, root2, rstd2, tmp2, 3, D, 0)
            query_out(PAIR_OUT, 0)
            for k in range(4):
                if k < 2:
                    norm_scaled(x, work2, k, k, 1, rstd2, LIVE)
                split_lo(dve, 8 * PAIR_OUT, 4 + AHEAD + k)
                if 1 <= k < 3:
                    norm_lo_part(dve, h2, work2, k - 1, k - 1, CALL_N + k - 1, LIVE)
            dve.wait_ge(zero_done, 1)
            keep_scores(0, 0)
            query_out(PAIR_OUT, 1)
            with dve.Fori(PAIR_OUT + 1, PAIR_QRY) as i:
                for b in range(2):
                    j = 2 * (i - PAIR_OUT) + b
                    dve.wait_ge(norm_hi, CALL_N + j - 1)
                    dve.wait_ge(norm_lo, CALL_N + j - 1)
                    dve.sem_inc(dve_go, 1)
                    norm_scaled(x, work2, b, j, 1, rstd2, LIVE)
                    for k in range(4):
                        split_lo(dve, 8 * i, 4 * b + AHEAD + k)
                        if k == 1:
                            norm_lo_part(dve, h2, work2, b, j, CALL_N + j, LIVE)
                    keep_scores(j - 1, 1 - b)
                    query_out(i, b)
            keep_scores(2 * (PAIR_QRY - PAIR_OUT) - 1, 1)

    route, route_seen = sem("route"), sem("route_seen")
    with nc.Block() as block:
        @block.sync
        def _(sp):
            with sp.Fori(PAIR_QRY + 1, PAIR_U) as i:
                for s in range(RAW):
                    load_half(sp, 4 * i + s, s, u_tiles[4 * (i - PAIR_QRY) + s])
            for s in range(RAW):
                load_half(sp, 4 * PAIR_U + s, s, expert_v[0, s])

        @block.scalar
        def _(act):
            def gelu(b):
                def f(i):
                    nc.scalar.activation(W[:, 2 * (i - PAIR_QRY) + b, :], ps[:, b, 0:LIVE],
                                         ACT.Gelu_apprx_tanh).then_inc(tile_free[b], 1)
                return f
            act_pairs(act, PAIR_QRY, PAIR_U, gelu(0), gelu(1))

        @block.tensor
        def _(pe):
            pe_pairs(pe, PAIR_QRY, PAIR_U, h2, LIVE)

        @block.vector
        def _(dve):
            STEPS = 1 + TT * 2 * 5 + 2 + TT * 5 + 4 + 2 * 3
            with dve.Fori(0, PH) as hd:
                count = [0]

                def step(ins):
                    count[0] += 1
                    ins.then_inc(route, 1)

                def after():
                    dve.wait_ge(route, STEPS * hd + count[0])
                    dve.sem_inc(route_seen, 1)

                split = [0]

                def lo_next(n=1):
                    for _ in range(n):
                        split_lo(dve, 8 * PAIR_QRY + 8 * HEAD_PAIRS * hd, AHEAD + split[0])
                        split[0] += 1

                def best8(dst, idx, src):
                    lo_next()
                    step(nc.vector.max(dst, src))
                    lo_next()
                    after()
                    step(nc.vector.max_index(idx.bitcast(U32), dst, src))

                def drop8(dst, src):
                    step(nc.vector.match_replace(src, dst, src, NEG_BIG))
                    after()

                lo_next()
                step(nc.vector.tensor_copy(sh, sc_all[:, :, bass.ds(2 * hd, 2), :]))
                after()
                for t in range(TT):
                    for q in range(2):
                        s, v, ix = sh[:, t, q, :], top1[:, t, q, :], idx1[:, t, q, :]
                        best8(v[:, 0:8], ix[:, 0:8], s)
                        drop8(v[:, 0:8], s)
                        best8(v[:, 8:16], ix[:, 8:16], s)
                lo_next()
                after()
                step(nc.vector.tensor_tensor(cand, spread(top1[:, :, 0, :], 3, PK), spread(top1[:, :, 1, :], 2, PK),
                                             ALU.add))
                step(nc.vector.tensor_copy(idx1f, idx1.bitcast(U32)))
                for t in range(TT):
                    s = cand[:, t].rearrange("p a b -> p (a b)")
                    lo_next()
                    after()
                    step(nc.vector.max(top2[:, t, 0:8], s))
                    after()
                    step(nc.vector.max_index(pos2[:, t, 0:8].bitcast(U32), top2[:, t, 0:8], s))
                    drop8(top2[:, t, 0:8], s)
                    lo_next()
                    step(nc.vector.max(top2[:, t, 8:16], s))
                    after()
                    step(nc.vector.max_index(pos2[:, t, 8:16].bitcast(U32), top2[:, t, 8:16], s))
                lo_next()
                after()
                step(nc.vector.tensor_scalar(pab[:, 0].bitcast(U32), pos2.bitcast(U32), 4, None,
                                             ALU.logical_shift_right))
                step(nc.vector.tensor_scalar(pab[:, 1].bitcast(U32), pos2.bitcast(U32), 15, None,
                                             ALU.bitwise_and))
                after()
                step(nc.vector.tensor_copy(pabf, pab.bitcast(U32)))
                step(nc.vector.tensor_copy(chosen[:, 2, :, bass.ds(hd, 1), :],
                                           top2.rearrange("p t (o k) -> p t o k", o=1)))
                for q in range(2):
                    lo_next()
                    after()
                    ranks = spread(spread(iota[:, 0:PK], 1, PK), 1, TT)
                    step(nc.vector.tensor_tensor(eq, spread(pabf[:, q], 3, PK), ranks, ALU.is_equal))
                    lo_next()
                    after()
                    step(nc.vector.tensor_tensor(eq, eq, spread(idx1f[:, :, q, :], 2, PK), ALU.mult))
                    lo_next()
                    after()
                    step(nc.vector.tensor_reduce(chosen[:, q, :, bass.ds(hd, 1), :].rearrange("p t o k -> p t (o k)"),
                                                 eq, AX_X, ALU.add))
                lo_next(8 * HEAD_PAIRS - split[0])
                after()
                assert split[0] == 8 * HEAD_PAIRS and count[0] == STEPS, (split[0], count[0], STEPS)
            with dve.Fori(PAIR_QRY + PH * HEAD_PAIRS, PAIR_U) as i:
                four(split_lo, dve, i, 0)
                four(split_lo, dve, i, 1)

    soft = sem("soft")
    soft_act, tr_ready, ch_done = sem("soft_act"), sem("tr_ready"), sem("ch_done")
    l_ready, r_ready, g_ready, g_used = sem("l_ready"), sem("r_ready"), sem("g_ready"), sem("g_used")
    l_act, sq_done, diff_done, diff_seen = sem("l_act"), sem("sq_done"), sem("diff_done"), sem("diff_seen")
    GROUPS = LIVE // 4

    def by_vector(b):
        return 2
    SQ = sum(4 - by_vector(b) for b in range(GS))
    with nc.Block() as block:
        @block.scalar
        def _(act):
            act.wait_ge(soft, 2)
            nc.scalar.activation(chosen[:, 2], chosen[:, 2], ACT.Exp).then_inc(soft_act, 1)
            act.wait_ge(ch_done, 4)
            with act.Fori(0, GROUPS // GS) as i:
                for b in range(GS):
                    act.wait_ge(g_ready, GS * i + b + 1)
                    toks = range(by_vector(b), 4)
                    for t in toks:
                        nc.scalar.activation(ldiff[:, b % 2, t - 2], iota[:], ACT.Square,
                                             bias=chT[:, 3, bass.ds(4 * GS * i + 4 * b + t, 1)]).then_inc(sq_done, 1)
                    for t in toks:
                        act.wait_ge(sq_done, SQ * i + sum(4 - by_vector(k) for k in range(b)) + t - toks[0] + 1)
                        m = nc.scalar.activation(lhot[:, b, t], ldiff[:, b % 2, t - 2], ACT.Relu, scale=-2.0,
                                                 bias=chT[:, 2, bass.ds(4 * GS * i + 4 * b + t, 1)])
                    m.then_inc(l_act, 1)

        @block.gpsimd
        def _(pool):
            pool.sem_inc(g_used, GS)
            pool.wait_ge(ch_done, 3)
            with pool.Fori(0, GROUPS // GS) as i:
                for b in range(0, GS, 2):
                    n = (GS // 2) * i + b // 2
                    pool.wait_ge(g_ready, GS * i + b + 1)
                    pool.wait_ge(r_ready, n + 1)
                    pool.sem_inc(diff_seen, 1)
                    nc.gpsimd.tensor_tensor(rdiff[:], spread(iota[:], 1, 4),
                                            spread(chT[:, 1, bass.ds(4 * GS * i + 4 * b, 4)], 2, NK),
                                            ALU.subtract).then_inc(diff_done, 1)
                    pool.wait_ge(diff_done, n + 1)
                    pool.sem_inc(diff_seen, 1)
                    nc.gpsimd.tensor_scalar(rhot[:, b], rdiff[:], 0.0, None, ALU.is_equal).then_inc(r_ready, 1)

        @block.tensor
        def _(pe):
            pe.sem_inc(g_ready, GS)
            pe.sem_inc(r_ready, 1)
            pe.wait_ge(soft, 5)
            for t in range(TT):
                n = (P, P, DEC)[t]
                for q in range(3):
                    m = pe.transpose(ps[:, q, P * t:P * t + n],
                                     chosen[0:n, q, t].rearrange("p h k -> p (h k)"), ident[0:n, 0:n])
            m.then_inc(tr_ready, 1)
            with pe.Fori(0, GROUPS // GS) as i:
                for b in range(GS):
                    pe.wait_ge(l_ready, GS * i + b + 1)
                    pe.wait_ge(l_act, GS * i + b + 1)
                    if b % 2 == 0:
                        pe.wait_ge(r_ready, (GS // 2) * i + b // 2 + 2)
                    pe.wait_ge(g_used, GS * i + b + 1)
                    for t in range(4):
                        m = pe.matmul(ps[:, 2 + b, NK * t:NK * t + NK], lhot[:, b, t], rhot[:, b, t],
                                      start=True, stop=True)
                    m.then_inc(g_ready, 1)

        @block.vector
        def _(dve):
            sc = chosen[:, 2]
            nc.vector.tensor_copy(sums[:, 0], sc[:, :, :, 0]).then_inc(soft, 1)
            dve.wait_ge(soft, 1)
            nc.vector.tensor_tensor(sc, sc, spread(sums[:, 0], 3, PK), ALU.subtract).then_inc(soft, 1)
            dve.wait_ge(soft_act, 1)
            nc.vector.tensor_reduce(sums[:, 0], sc, AX_X, ALU.add).then_inc(soft, 1)
            dve.wait_ge(soft, 3)
            nc.vector.reciprocal(sums[:, 1], sums[:, 0]).then_inc(soft, 1)
            dve.wait_ge(soft, 4)
            nc.vector.tensor_tensor(sc, sc, spread(sums[:, 1], 3, PK), ALU.mult).then_inc(soft, 1)
            dve.wait_ge(tr_ready, 1)
            for q in range(3):
                nc.vector.tensor_copy(chT[:, q, :], ps[:, q, 0:LIVE]).then_inc(ch_done, 1)
            dve.wait_ge(ch_done, 3)
            nc.vector.tensor_scalar(chT[:, 3, :], chT[:, 0, :], -1.0, None, ALU.mult).then_inc(ch_done, 1)

            def left(tok, b, t):
                return nc.vector.tensor_scalar(lhot[:, b, t], iota[:], chT[:, 0, bass.ds(tok, 1)],
                                               chT[:, 2, bass.ds(tok, 1)], ALU.is_equal, ALU.mult)
            def hots(i, b):
                tok = 4 * GS * i + 4 * b
                if b % 2:
                    nc.vector.tensor_tensor(rhot[:, b], spread(iota[:], 1, 4),
                                            spread(chT[:, 1, bass.ds(tok, 4)], 2, NK), ALU.is_equal)
                for t in range(by_vector(b)):
                    m = left(tok + t, b, t)
                m.then_inc(l_ready, 1)

            def weigh(i, b):
                dve.wait_ge(g_ready, GS + GS * i + b + 1)
                wv = W[:, :, bass.ds(4 * GS * i + 4 * b, 4)]
                nc.vector.tensor_tensor(wv, wv, ps[:, 2 + b, :].rearrange("p (t n) -> p n t", t=4),
                                        ALU.mult).then_inc(g_used, 1)

            for b in range(GS):
                hots(0, b)
            with dve.Fori(0, GROUPS // GS - 1) as i:
                for b in range(GS):
                    weigh(i, b)
                    hots(i + 1, b)
            for b in range(GS):
                weigh(GROUPS // GS - 1, b)

    x2_in, whi_done, wlo_done, acc_done = sem("x2_in"), sem("whi_done"), sem("wlo_done"), sem("acc_done")
    y_done = sem("y_done")
    C0 = 4 * PAIR_U
    with nc.Block() as block:
        @block.sync
        def _(sp):
            def stream(first, last):
                with sp.Fori(first, last) as i:
                    for s in range(RAW):
                        load_half(sp, C0 + 4 * i + s, s, expert_v[0, 4 * i + s])
            stream(1, 4)
            sp.dma_start(x2[:], x2_dram).then_inc(x2_in, 16)
            stream(4, NK // 4)
            with sp.Fori(0, NK // 4) as i:
                for s in range(RAW):
                    load_half(sp, C0 + NK + 4 * i + s, s, expert_v[1, 4 * i + s])
            for q in range(4):
                sp.wait_ge(y_done, 4 * q + 4)
                sp.dma_start(yT[:, 4 * q:4 * q + 4], x2[:, 4 * q:4 * q + 4, :]).then_inc(out_done, 16)
            sp.wait_ge(out_done, 64)

        def halves(eng, w_part, split, after_pass):
            def half(c, n, k, last=2):
                w_part(c + 1, n, k + 1)
                for r in range(last):
                    split(eng, C0 * 2 + 2 * (c - k), 2 * k + AHEAD + r)
            w_part(0, 0, 0)
            for p in range(2):
                with eng.Fori(0, NK // 4 - 1) as i:
                    for k in range(4):
                        half(NK * p + 4 * i + k, 4 * i + k + 1, k)
                for k in range(4):
                    if p == 0 or k < 2:
                        half(NK * p + NK - 4 + k, (NK - 3 + k) % NK, k)
                    elif k == 2:
                        half(NK * p + NK - 4 + k, NK - 3 + k, k, 1)
                after_pass(p)

        @block.scalar
        def _(act):
            def w_part(c, n, k):
                act.wait_ge(mm_done, 2 * C0 + 2 * c + 2)
                nc.scalar.copy(w_hi[k % 2][:], W[:, n, :]).then_inc(whi_done, 1)
            halves(act, w_part, split_hi, lambda p: None)
            for j in range(HALF, KD):
                act.wait_ge(acc_done, 1 + j // 2 - HALF // 2 + 1)
                act.wait_ge(sq_used, CALL[3] + max(j - 3, HALF))
                nc.scalar.square(fin[:, j % 4, :], x2[:, j, :]).then_inc(sq_ready, 1)
            act.wait_ge(sq_used, CALL[3] + KD)
            act_root(act, fin_r[:, 0], 4, D, 0, LIVE)

        @block.gpsimd
        def _(pool):
            pool.wait_ge(acc_done, 1)
            for j in range(HALF):
                if j >= 4:
                    pool.wait_ge(sq_used, CALL[3] + j - 3)
                nc.gpsimd.tensor_tensor(fin[:, j % 4, :], x2[:, j, :], x2[:, j, :], ALU.mult).then_inc(sq_ready, 1)
                if j >= 1:
                    pool_sum(pool, fin_r[:, 3], fin, j, CALL[3], LIVE)

        @block.vector
        def _(dve):
            def w_part(c, n, k):
                dve.wait_ge(whi_done, c + 1)
                dve.wait_ge(mm_done, 2 * C0 + 2 * c + 2)
                nc.vector.tensor_tensor(w_lo[k % 2][:], W[:, n, :], w_hi[k % 2][:].bitcast(F32),
                                        ALU.subtract).then_inc(wlo_done, 1)

            def after_pass(p):
                dve.wait_ge(mm_done, 2 * C0 + 2 * NK * (p + 1) + SPLIT)
                if p == 0:
                    dve.wait_ge(x2_in, 16)
                step = HALF if p == 0 else 2
                for j in range(0, HALF, step):
                    a = HALF * p + j
                    nc.vector.tensor_tensor(x2[:, a:a + step, :], x2[:, a:a + step, :], ps[:, j:j + step, 0:LIVE],
                                            ALU.add).then_inc(acc_done, 1)
            halves(dve, w_part, split_lo, after_pass)
            dve_rstd(dve, LIVE, fin_r[:, 0], fin_r[:, 1], fin_r[:, 2], 4, D, 0)
            for j in range(KD):
                nc.vector.scalar_tensor_tensor(out=x2[:, j, :], in0=x2[:, j, :], scalar=gain[:, 2, j:j + 1],
                                               in1=fin_r[:, 1], op0=ALU.mult, op1=ALU.mult).then_inc(y_done, 1)

        @block.tensor
        def _(pe):
            def f(c, k, start, stop):
                pe.wait_ge(wlo_done, c + 1)
                for r in range(2):
                    pe.wait_ge(lo_done, 2 * C0 + 2 * c + r + 2 * RAW + 1)
                    a, b = hi[(2 * k + r) % SPLIT], lo[(2 * k + r) % SPLIT]
                    for j in range(QT):
                        o = ps[:, QT * r + j, 0:LIVE]
                        pe.matmul(o, a[:, j], w_hi[k % 2][:], start=start, stop=False, skip_group_check=True)
                        pe.matmul(o, a[:, j], w_lo[k % 2][:], start=False, stop=False, skip_group_check=True)
                        m = pe.matmul(o, b[:, j], w_hi[k % 2][:], start=False, stop=stop, skip_group_check=True)
                    m.then_inc(mm_done, 1)
            for p in range(2):
                if p == 1:
                    pe.wait_ge(acc_done, 1)
                for k in range(4):
                    f(NK * p + k, k, k == 0, False)
                with pe.Fori(1, NK // 4 - 1) as i:
                    for k in range(4):
                        f(NK * p + 4 * i + k, k, False, False)
                for k in range(4):
                    f(NK * p + NK - 4 + k, k, False, k == 3)
            pe.wait_ge(sq_used, CALL[3] + HALF)
            pe.wait_ge(acc_done, 1 + HALF // 2)
            pe.matmul(ps[:, 7, 0:LIVE], ones[:], fin_r[:, 3], start=True, stop=False)
            for j in range(HALF, KD):
                pe.wait_ge(sq_ready, CALL[3] + j + 1)
                m = pe.matmul(ps[:, 7, 0:LIVE], ones[:], fin[:, j % 4, :], start=False, stop=j == KD - 1)
                m.then_inc(sq_used, 1)
            pe.sem_inc(sum_ready, 1)


def build(nc, arrays):
    args = {}
    for name, v in arrays.items():
        args[name] = nc.dram_tensor(name, v.shape, mybir.dt.from_np(v.dtype), kind="ExternalInput").ap()
    args["expert_v"] = args["expert_v"].rearrange("(a n) (h d) -> h n a d", a=NK, h=2)
    outs = {"yT": (P, KD, LIVE), "kvT": (2 * DA, NT), "conv_p": (DC, TAPS - 1), "conv_s": (P, KC, DEC, TAPS - 1)}
    for name, shape in outs.items():
        args[name] = nc.dram_tensor(name, shape, F32, kind="ExternalOutput").ap()
    trunk(nc, *args.values())


def kernel(**inputs):
    import numpy as np
    import concourse.bacc as bacc
    from concourse.bass_utils import run_bass_kernel_spmd

    def tiles(w):
        k, c = w.shape
        return w.reshape(k // (HALF * P), HALF, P, c // P, P).transpose(3, 0, 2, 1, 4)

    def columns(v):
        v = v.reshape(v.shape[:-1] + (v.shape[-1] // P, P))
        return np.moveaxis(v, -1, 0)

    a = {k: np.asarray(v) for k, v in inputs.items()}
    tokens = np.concatenate([a["x_prompt"][0], a["x_sample"][:, 0], a["meta_tokens"]], axis=0)
    w_in = tiles(a["w_in"][0])
    order = list(range(3 * KA))
    for c in range(KC):
        order += [3 * KA + KC + c, 3 * KA + c]
    order += list(range(3 * KA + 2 * KC, T_IN))
    w_br = np.concatenate([tiles(a["w_branch_attn"][0]), tiles(a["w_branch_conv"][0])])
    w_br = w_br.reshape((-1, 2) + w_br.shape[2:])
    weights = np.concatenate([w_in[order], w_br, tiles(a["w_out"][0]), tiles(a["w_query"][0])], axis=0)
    u = a["expert_u"][0].reshape(NK, NK, 2, HALF, P).transpose(1, 2, 4, 3, 0)
    arrays = {
        "weights": weights.reshape(-1, P, HALF * P),
        "xT": columns(tokens).transpose(0, 2, 1),
        "gains": columns(np.stack([a["norm_mix_g"][0], a["norm_ffn_g"][0], a["norm_final_g"]])),
        "u_tiles": u.reshape(-1, P, HALF * P),
        "expert_v": a["expert_v"][0],
        "cache_k": a["cache_k"][0].reshape(-1, DA),
        "cache_v": a["cache_v"][0].reshape(-1, DA),
        "stateT": columns(a["state_conv"][0]).transpose(0, 3, 1, 2),
        "page_table": np.broadcast_to(a["page_table"].reshape(1, -1), (P, DEC * PAGES)),
        "sb_bias": np.broadcast_to(a["sb_bias"], (P, HEADS)),
        "w_dwT": columns(a["w_dw"][0]).transpose(0, 2, 1),
        "conv_vecs": columns(np.stack([a["b_dw"][0], a["conv_ln_g"][0], a["conv_ln_b"][0]])),
        "sub_keysT": a["sub_keys"][0].transpose(2, 0, 1),
    }
    arrays = {k: np.ascontiguousarray(v) for k, v in arrays.items()}
    nc = bacc.Bacc("TRN2", target_bir_lowering=False, num_devices=1)
    build(nc, arrays)
    r = run_bass_kernel_spmd(nc, [arrays], core_ids=[0]).results[0]
    y = np.transpose(r["yT"], (2, 1, 0)).reshape(LIVE, D)
    kv = np.transpose(r["kvT"].reshape(2, HEADS, HD, NT), (0, 3, 1, 2))
    prompt = np.concatenate([kv[:, LIVE:], kv[:, :SEQ]], axis=1)[:, None, None]
    sample = kv[:, SEQ:LIVE][:, None, :, None]
    conv_prompt = np.transpose(r["conv_p"], (1, 0))[None, None]
    conv_sample = np.transpose(r["conv_s"], (2, 3, 1, 0)).reshape(1, DEC, TAPS - 1, DC)
    return (y[None, :SEQ], y[SEQ:, None], prompt[0], prompt[1], conv_prompt, sample[0], sample[1], conv_sample)
```
